# Optimizing a Trainium2 kernel written in Bass

```python
import math
import jax, jax.numpy as jnp
from jax import lax
import numpy as np

D_MODEL = 1024
BATCH = 1
SEQ = 512
DEPTH = 1

CHUNK = 64
D_MIX = D_MODEL
GM_GROUPS = 8
GM_GROUP_DIM = 64
GM_WIDTH = GM_GROUPS * GM_GROUP_DIM
GM_BLOCK = 128
DN_HEADS = 4
DN_HEAD_DIM = 128
DN_WIDTH = DN_HEADS * DN_HEAD_DIM
DN_CONV = 4
D_IN = 2 * GM_WIDTH + 4 * DN_WIDTH + 2 * DN_HEADS
D_FF = 2816
EPS = 1e-6


def rmsnorm(x, g):
    xf = x.astype(jnp.float32)
    y = xf * lax.rsqrt(jnp.mean(xf * xf, axis=-1, keepdims=True) + EPS)
    return (y * g.astype(jnp.float32)).astype(x.dtype)

def layernorm(x, g, b):
    xf = x.astype(jnp.float32)
    mu = jnp.mean(xf, axis=-1, keepdims=True)
    var = jnp.mean(jnp.square(xf - mu), axis=-1, keepdims=True)
    y = (xf - mu) * lax.rsqrt(var + EPS)
    return (y * g.astype(jnp.float32) + b.astype(jnp.float32)).astype(x.dtype)

def l2norm(x):
    return x * lax.rsqrt(jnp.sum(x * x, axis=-1, keepdims=True) + EPS)

def swiglu(x, w_gate, w_up, w_down):
    return (jax.nn.silu(x @ w_gate) * (x @ w_up)) @ w_down

def chunk_causal_mask(n):
    c = jnp.arange(n) // CHUNK
    return c[None, :] <= c[:, None]

def spatial_gating(u, v, w_s, b_s, ln_g, ln_b):
    B, T, _ = v.shape
    v = layernorm(v, ln_g, ln_b)
    nb = T // GM_BLOCK
    vb = v.reshape(B, nb, GM_BLOCK, GM_GROUPS, GM_GROUP_DIM)
    w = jnp.where(chunk_causal_mask(GM_BLOCK)[None], w_s, 0.0).astype(v.dtype)
    mixed = jnp.einsum('gij,bnjgc->bnigc', w, vb) + b_s.T[:, :, None].astype(v.dtype)
    return u * mixed.reshape(B, T, GM_WIDTH)

def causal_dwconv(x, w):
    K, C = w.shape
    return lax.conv_general_dilated(
        x, w[:, None, :].astype(x.dtype), window_strides=(1,), padding=[(K - 1, 0)],
        dimension_numbers=('NWC', 'WIO', 'NWC'), feature_group_count=C)

def gated_delta_rule(q, k, v, beta, g):
    B, T, H, Dk = q.shape
    Dv = v.shape[-1]
    C = CHUNK
    N = T // C
    scale = Dk ** -0.5

    def to_chunks(t):
        return t.reshape(B, N, C, H, *t.shape[3:]).swapaxes(2, 3)

    q, k, v = to_chunks(q * scale), to_chunks(k), to_chunks(v)
    beta, g = to_chunks(beta), to_chunks(g)
    g = jnp.cumsum(g, axis=-1)
    tri = jnp.tril(jnp.ones((C, C), bool))
    strict = jnp.tril(jnp.ones((C, C), bool), -1)
    decay = jnp.exp(jnp.where(tri, g[..., :, None] - g[..., None, :], -jnp.inf))
    k_beta = k * beta[..., None]
    v_beta = v * beta[..., None]
    L = jnp.where(strict, jnp.einsum('bnhid,bnhjd->bnhij', k_beta, k) * decay, 0.0)
    eye = jnp.eye(C, dtype=L.dtype)
    rhs = jnp.concatenate([v_beta, k_beta * jnp.exp(g)[..., None]], axis=-1)
    sol = lax.linalg.triangular_solve(L + eye, rhs, left_side=True, lower=True,
                                      unit_diagonal=True)
    u_c, w_c = sol[..., :Dv], sol[..., Dv:]
    attn = jnp.where(tri, jnp.einsum('bnhid,bnhjd->bnhij', q, k) * decay, 0.0)
    g_last = g[..., -1]
    k_dec = k * jnp.exp(g_last[..., None] - g)[..., None]
    q_dec = q * jnp.exp(g)[..., None]
    xs = tuple(jnp.moveaxis(t, 1, 0) for t in (q_dec, k_dec, u_c, w_c, attn, g_last))

    def step(S, inp):
        qd, kd, uc, wc, a, gl = inp
        v_new = uc - jnp.einsum('bhcd,bhde->bhce', wc, S)
        o = jnp.einsum('bhcd,bhde->bhce', qd, S) + jnp.einsum('bhij,bhje->bhie', a, v_new)
        S = S * jnp.exp(gl)[..., None, None] + jnp.einsum('bhcd,bhce->bhde', kd, v_new)
        return S, o

    S0 = jnp.zeros((B, H, Dk, Dv), q.dtype)
    _, o = lax.scan(step, S0, xs)
    return jnp.moveaxis(o, 0, 1).swapaxes(2, 3).reshape(B, T, H, Dv)

def first_inputs(seed: int = 0) -> dict:
    key = jax.random.key(seed)
    ks = jax.random.split(key, 24)
    f32 = jnp.float32
    L = DEPTH

    def nrm(k, shape, scale):
        return jax.random.normal(k, shape, f32) * scale

    def gain(k, shape):
        return 1.0 + 0.05 * jax.random.normal(k, shape, f32)

    dt = jnp.exp(jax.random.uniform(ks[13], (L, DN_HEADS), f32, math.log(1e-3), math.log(1e-1)))
    return {
        "x": jax.random.normal(ks[0], (BATCH, SEQ, D_MODEL), f32),
        "ffn1_norm": gain(ks[1], (L, D_MODEL)),
        "ffn1_w_gate": nrm(ks[2], (L, D_MODEL, D_FF), D_MODEL ** -0.5),
        "ffn1_w_up": nrm(ks[3], (L, D_MODEL, D_FF), D_MODEL ** -0.5),
        "ffn1_w_down": nrm(ks[4], (L, D_FF, D_MODEL), D_FF ** -0.5),
        "mix_norm": gain(ks[5], (L, D_MODEL)),
        "w_in": nrm(ks[6], (L, D_MODEL, D_IN), D_MODEL ** -0.5),
        "gm_ln_g": gain(ks[7], (L, GM_WIDTH)),
        "gm_ln_b": nrm(ks[8], (L, GM_WIDTH), 0.02),
        "gm_w_s": nrm(ks[9], (L, GM_GROUPS, GM_BLOCK, GM_BLOCK), GM_BLOCK ** -0.5),
        "gm_b_s": 1.0 + nrm(ks[10], (L, GM_GROUPS, GM_BLOCK), 0.1),
        "dn_conv_w": nrm(ks[11], (L, DN_CONV, 3 * DN_WIDTH), DN_CONV ** -0.5),
        "dn_a_log": jnp.log(jax.random.uniform(ks[12], (L, DN_HEADS), f32, 1.0, 16.0)),
        "dn_dt_bias": dt + jnp.log(-jnp.expm1(-dt)),
        "dn_norm": gain(ks[14], (L, DN_HEAD_DIM)),
        "w_out": nrm(ks[15], (L, D_MIX, D_MODEL), D_MIX ** -0.5),
        "ffn2_norm": gain(ks[16], (L, D_MODEL)),
        "ffn2_w_gate": nrm(ks[17], (L, D_MODEL, D_FF), D_MODEL ** -0.5),
        "ffn2_w_up": nrm(ks[18], (L, D_MODEL, D_FF), D_MODEL ** -0.5),
        "ffn2_w_down": nrm(ks[19], (L, D_FF, D_MODEL), D_FF ** -0.5),
        "final_norm": gain(ks[20], (D_MODEL,)),
    }

def first_block(x, ffn1_norm, ffn1_w_gate, ffn1_w_up, ffn1_w_down, mix_norm, w_in,
              gm_ln_g, gm_ln_b, gm_w_s, gm_b_s, dn_conv_w, dn_a_log, dn_dt_bias, dn_norm,
              w_out, ffn2_norm, ffn2_w_gate, ffn2_w_up, ffn2_w_down, final_norm):
    B, T, _ = x.shape
    split_at = [GM_WIDTH, 2 * GM_WIDTH, 2 * GM_WIDTH + 3 * DN_WIDTH,
                2 * GM_WIDTH + 4 * DN_WIDTH, 2 * GM_WIDTH + 4 * DN_WIDTH + DN_HEADS]
    for l in range(DEPTH):
        x = x + 0.5 * swiglu(rmsnorm(x, ffn1_norm[l]), ffn1_w_gate[l], ffn1_w_up[l], ffn1_w_down[l])

        h = rmsnorm(x, mix_norm[l])
        p = h @ w_in[l]
        u_a, v_a, qkv, z, b_raw, a_raw = jnp.split(p, split_at, axis=-1)

        y_a = spatial_gating(jax.nn.gelu(u_a), jax.nn.gelu(v_a), gm_w_s[l], gm_b_s[l],
                             gm_ln_g[l], gm_ln_b[l])

        qkv = jax.nn.silu(causal_dwconv(qkv, dn_conv_w[l])).astype(jnp.float32)
        q, k, v = jnp.split(qkv, 3, axis=-1)
        q = l2norm(q.reshape(B, T, DN_HEADS, DN_HEAD_DIM))
        k = l2norm(k.reshape(B, T, DN_HEADS, DN_HEAD_DIM))
        v = v.reshape(B, T, DN_HEADS, DN_HEAD_DIM)
        beta = jax.nn.sigmoid(b_raw.astype(jnp.float32))
        g = -jnp.exp(dn_a_log[l].astype(jnp.float32)) * jax.nn.softplus(
            a_raw.astype(jnp.float32) + dn_dt_bias[l].astype(jnp.float32))
        o = gated_delta_rule(q, k, v, beta, g)
        zg = jax.nn.silu(z.astype(jnp.float32)).reshape(B, T, DN_HEADS, DN_HEAD_DIM)
        y_b = (rmsnorm(o, dn_norm[l]) * zg).reshape(B, T, DN_WIDTH).astype(x.dtype)

        x = x + jnp.concatenate([y_a, y_b], axis=-1) @ w_out[l]

        x = x + 0.5 * swiglu(rmsnorm(x, ffn2_norm[l]), ffn2_w_gate[l], ffn2_w_up[l], ffn2_w_down[l])
    return rmsnorm(x, final_norm)


N_META = 16
BLOCK = 128
PAD = BLOCK - N_META
HEAD_DIM = 64
SB_HEADS = 8
SB_WIDTH = SB_HEADS * HEAD_DIM
SWA_Q_HEADS = 16
SWA_KV_HEADS = 2
SWA_GROUP = SWA_Q_HEADS // SWA_KV_HEADS
SWA_WIDTH = SWA_Q_HEADS * HEAD_DIM
SWA_KV_WIDTH = SWA_KV_HEADS * HEAD_DIM
WINDOW = 128
ROPE_THETA = 10000.0
RMS_EPS = 1e-6
SPLITS = (SB_WIDTH, SB_WIDTH, SB_WIDTH, SWA_WIDTH, SWA_KV_WIDTH, SWA_KV_WIDTH, SB_WIDTH, SWA_WIDTH, D_MODEL, D_MODEL)
IN_COLS = sum(SPLITS)


def rms_norm(x, g):
    xf = x.astype(jnp.float32)
    y = xf * lax.rsqrt(jnp.mean(xf * xf, axis=-1, keepdims=True) + RMS_EPS)
    return (y * g.astype(jnp.float32)).astype(x.dtype)

def rope(x, pos):
    half = HEAD_DIM // 2
    inv = ROPE_THETA ** (-jnp.arange(half, dtype=jnp.float32) / half)
    ang = pos.astype(jnp.float32)[:, None] * inv[None, :]
    cos = jnp.cos(ang)[None, :, None, :]
    sin = jnp.sin(ang)[None, :, None, :]
    x1 = x[..., :half].astype(jnp.float32)
    x2 = x[..., half:].astype(jnp.float32)
    out = jnp.concatenate([x1 * cos - x2 * sin, x2 * cos + x1 * sin], axis=-1)
    return out.astype(x.dtype)

def stick_breaking_attention(q, k, v, valid):
    B, L, H, d = q.shape
    scale = d ** -0.5
    outs = []
    for blk in range(L // BLOCK):
        q0 = blk * BLOCK
        end = q0 + BLOCK
        z = jnp.einsum('bqhd,bkhd->bhqk', q[:, q0:end], k[:, :end],
                       preferred_element_type=jnp.float32) * scale
        t = q0 + jnp.arange(BLOCK)
        s = jnp.arange(end)
        mask = (s[None, :] < t[:, None]) & valid[None, :end]
        log_beta = jax.nn.log_sigmoid(z)
        log_1m = jnp.where(mask, log_beta - z, 0.0)
        rev = lax.cumsum(log_1m, axis=3, reverse=True)
        suffix = jnp.concatenate([rev[..., 1:], jnp.zeros_like(rev[..., :1])], axis=-1)
        w = jnp.where(mask, jnp.exp(log_beta + suffix), 0.0)
        outs.append(jnp.einsum('bhqk,bkhd->bqhd', w.astype(v.dtype), v[:, :end]))
    return jnp.concatenate(outs, axis=1)

def sliding_window_sink_attention(q, k, v, sinks, valid):
    B, L, Hq, d = q.shape
    nb = L // BLOCK
    scale = d ** -0.5
    qb = q.reshape(B, nb, BLOCK, SWA_KV_HEADS, SWA_GROUP, d)

    def band(t):
        tb = t.reshape(B, nb, BLOCK, SWA_KV_HEADS, d)
        prev = jnp.pad(tb[:, :-1], ((0, 0), (1, 0), (0, 0), (0, 0), (0, 0)))
        return jnp.concatenate([prev, tb], axis=2)

    kb, vb = band(k), band(v)
    vblk = valid.reshape(nb, BLOCK)
    kvalid = jnp.concatenate([jnp.pad(vblk[:-1], ((1, 0), (0, 0)), constant_values=False), vblk], axis=1)
    scores = jnp.einsum('bnqhgd,bnkhd->bnhgqk', qb, kb,
                        preferred_element_type=jnp.float32) * scale
    diff = (BLOCK + jnp.arange(BLOCK))[:, None] - jnp.arange(2 * BLOCK)[None, :]
    mask = ((diff >= 0) & (diff < WINDOW))[None] & kvalid[:, None, :]
    scores = jnp.where(mask[None, :, None, None], scores, -jnp.inf)
    sink = sinks.astype(jnp.float32).reshape(SWA_KV_HEADS, SWA_GROUP)[None, None, :, :, None, None]
    sink = jnp.broadcast_to(sink, scores.shape[:-1] + (1,))
    probs = jax.nn.softmax(jnp.concatenate([scores, sink], axis=-1), axis=-1)[..., :-1]
    o = jnp.einsum('bnhgqk,bnkhd->bnqhgd', probs.astype(v.dtype), vb)
    return o.reshape(B, L, Hq * d)

def second_inputs(seed: int = 0) -> dict:
    key = jax.random.key(seed)
    ks = jax.random.split(key, 10)
    f32 = jnp.float32
    x = jax.random.normal(ks[0], (BATCH, SEQ, D_MODEL), f32)
    meta_tokens = jax.random.normal(ks[1], (N_META, D_MODEL), f32)
    norm_gain = 1.0 + 0.02 * jax.random.normal(ks[2], (DEPTH, D_MODEL), f32)
    w_in = jax.random.normal(ks[3], (DEPTH, D_MODEL, IN_COLS), f32) * D_MODEL ** -0.5
    w_branch_sb = jax.random.normal(ks[4], (DEPTH, SB_WIDTH, D_MODEL), f32) * SB_WIDTH ** -0.5
    w_branch_swa = jax.random.normal(ks[5], (DEPTH, SWA_WIDTH, D_MODEL), f32) * SWA_WIDTH ** -0.5
    w_out = jax.random.normal(ks[6], (DEPTH, D_MODEL, D_MODEL), f32) * D_MODEL ** -0.5
    attn_sinks = jax.random.normal(ks[7], (DEPTH, SWA_Q_HEADS), f32)
    final_norm_gain = 1.0 + 0.02 * jax.random.normal(ks[8], (D_MODEL,), f32)
    return {"x": x, "meta_tokens": meta_tokens, "norm_gain": norm_gain, "w_in": w_in,
            "w_branch_sb": w_branch_sb, "w_branch_swa": w_branch_swa, "w_out": w_out,
            "attn_sinks": attn_sinks, "final_norm_gain": final_norm_gain}

def second_block(x, meta_tokens, norm_gain, w_in, w_branch_sb, w_branch_swa, w_out, attn_sinks, final_norm_gain):
    B = x.shape[0]
    meta = jnp.broadcast_to(meta_tokens[None].astype(x.dtype), (B, N_META, D_MODEL))
    pad = jnp.zeros((B, PAD, D_MODEL), x.dtype)
    h = jnp.concatenate([pad, meta, x], axis=1)
    L = h.shape[1]
    idx = jnp.arange(L)
    valid = idx >= PAD
    pos = idx - PAD
    offsets = [int(o) for o in np.cumsum(SPLITS)[:-1]]
    for l in range(DEPTH):
        xn = rms_norm(h, norm_gain[l])
        proj = xn @ w_in[l]
        sb_q, sb_k, sb_v, sw_q, sw_k, sw_v, sb_z, sw_z, g_sb, g_sw = jnp.split(proj, offsets, axis=-1)
        o_sb = stick_breaking_attention(sb_q.reshape(B, L, SB_HEADS, HEAD_DIM),
                                        sb_k.reshape(B, L, SB_HEADS, HEAD_DIM),
                                        sb_v.reshape(B, L, SB_HEADS, HEAD_DIM), valid).reshape(B, L, SB_WIDTH)
        q = rope(sw_q.reshape(B, L, SWA_Q_HEADS, HEAD_DIM), pos)
        k = rope(sw_k.reshape(B, L, SWA_KV_HEADS, HEAD_DIM), pos)
        o_sw = sliding_window_sink_attention(q, k, sw_v.reshape(B, L, SWA_KV_HEADS, HEAD_DIM),
                                             attn_sinks[l], valid)
        y_sb = (o_sb * jax.nn.silu(sb_z)) @ w_branch_sb[l]
        y_sw = (o_sw * jax.nn.silu(sw_z)) @ w_branch_swa[l]
        merged = jax.nn.sigmoid(g_sb) * y_sb + jax.nn.sigmoid(g_sw) * y_sw
        h = h + merged @ w_out[l]
    return rms_norm(h, final_norm_gain)[:, BLOCK:]


def setup_inputs(seed=0):
    out = dict(first_inputs(seed))
    for name, value in second_inputs(seed + 1).items():
        if name != "x":
            out[name + "_2"] = value
    return out


def reference(
    x, ffn1_norm, ffn1_w_gate, ffn1_w_up, ffn1_w_down, mix_norm, w_in, gm_ln_g, gm_ln_b, gm_w_s,
    gm_b_s, dn_conv_w, dn_a_log, dn_dt_bias, dn_norm, w_out, ffn2_norm, ffn2_w_gate, ffn2_w_up,
    ffn2_w_down, final_norm, meta_tokens_2, norm_gain_2, w_in_2, w_branch_sb_2, w_branch_swa_2,
    w_out_2, attn_sinks_2, final_norm_gain_2,
):
    x = first_block(
        x, ffn1_norm, ffn1_w_gate, ffn1_w_up, ffn1_w_down, mix_norm, w_in, gm_ln_g, gm_ln_b,
        gm_w_s, gm_b_s, dn_conv_w, dn_a_log, dn_dt_bias, dn_norm, w_out, ffn2_norm, ffn2_w_gate,
        ffn2_w_up, ffn2_w_down, final_norm,
    )
    return second_block(
        x, meta_tokens_2, norm_gain_2, w_in_2, w_branch_sb_2, w_branch_swa_2, w_out_2,
        attn_sinks_2, final_norm_gain_2,
    )


_drawn_inputs = setup_inputs


def setup_inputs(seed=0):
    import zlib

    import numpy as np

    out = dict(_drawn_inputs(seed))
    spreads = {}
    factors = {'gm_ln_g': 3.445,
     'gm_ln_b': 8.0,
     'dn_norm': 3.304,
     'ffn2_norm': 3.352,
     'norm_gain_2': 8.0,
     'attn_sinks_2': 8.0,
     'final_norm_gain_2': 2.702}
    for name, (base, spread) in spreads.items():
        noise = np.random.default_rng([zlib.crc32(name.encode()), seed]).standard_normal(out[name].shape)
        drawn = base * np.exp(spread * noise) if base else spread * noise
        out[name] = __import__('jax').numpy.asarray(drawn.astype(out[name].dtype))
    for name, factor in factors.items():
        out[name] = (out[name] * factor).astype(out[name].dtype)
    return out
```

```python
from contextlib import ExitStack

import numpy as np

import concourse.bass as bass
from concourse import mybir

P = 128
F32 = mybir.dt.float32
F32R = mybir.dt.float32r
ALU = mybir.AluOpType
ACT = mybir.ActivationFunctionType
AX_X = mybir.AxisListType.X

T = 512
D = 1024
KD = D // P
TT = T // P
FF = 2816
FP = FF // (2 * P)
SLAB = 2048
SC = SLAB // KD
META = 16
TM = META + T
CH = 64
NC = T // CH
H = 4
LEVELS = 6
GG = 8
HD = 64
NEG = -1e30

V_FFN1, V_MIX, V_FFN2, V_FIN1, V_N2, V_FIN2, V_DN, V_CONV = 0, 8, 16, 24, 32, 40, 48, 49
ROWS = V_CONV + 48

N_FFN1 = 0
N_MIX = N_FFN1 + 3 * FP
MIX_SLABS = (4, 5, 6, 7, 8, 9, 2, 3, 0, 1, 10, 11)
N_OUT1 = N_MIX + len(MIX_SLABS)
N_FFN2 = N_OUT1 + 4
N_P2 = N_FFN2 + 3 * FP
P2_SLABS = (0, 1, 2, 3, 4, 5, 10, 6, 7, 8, 9) + tuple(range(11, 25))
N_BR = N_P2 + len(P2_SLABS)
N_OUT2 = N_BR + 6
N_SLABS = N_OUT2 + 4


def constants():
    i, j = np.arange(P)[:, None], np.arange(P)[None, :]
    same = i // CH == j // CH
    f = lambda m: np.asarray(m, np.float32)
    ones = np.ones((P, P))
    base = [np.eye(P), ones, np.full((P, 8), 1e-6)]
    neg = lambda keep: np.where(keep, 0.0, NEG)
    mix = [same & (i <= j), same, (i // CH == 0) * ones, (i // CH == 1) * ones, neg(same & (i <= j)), neg(same & (j < i))]
    mix += [(i // (2 << s) == j // (2 << s)) & ((i >> s) % 2 == 1) & ((j >> s) % 2 == 0) for s in range(LEVELS)]
    prev = neg(j > i)
    own = neg(j <= i)
    att = [np.ones((P, 384)), j < i, neg(j < i), prev, own, (np.arange(T)[None, :] % META != META - 1) * np.ones((P, T))]
    half = HD // 2
    rot = np.zeros((P, P))
    for m in range(P):
        if m % HD < half:
            rot[m + half, m] = -1.0
        else:
            rot[m - half, m] = 1.0
    rope = [rot]
    for g in range(2):
        dup = np.zeros((P, P))
        for m in range(P):
            dup[g * HD + m % HD, m] = 1.0
        rope += [dup, dup @ rot]
    inv = np.float32(10000.0) ** (-np.arange(half, dtype=np.float32) / np.float32(half))
    ang = np.tile(inv, 4)[:, None] * np.arange(TM, dtype=np.float32)[None, :]
    rope += [np.cos(ang), np.sin(ang)]
    cat = lambda parts: np.ascontiguousarray(np.concatenate([f(m) for m in parts], axis=1))
    return {"c_base": cat(base), "c_mix": cat(mix), "c_att": cat(att), "c_rope": cat(rope)}


def program(nc, a, out):
    with ExitStack() as ctx:
        sem = lambda name: ctx.enter_context(nc.semaphore(name))
        cursor = [(nc.sbuf_base + 31) // 32 * 32]

        def sb(name, shape, dt=F32):
            t = nc.alloc_sbuf_tensor_at(name, shape, dt, offset=cursor[0])
            cursor[0] += (4 * int(np.prod(shape[1:])) + 31) // 32 * 32
            return t

        raw = sb("raw", [P, 2, SLAB])
        w_hi = sb("w_hi", [P, 2, SLAB], F32R)
        w_lo = sb("w_lo", [P, 2, SLAB], F32R)
        xT = sb("xT", [P, KD, T])
        xn_hi = sb("xn_hi", [P, KD, TM], F32R)
        xn_lo = sb("xn_lo", [P, KD, TM], F32R)
        base_c = sb("base_c", [P, 2 * P + 8])
        ident, ones, epsc = base_c[:, 0:P], base_c[:, P:2 * P], base_c[:, 2 * P:2 * P + 1]
        rows_at = cursor[0]
        rows = sb("rows", [P, P])
        cols = sb("cols", [P, P])
        rstd = sb("rstd", [P, T])
        hvec = sb("hvec", [P, 2, 4])
        sinks = sb("sinks", [P, 16])
        tiny = sb("tiny", [P, 48])
        sq = sb("sq", [P, 2, T])
        smalls_at = cursor[0]
        sumsq = sb("sumsq", [P, T])
        gs = sb("gs", [P, 2, T])
        hf = sb("hf", [P, 2, T])
        region = cursor[0]

        h_hi = sb("h_hi", [P, 2 * FP, T], F32R)
        h_lo = sb("h_lo", [P, 2 * FP, T], F32R)
        assert cursor[0] <= nc.sbuf_usable_end
        cursor[0] = region
        xload = sb("xload", [P, TT, D])
        meta_in = sb("meta_in", [META, D])
        meta_sq = sb("meta_sq", [META, D])
        meta_f = sb("meta_f", [P, KD, META])

        cursor[0] = region
        mixm = sb("mixm", [P, 12, P])
        cumT, same, half0, half1 = (mixm[:, n] for n in range(4))
        neg_incl, neg_strict = mixm[:, 4], mixm[:, 5]
        wba_lo = sb("wba_lo", [P, KD, 8], F32R)
        here, cursor[0] = cursor[0], rows_at
        wba = sb("wba", [P, KD, 8])
        wba_hi = sb("wba_hi", [P, KD, 8], F32R)
        cursor[0] = here
        qkv = sb("qkv", [P, 12, T])
        cursor[0] -= 4 * T * 4
        ya = sb("ya", [P, 4, T])
        rw_at = cursor[0]
        rw = sb("rw", [P, 2, T + 8])
        cursor[0] = rw_at
        lnc = sb("lnc", [P, 2, T])
        cursor[0] = rw_at
        vnew = sb("vnew", [P, T])
        cursor[0] = rw_at + 2 * 4 * (T + 8)
        vb = sb("vb", [P, H, T])
        kb = sb("kb", [P, H, T])
        kd = sb("kd", [P, H, T])
        Z = sb("Z", [P, H, T])
        tmp_at = cursor[0]
        Tm = sb("Tm", [P, 2, T])
        Mm = sb("Mm", [P, 2, T])
        Pp = sb("Pp", [P, 2, T])
        cursor[0] = tmp_at
        wsraw = sb("wsraw", [P, GG, P])
        cursor[0] = tmp_at
        zT = sb("zT", [P, 4, T])
        S = sb("S", [P, 2, T])
        vtok = sb("vtok", [P, TT, T])
        wsT = sb("wsT", [P, GG, P])
        bs = sb("bs", [P, 4, P])
        assert cursor[0] <= nc.sbuf_usable_end
        cursor[0] = smalls_at
        sm = sb("sm", [P, 14, 16])
        s_e, s_beta, s_a, s_t, s_g, s_ea = (sm[:, n] for n in range(6))
        s_c = sm[:, 6:10]
        s_ngc, s_kd, s_eg, s_be = (sm[:, n] for n in range(10, 14))
        egl = sb("egl", [P, 2, 16])
        st6 = sb("st6", [P, 4, 6])
        mv = sb("mv", [P, 4, 2])
        rln = sb("rln", [P, 4])

        cursor[0] = region
        Qs = sb("Qs", [P, 4, T])
        Ks = sb("Ks", [P, 4, TM])
        Vs = sb("Vs", [P, TT, T])
        Vm = sb("Vm", [META, T])
        zs = sb("zs", [P, 12, T])
        qw_at = cursor[0]
        Qw = sb("Qw", [P, 8, T])
        Kw = sb("Kw", [P, 2, TM])
        Vw = sb("Vw", [P, TT, P])
        Vwm = sb("Vwm", [META, P])
        attm = sb("attm", [P, 1408])
        scan_mask, neg_diag, win_mask, meta_mask = attm[:, 0:512], attm[:, 512:640], attm[:, 640:896], attm[:, 896:1408]
        work_at = cursor[0]
        ropec = sb("ropec", [P, 5 * P + 2 * TM])
        rot_q = ropec[:, 0:P]
        dup_k = [ropec[:, (1 + 2 * g) * P:(2 + 2 * g) * P] for g in range(2)]
        rot_k = [ropec[:, (2 + 2 * g) * P:(3 + 2 * g) * P] for g in range(2)]
        cosT, sinT = ropec[:, 5 * P:5 * P + TM], ropec[:, 5 * P + TM:]
        kraw = sb("kraw", [P, TM])
        cursor[0] = work_at
        wT = sb("wT", [P, 2, T])
        argm = sb("argm", [P, T])
        ctok = sb("ctok", [P, 32])
        wm = sb("wm", [P, 2, HD])
        wTm = sb("wTm", [META, T])
        assert cursor[0] <= nc.sbuf_usable_end
        cursor[0] = region
        g_lowt = sb("g_lowt", [P, 12, T])
        ost_at = region
        cursor[0] = qw_at
        g_hight = sb("g_hight", [P, 4, T])
        asb_hi = sb("asb_hi", [P, 4, T], F32R)
        asb_lo = sb("asb_lo", [P, 4, T], F32R)
        mg_lo = sb("mg_lo", [P, KD, T], F32R)
        assert cursor[0] <= nc.sbuf_usable_end
        cursor[0] = qw_at - 8 * T * 4
        mg_hi = sb("mg_hi", [P, KD, T], F32R)
        cursor[0] = ost_at
        ost = sb("ost", [P, TT, D])
        gt = lambda t: g_lowt[:, t] if t < 12 else g_hight[:, t - 12]

        banks = [ctx.enter_context(nc.psum_tensor(f"bank{i}", [P, 512], F32)) for i in range(8)]

        def quarters(ap):
            return ap.rearrange("p (a b) -> p a b", a=4)

        def over4(ap):
            return ap.unsqueeze(1).to_broadcast([P, 4, P])

        def per_block(ap):
            return ap.unsqueeze(2).to_broadcast([P, 4, P])

        x_loaded, consts, rows_in = sem("x_loaded"), sem("consts"), sem("rows_in")
        slab_loaded = [sem("slab_loaded0"), sem("slab_loaded1")]
        hi_done, split_done = sem("hi_done"), sem("split_done")
        eighths = sem("eighths")
        xT_mm, x_ready, cols_ready = sem("xT_mm"), sem("x_ready"), sem("cols_ready")
        sq_done, acc_done, stat_mm, ln_done, rstd_done = (
            sem(s) for s in ("sq_done", "acc_done", "stat_mm", "ln_done", "rstd_done"))
        xf_done, xhi_done, xlo_done = sem("xf_done"), sem("xhi_done"), sem("xlo_done")
        meta_act, meta_dve, meta_mm, meta_loaded = sem("meta_act"), sem("meta_dve"), sem("meta_mm"), sem("meta_loaded")
        out_done = sem("out_done")

        class FfnSems:
            def __init__(self, n):
                self.silu, self.hmul, self.h_hi, self.h_lo = (sem(f"{n}_{s}") for s in ("silu", "hmul", "h_hi", "h_lo"))
        F1, F2 = FfnSems("ffn1"), FfnSems("ffn2")

        mix_in, lnc_in = sem("mix_in"), sem("lnc_in")
        rw_done, conv_step, conv_done, qkv_done = sem("rw_done"), sem("conv_step"), sem("conv_done"), sem("qkv_done")
        ba_split, ba_mm, act_sm, dve_sm, cum_mm = sem("ba_split"), sem("ba_mm"), sem("act_sm"), sem("dve_sm"), sem("cum_mm")
        ws_mm, ws_done = sem("ws_mm"), sem("ws_done")
        l2sq, l2mm, l2rn, l2n, va_done = sem("l2sq"), sem("l2mm"), sem("l2rn"), sem("l2n"), sem("va_done")
        r_mm, kk_mm, kq_mm, kt_mm, vt_mm = sem("r_mm"), sem("kk_mm"), sem("kq_mm"), sem("kt_mm"), sem("vt_mm")
        rs_done, er_done, exp_done = sem("rs_done"), sem("er_done"), sem("exp_done")
        arg_done, at_done, qd_done, l_done, tok_done, vb_done = (
            sem(s) for s in ("arg_done", "at_done", "qd_done", "l_done", "tok_done", "vb_done"))
        ln_st, ln_act, ln_app = sem("ln_st"), sem("ln_act"), sem("ln_app")
        m_done, t_init, z_mm0, pp_mm, pp_copy, zt_mm, z_sub, t_sub = (
            sem(s) for s in ("m_done", "t_init", "z_mm0", "pp_mm", "pp_copy", "zt_mm", "z_sub", "t_sub"))
        nw_mm, nw_done, sgu_mm, ya_done = sem("nw_mm"), sem("nw_done"), sem("sgu_mm"), sem("ya_done")
        vn_mm, vn_done, su_mm, s_done, o_mm, f_ev, ya_mul = (
            sem(s) for s in ("vn_mm", "vn_done", "su_mm", "s_done", "o_mm", "f_ev", "ya_mul"))
        ob_done, ob_sq, ob_mm, ob_rn, ob_nrm, yb_done, y_hi, y_lo = (
            sem(s) for s in ("ob_done", "ob_sq", "ob_mm", "ob_rn", "ob_nrm", "yb_done", "y_hi", "y_lo"))
        att_in, p_ev, kr_mm, kr_st, kr_done, rot_mm, rp_st, rope_done = (
            sem(s) for s in ("att_in", "p_ev", "kr_mm", "kr_st", "kr_done", "rot_mm", "rp_st", "rope_done"))
        zm_mm, am_st, gm_st, z_mm, a_st, d_st, g_done, w_done, x_mm, e_done, pv_mm = (
            sem(s) for s in ("zm_mm", "am_st", "gm_st", "z_mm", "a_st", "d_st", "g_done", "w_done", "x_mm", "e_done", "pv_mm"))
        tm_done, wm_done, xm_mm, em_done, pvm_mm, o1_done, f2_ev = (
            sem(s) for s in ("tm_done", "wm_done", "xm_mm", "em_done", "pvm_mm", "o1_done", "f2_ev"))
        zsilu, bz_done = sem("zsilu"), sem("bz_done")
        z2_mm, s_st, s2_done, p2_done, n_st, pn_done, x2_mm, e2_done, pv2_mm, o2_done = (
            sem(s) for s in ("z2_mm", "s_st", "s2_done", "p2_done", "n_st", "pn_done", "x2_mm", "e2_done", "pv2_mm", "o2_done"))
        a_hi, a_lo, sb_ev, sw_st, mg_done, mghi_done, mglo_done = (
            sem(s) for s in ("a_hi", "a_lo", "sb_ev", "sw_st", "mg_done", "mghi_done", "mglo_done"))
        fin_done, ft_mm, ost_a, ost_v = sem("fin_done"), sem("ft_mm"), sem("ost_a"), sem("ost_v")

        xf = lambda d: (gs[:, 0], gs[:, 1], hf[:, 0], hf[:, 1])[d % 4]
        qT = lambda h: qkv[:, h]
        kT = lambda h: qkv[:, 4 + h]
        vT = lambda h: qkv[:, 8 + h]
        atT, Lm = kT, vT
        w3 = lambda u: (gs[:, 0], gs[:, 1], hf[:, 0])[u % 3]
        EV_K, EV_V, EV_KW, EV_VW, EV_QW = 4, 12, 18, 20, 22

        block = ctx.enter_context(nc.Block())

        @block.sync
        def _(sp):
            def load(n, src, slot=None):
                slot = n % 2 if slot is None else slot
                if not isinstance(n, int) or n >= 2:
                    sp.wait_ge(split_done, n - 1)
                sp.dma_start(raw[:, slot, :].rearrange("p (k c) -> p k c", k=src.shape[1]), src).then_inc(slab_loaded[slot], 16)

            def ffn(n0, wg, wu, wd):
                g = wg.rearrange("(k p) f -> p k f", p=P)
                u = wu.rearrange("(k p) f -> p k f", p=P)
                d = wd.rearrange("(k p) c -> p k c", p=P)
                load(n0, g[:, :, 0:SC])
                load(n0 + 1, u[:, :, 0:SC])
                with sp.Fori(1, FP) as i:
                    load(n0 + 2 * i, g[:, :, bass.ds(i * SC, SC)], n0 % 2)
                    load(n0 + 2 * i + 1, u[:, :, bass.ds(i * SC, SC)], (n0 + 1) % 2)
                n1 = n0 + 2 * FP
                with sp.Fori(0, FP // 2) as j:
                    load(n1 + 2 * j, d[:, bass.ds(j * 4, 2), :], n1 % 2)
                    load(n1 + 2 * j + 1, d[:, bass.ds(j * 4 + 2, 2), :], (n1 + 1) % 2)
                load(n1 + FP - 1, d[:, 2 * FP - 2:2 * FP, :])

            def columns(n0, w, slabs):
                v = w.rearrange("(k p) c -> p k c", p=P)
                for i, s in enumerate(slabs):
                    load(n0 + i, v[:, :, s * SC:(s + 1) * SC])

            vectors = (("ffn1_norm", V_FFN1, 8), ("mix_norm", V_MIX, 8), ("ffn2_norm", V_FFN2, 8), ("norm_gain_2", V_N2, 8), ("dn_norm", V_DN, 1))
            sp.dma_start(base_c[:], a["c_base"]).then_inc(consts, 16)
            for name, r, n in vectors:
                sp.dma_start(rows[r:r + n, :], a[name].rearrange("b (k p) -> (b k) p", p=P)).then_inc(rows_in, 16)
            for name, r in (("final_norm", V_FIN1), ("final_norm_gain_2", V_FIN2)):
                sp.dma_start(rows[r:r + 8, :], a[name].rearrange("(k p) -> k p", p=P)).then_inc(rows_in, 16)
            sp.dma_start(rows[V_CONV:V_CONV + 48, :], a["dn_conv_w"][0].rearrange("j (c p) -> (j c) p", p=P)).then_inc(rows_in, 16)
            xv = a["x"].rearrange("b (t p) d -> (b p) t d", p=P)
            for t in range(TT):
                sp.dma_start(xload[:, t, :], xv[:, t, :]).then_inc(x_loaded, 16)
            sp.dma_start(meta_in[:], a["meta_tokens_2"]).then_inc(meta_loaded, 16)
            sp.dma_start(hvec[:, 0, :], a["dn_dt_bias"][0].partition_broadcast(P)).then_inc(consts, 16)
            sp.dma_start(hvec[:, 1, :], a["dn_a_log"][0].partition_broadcast(P)).then_inc(consts, 16)
            sp.dma_start(sinks[:], a["attn_sinks_2"][0].partition_broadcast(P)).then_inc(consts, 16)
            ffn(N_FFN1, a["ffn1_w_gate"][0], a["ffn1_w_up"][0], a["ffn1_w_down"][0])
            sp.wait_ge(eighths, 8 * N_MIX)
            sp.dma_start(mixm[:].rearrange("p a b -> p (a b)"), a["c_mix"]).then_inc(mix_in, 16)
            with nc.allow_non_contiguous_dma(reason="eight columns of a row"):
                sp.dma_start(wba[:], a["w_in"][0].rearrange("(k p) c -> p k c", p=P)[:, :, 3072:3080]).then_inc(mix_in, 16)
            sp.dma_start(wsraw[:], a["gm_w_s"][0].rearrange("g i j -> i g j")).then_inc(mix_in, 16)
            bsv = a["gm_b_s"][0].rearrange("(m two) i -> two m i", two=2)
            for half in range(2):
                sp.dma_start(bs[64 * half:64 * half + 64], bsv[half].partition_broadcast(64)).then_inc(mix_in, 16)
            columns(N_MIX, a["w_in"][0], MIX_SLABS[0:7])
            sp.wait_ge(conv_done, 12)
            sp.dma_start(lnc[:, 0, :], a["gm_ln_g"][0].partition_broadcast(P)).then_inc(lnc_in, 16)
            sp.dma_start(lnc[:, 1, :], a["gm_ln_b"][0].partition_broadcast(P)).then_inc(lnc_in, 16)
            columns(N_MIX + 7, a["w_in"][0], MIX_SLABS[7:])
            columns(N_OUT1, a["w_out"][0], range(4))
            ffn(N_FFN2, a["ffn2_w_gate"][0], a["ffn2_w_up"][0], a["ffn2_w_down"][0])
            sp.wait_ge(eighths, 8 * N_P2)
            sp.dma_start(attm[:], a["c_att"]).then_inc(att_in, 16)
            sp.dma_start(ropec[:], a["c_rope"]).then_inc(att_in, 16)
            columns(N_P2, a["w_in_2"][0], P2_SLABS)
            wsb = a["w_branch_sb_2"][0].rearrange("(k p) c -> p k c", p=P)
            for i in range(2):
                load(N_BR + 3 * i, wsb[:, :, i * 512:(i + 1) * 512])
                columns(N_BR + 3 * i + 1, a["w_branch_swa_2"][0], (2 * i, 2 * i + 1))
            columns(N_OUT2, a["w_out_2"][0], range(4))
            ov = out[0].rearrange("(t p) d -> t p d", p=P)
            for t in range(TT):
                sp.wait_ge(ost_a, t + 1)
                sp.wait_ge(ost_v, t + 1)
                sp.dma_start(ov[t], ost[:, t]).then_inc(out_done, 16)
            sp.wait_ge(out_done, 16 * TT)

        @block.gpsimd
        def _(pool):
            parts = pool.alloc_register("high_parts")

            def split(n, slot, loads):
                pool.wait_ge(slab_loaded[slot], 16 * loads)
                if not isinstance(n, int) or n >= 2:
                    pool.wait_ge(eighths, 8 * (n - 1))
                done = n + 1
                if not isinstance(n, int):
                    pool.reg_add(parts, parts, 1)
                    done = parts
                nc.gpsimd.tensor_scalar(w_hi[:, slot], raw[:, slot], 1.0, 0.0, ALU.mult, ALU.add).then_inc(hi_done, 1)
                pool.wait_ge(hi_done, done)
                nc.gpsimd.tensor_tensor(w_lo[:, slot], raw[:, slot], w_hi[:, slot].bitcast(F32), ALU.subtract).then_inc(split_done, 1)
            split(0, 0, 1)
            split(1, 1, 1)
            pool.reg_mov(parts, 2)
            with pool.Fori(1, N_SLABS // 2) as i:
                split(2 * i, 0, i + 1)
                split(2 * i + 1, 1, i + 1)
            if N_SLABS % 2:
                split(N_SLABS - 1, 0, N_SLABS // 2 + 1)

        @block.scalar
        def _(act):
            A = nc.scalar.activation

            def norm(q):
                for d in range(KD):
                    act.wait_ge(x_ready, 8 * q + d + 1)
                    if 8 * q + d >= 2:
                        act.wait_ge(acc_done, 8 * q + d - 1)
                    A(sq[:, d % 2], xT[:, d], ACT.Square).then_inc(sq_done, 1)
                act.preload_act_table_set("natural_log_exp_and_others")
                act.wait_ge(stat_mm, q + 1)
                A(rstd[:], banks[4][:], ACT.Ln, bias=epsc, scale=1.0 / D).then_inc(ln_done, 1)
                act.wait_ge(ln_done, q + 1)
                A(rstd[:], rstd[:], ACT.Exp, scale=-0.5).then_inc(rstd_done, 1)

            def norm_hi(q):
                for d in range(KD):
                    act.wait_ge(xf_done, 8 * q + d + 1)
                    nc.scalar.copy(xn_hi[:, d, META:TM], xf(d)).then_inc(xhi_done, 1)

            def ffn(S_, n0):
                def pair(i, guard):
                    for f in range(2):
                        act.wait_ge(eighths, 8 * (n0 + 2 * i) + 4 * f + 4)
                        if guard:
                            act.wait_ge(S_.hmul, 2 * i + f - 1)
                        A(gs[:, f], banks[f][:], ACT.Silu).then_inc(S_.silu, 1)
                    for f in range(2):
                        act.wait_ge(S_.hmul, 2 * i + f + 1)
                        dst = h_hi[:, bass.ds(2 * i + f, 1), :] if guard else h_hi[:, f:f + 1, :]
                        nc.scalar.copy(dst.rearrange("p a t -> p (a t)"), hf[:, f]).then_inc(S_.h_hi, 1)
                pair(0, False)
                with act.Fori(1, FP) as i:
                    pair(i, True)

            act.wait_ge(consts, 64)
            act.wait_ge(meta_loaded, 16)
            A(meta_sq[:], meta_in[:], ACT.Square, accum_out=tiny[0:META, 0:1]).then_inc(meta_act, 1)
            act.preload_act_table_set("natural_log_exp_and_others")
            act.wait_ge(meta_act, 1)
            A(tiny[0:META, 1:2], tiny[0:META, 0:1], ACT.Ln, bias=epsc[0:META], scale=1.0 / D).then_inc(meta_act, 1)
            act.wait_ge(meta_act, 2)
            A(tiny[0:META, 2:3], tiny[0:META, 1:2], ACT.Exp, scale=-0.5).then_inc(meta_act, 1)
            norm(0)
            act.wait_ge(meta_dve, 2)
            nc.scalar.copy(xn_hi[:, :, 0:META], meta_f[:]).then_inc(meta_act, 1)
            norm_hi(0)
            ffn(F1, N_FFN1)

            norm(1)
            norm_hi(1)
            act.wait_ge(mix_in, 80)
            nc.scalar.copy(wba_hi[:], wba[:]).then_inc(ba_split, 1)
            act.preload_act_table(ACT.Silu)
            for j in range(13):
                if j < 12:
                    act.wait_ge(eighths, 8 * N_MIX + 4 * j + 4)
                    if j >= 2:
                        act.wait_ge(conv_done, j - 1)
                    nc.scalar.copy(rw[:, j % 2, 3:3 + T], banks[j % 4][:]).then_inc(rw_done, 1)
                if j:
                    act.wait_ge(conv_done, j)
                    A(qkv[:, j - 1], hf[:, (j - 1) % 2], ACT.Silu).then_inc(qkv_done, 1)
            act.preload_act_table_set("natural_log_exp_and_others")
            hp = lambda ap: ap.rearrange("p (h t) -> p h t", h=4)
            ba = banks[4][:, 0:32].rearrange("p (t c) -> p c t", c=8)
            act.wait_ge(ba_mm, 1)
            A(hp(s_e), ba[:, 0:4], ACT.Exp, scale=-1.0).then_inc(act_sm, 1)
            act.wait_ge(dve_sm, 1)
            A(s_t, s_a, ACT.Abs).then_inc(act_sm, 1)
            act.wait_ge(act_sm, 2)
            A(s_t, s_t, ACT.Exp, scale=-1.0).then_inc(act_sm, 1)
            act.wait_ge(act_sm, 3)
            A(s_t, s_t, ACT.Ln, bias=1.0).then_inc(act_sm, 1)
            A(s_ea[:, 0:4], hvec[:, 1], ACT.Exp).then_inc(act_sm, 1)
            act.wait_ge(dve_sm, 6)
            A(s_eg, s_c[:, 0], ACT.Exp).then_inc(act_sm, 1)
            act.wait_ge(dve_sm, 8)
            A(s_kd, s_kd, ACT.Exp).then_inc(act_sm, 1)
            A(egl[:], s_c[:, 2:4], ACT.Exp).then_inc(act_sm, 1)

            def l2_root(j):
                act.wait_ge(l2mm, j + 1)
                if j >= 2:
                    act.wait_ge(l2n, j - 1)
                A(gs[:, j % 2], banks[4 + j % 2][:], ACT.Ln, bias=epsc).then_inc(l2rn, 1)
                act.wait_ge(l2rn, 2 * j + 1)
                A(gs[:, j % 2], gs[:, j % 2], ACT.Exp, scale=-0.5).then_inc(l2rn, 1)
            for j in range(9):
                if j < 8:
                    act.wait_ge(qkv_done, j + 1)
                    if j >= 2:
                        act.wait_ge(l2mm, j - 1)
                    A(sq[:, j % 2], qkv[:, j], ACT.Square).then_inc(l2sq, 1)
                if j:
                    l2_root(j - 1)
            for b in range(4):
                act.wait_ge(eighths, 8 * (N_MIX + 6) + 4 * b + 4)
                A(vtok[:, 2 * (b % 2):2 * (b % 2) + 2, (b // 2) * SC:(b // 2 + 1) * SC],
                  banks[(6, 7, 0, 1)[b]][:].rearrange("p (a b) -> p a b", a=2), ACT.Gelu_apprx_tanh).then_inc(va_done, 1)
            act.preload_act_table_set("natural_log_exp_and_others")
            for h in range(H):
                act.wait_ge(r_mm, h + 1)
                if h:
                    act.wait_ge(arg_done, 2 * h)
                    act.wait_ge(er_done, h)
                else:
                    act.wait_ge(l2n, 8)
                nc.scalar.copy(gs[:, 0], banks[2][:]).then_inc(rs_done, 1)
                act.wait_ge(rs_done, h + 1)
                if h:
                    act.wait_ge(qd_done, h)
                A(gs[:, 1], gs[:, 0], ACT.Exp).then_inc(er_done, 1)
                for part, bias in ((0, s_ngc), (1, s_c[:, 0])):
                    act.wait_ge(arg_done, 2 * h + part + 1)
                    for p in range(4):
                        A(sq[:, part, p * P:(p + 1) * P], sq[:, part, p * P:(p + 1) * P], ACT.Exp,
                          bias=bias[:, 4 * h + p:4 * h + p + 1]).then_inc(exp_done, 1)
            act.wait_ge(ln_st, 8)
            A(rln[:], mv[:, :, 1], ACT.Ln, bias=epsc).then_inc(ln_act, 1)
            act.wait_ge(ln_act, 1)
            A(rln[:], rln[:], ACT.Exp, scale=-0.5).then_inc(ln_act, 1)
            for g in range(2):
                for level in range(1, LEVELS):
                    for hh in range(2):
                        n = (g * (LEVELS - 1) + level - 1) * 2 + hh
                        act.wait_ge(pp_mm, n + 1)
                        if n >= 2:
                            act.wait_ge(zt_mm, n - 1)
                        nc.scalar.copy(Pp[:, hh], banks[hh][:]).then_inc(pp_copy, 1)
            for h in range(H):
                act.wait_ge(nw_mm, h + 1)
                nc.scalar.mul(kb[:, h], banks[6 + h % 2][:], -1.0).then_inc(nw_done, 1)
            for c in range(NC):
                act.wait_ge(eighths, 8 * (N_MIX + 8) + 4 * c + 4)
                if c < 4:
                    if c >= 2:
                        act.wait_ge(ya_mul, c - 1)
                    A(gs[:, c % 2], banks[6 + c % 2][:], ACT.Gelu_apprx_tanh).then_inc(f_ev, 1)
                else:
                    A(zT[:, c - 4], banks[6 + c % 2][:], ACT.Silu).then_inc(f_ev, 1)
            act.preload_act_table_set("natural_log_exp_and_others")
            for m in range(4):
                act.wait_ge(ya_mul, 4)
                act.wait_ge(eighths, 8 * N_OUT1)
                nc.scalar.copy(xn_hi[:, m, META:TM], ya[:, m]).then_inc(y_hi, 1)
            for h in range(H + 1):
                if h < H:
                    act.wait_ge(ob_done, h + 1)
                    if h >= 2:
                        act.wait_ge(ob_mm, h - 1)
                    A(sq[:, h % 2], vb[:, h], ACT.Square).then_inc(ob_sq, 1)
                if h:
                    e = h - 1
                    act.wait_ge(ob_mm, e + 1)
                    if e >= 2:
                        act.wait_ge(ob_nrm, e - 1)
                    A(gs[:, e % 2], banks[4 + e % 2][:], ACT.Ln, bias=epsc, scale=1.0 / P).then_inc(ob_rn, 1)
                    act.wait_ge(ob_rn, 2 * e + 1)
                    A(gs[:, e % 2], gs[:, e % 2], ACT.Exp, scale=-0.5).then_inc(ob_rn, 1)
            for h in range(H):
                act.wait_ge(yb_done, h + 1)
                nc.scalar.copy(xn_hi[:, 4 + h, META:TM], vb[:, h]).then_inc(y_hi, 1)

            norm(2)
            norm_hi(2)
            ffn(F2, N_FFN2)
            norm(3)

            norm(4)
            norm_hi(3)
            for j in range(4):
                act.wait_ge(eighths, 8 * N_P2 + 4 * j + 4)
                nc.scalar.mul(Qs[:, j], banks[j % 2][:], 0.125).then_inc(p_ev, 1)
            for j in range(4):
                act.wait_ge(eighths, 8 * (N_P2 + 2) + 4 * j + 4)
                for half in range(2):
                    nc.scalar.copy(Ks[:, j, 264 * half:264 * half + 264], banks[2 * (j % 2) + half][:, 0:264]).then_inc(p_ev, 1)
            for s in range(2):
                for b in range(2):
                    act.wait_ge(eighths, 8 * (N_P2 + 4 + s) + 4 * b + 4)
                    nc.scalar.copy(Vs[:, 2 * b:2 * b + 2, s * SC:(s + 1) * SC], banks[4 + b][:].rearrange("p (a b) -> p a b", a=2)).then_inc(p_ev, 1)
                nc.scalar.copy(Vm[:, s * SC:(s + 1) * SC], banks[6][0:META, 0:SC]).then_inc(p_ev, 1)
            act.wait_ge(eighths, 8 * (N_P2 + 6) + 4)
            act.wait_ge(att_in, 32)
            for half in range(2):
                nc.scalar.copy(kraw[:, 264 * half:264 * half + 264], banks[half][:, 0:264]).then_inc(p_ev, 1)
            act.wait_ge(eighths, 8 * (N_P2 + 6) + 8)
            nc.scalar.copy(Vw[:].rearrange("p a b -> p (a b)"), banks[4][:]).then_inc(p_ev, 1)
            nc.scalar.copy(Vwm[:], banks[6][0:META, 0:P]).then_inc(p_ev, 1)
            for j in range(8):
                act.wait_ge(eighths, 8 * (N_P2 + 7) + 4 * j + 4)
                if j >= 2:
                    act.wait_ge(rope_done, j - 1)
                    act.wait_ge(rp_st, 2 * (j - 1))
                nc.scalar.mul(gs[:, j % 2], banks[j % 2][:], 0.125).then_inc(p_ev, 1)

            def fill_ev(t):
                act.wait_ge(eighths, 8 * (N_P2 + 11) + 4 * t + 4)
                if t < 12:
                    nc.scalar.copy(zs[:, t], banks[6 + t % 2][:]).then_inc(f2_ev, 1)
                else:
                    A(gt(t - 12), banks[6 + t % 2][:], ACT.Tanh, scale=0.5).then_inc(f2_ev, 1)

            act.preload_act_table_set("natural_log_exp_and_others")
            for half in range(2):
                act.wait_ge(zm_mm, half + 1)
                A(sq[:, 0, 256 * half:256 * half + 256], banks[2 + half][:, 0:256], ACT.Abs).then_inc(am_st, 1)
            act.wait_ge(am_st, 2)
            A(sq[:, 0], sq[:, 0], ACT.Exp, scale=-1.0).then_inc(am_st, 1)
            act.wait_ge(am_st, 3)
            A(sq[:, 0], sq[:, 0], ACT.Ln, bias=1.0).then_inc(am_st, 1)
            act.wait_ge(gm_st, 2)
            for step in range(32 + 3):
                u = step
                if u < 32:
                    n = (u % 4 + 1) * P
                    act.wait_ge(z_mm, u + 1)
                    if u >= 2:
                        act.wait_ge(g_done, u - 1)
                    A(sq[:, u % 2, 0:n], banks[u % 2][:, 0:n], ACT.Abs).then_inc(a_st, 1)
                    act.wait_ge(a_st, 3 * u + 1)
                    A(sq[:, u % 2, 0:n], sq[:, u % 2, 0:n], ACT.Exp, scale=-1.0).then_inc(a_st, 1)
                    act.wait_ge(a_st, 3 * u + 2)
                    A(sq[:, u % 2, 0:n], sq[:, u % 2, 0:n], ACT.Ln, bias=1.0).then_inc(a_st, 1)
                u = step - 1
                if 0 <= u < 32:
                    n = (u % 4 + 1) * P
                    act.wait_ge(g_done, u + 1)
                    A(w3(u)[:, 0:n], w3(u)[:, 0:n], ACT.Exp).then_inc(w_done, 1)
                    if u % 4 == 3:
                        h = u // 4
                        act.wait_ge(tm_done, h + 1)
                        A(wm[:, h % 2], wm[:, h % 2], ACT.Exp).then_inc(wm_done, 1)
                u = step - 2
                if 0 <= u < 32:
                    n = (u % 4 + 1) * P
                    act.wait_ge(x_mm, u + 1)
                    if u >= 2:
                        act.wait_ge(pv_mm, u - 1)
                    nc.scalar.copy(wT[:, u % 2, 0:n], banks[2 + u % 2][:, 0:n]).then_inc(e_done, 1)
                    if u % 4 == 3:
                        h = u // 4
                        act.wait_ge(xm_mm, h + 1)
                        if h:
                            act.wait_ge(pvm_mm, h)
                        nc.scalar.copy(wTm[:], banks[5][0:META, :]).then_inc(em_done, 1)
                if step < 32 and (3 * step + 3) // 8 > 3 * step // 8:
                    fill_ev(3 * step // 8)
            act.preload_act_table(ACT.Silu)
            for t in range(12):
                act.wait_ge(f2_ev, t + 1)
                A(zs[:, t], zs[:, t], ACT.Silu).then_inc(zsilu, 1)
            act.preload_act_table_set("exp_and_others")
            for step in range(32 + 3):
                v = step
                if v < 32:
                    o = 112 if v % 4 == 0 else 0
                    s2 = w3(v).rearrange("p (a b) -> p a b", a=2)
                    act.wait_ge(s2_done, v + 1)
                    if v >= 2:
                        act.wait_ge(pn_done, v - 1)
                    for i in range(2):
                        A(s2[:, i, o:], s2[:, i, o:], ACT.Exp, bias=tiny[:, 8 * (v % 2) + 2 + i:8 * (v % 2) + 3 + i],
                          accum_out=tiny[:, 16 + 4 * (v % 2) + i:17 + 4 * (v % 2) + i]).then_inc(p2_done, 1)
                    A(tiny[:, 18 + 4 * (v % 2):20 + 4 * (v % 2)], tiny[:, 8 * (v % 2) + 4:8 * (v % 2) + 6], ACT.Exp).then_inc(p2_done, 1)
                v = step - 2
                if 0 <= v < 32:
                    act.wait_ge(x2_mm, v + 1)
                    if v >= 2:
                        act.wait_ge(pv2_mm, v - 1)
                    if v % 4:
                        nc.scalar.copy(wT[:, v % 2, 0:256], banks[2 + v % 2][:, 0:256]).then_inc(e2_done, 1)
                        nc.scalar.copy(wT[:, v % 2, 256:512], banks[2 + v % 2][:, 256:512]).then_inc(e2_done, 1)
                    else:
                        w2 = wT[:, v % 2].rearrange("p (a b c) -> p a b c", a=2, b=2)
                        b2 = banks[2 + v % 2][:].rearrange("p (a b c) -> p a b c", a=2, b=2)
                        nc.scalar.copy(w2[:, :, 1], b2[:, :, 1]).then_inc(e2_done, 1)
                        nc.scalar.copy(w2[0:META, :, 0], b2[0:META, :, 0]).then_inc(e2_done, 1)
                if step < 32 and (3 * step + 3) // 8 > 3 * step // 8:
                    t = 12 + 3 * step // 8
                    if t == 12:
                        act.wait_ge(bz_done, 4)
                    fill_ev(t)
            for t in range(24, 28):
                fill_ev(t)
            act.wait_ge(pv2_mm, 32)
            for j in range(4):
                act.wait_ge(bz_done, j + 1)
                nc.scalar.copy(asb_hi[:, j], zs[:, j]).then_inc(a_hi, 1)
            act.wait_ge(eighths, 8 * N_BR)
            for j in range(8):
                act.wait_ge(o2_done, j + 1)
                nc.scalar.copy(xn_hi[:, j, META:TM], zs[:, 4 + j]).then_inc(a_hi, 1)
            act.wait_ge(a_lo, 12)
            for m in range(KD):
                act.wait_ge(mg_done, m + 1)
                nc.scalar.copy(mg_hi[:, m], gt(m)).then_inc(mghi_done, 1)
            norm(5)
            for t in range(TT):
                act.wait_ge(ft_mm, t + 1)
                nc.scalar.copy(ost[:, t, 512:1024], banks[(1, 3, 7, 1)[t]][:]).then_inc(ost_a, 1)

        @block.vector
        def _(dve):
            V = nc.vector

            def norm(q):
                for d in range(KD):
                    dve.wait_ge(sq_done, 8 * q + d + 1)
                    if d == 0:
                        V.tensor_copy(sumsq[:], sq[:, 0]).then_inc(acc_done, 1)
                    else:
                        dve.wait_ge(acc_done, 8 * q + d)
                        V.tensor_tensor(sumsq[:], sumsq[:], sq[:, d % 2], ALU.add).then_inc(acc_done, 1)

            def norm_apply(q, qs, vec):
                dve.wait_ge(rstd_done, q + 1)
                for d in range(KD + 1):
                    if d < KD:
                        if d >= 4:
                            dve.wait_ge(xlo_done, 8 * qs + d - 3)
                        V.scalar_tensor_tensor(out=xf(d), in0=xT[:, d], scalar=cols[:, vec + d:vec + d + 1], in1=rstd[:],
                                               op0=ALU.mult, op1=ALU.mult).then_inc(xf_done, 1)
                    if d:
                        e = d - 1
                        dve.wait_ge(xhi_done, 8 * qs + e + 1)
                        dve.wait_ge(xf_done, 8 * qs + e + 1)
                        V.tensor_tensor(xn_lo[:, e, META:TM], xf(e), xn_hi[:, e, META:TM].bitcast(F32), ALU.subtract).then_inc(xlo_done, 1)

            def ffn(S_, n0):
                def pair(i, guard):
                    for f in range(2):
                        dve.wait_ge(eighths, 8 * (n0 + 2 * i + 1) + 4 * f + 4)
                        dve.wait_ge(S_.silu, 2 * i + f + 1)
                        if guard:
                            dve.wait_ge(S_.h_lo, 2 * i + f - 1)
                        V.tensor_tensor(hf[:, f], banks[2 + f][:], gs[:, f], ALU.mult).then_inc(S_.hmul, 1)
                    for f in range(2):
                        dve.wait_ge(S_.hmul, 2 * i + f + 1)
                        dve.wait_ge(S_.h_hi, 2 * i + f + 1)
                        at = bass.ds(2 * i + f, 1) if guard else slice(f, f + 1)
                        V.tensor_tensor(h_lo[:, at, :].rearrange("p a t -> p (a t)"), hf[:, f],
                                        h_hi[:, at, :].bitcast(F32).rearrange("p a t -> p (a t)"), ALU.subtract).then_inc(S_.h_lo, 1)
                pair(0, False)
                with dve.Fori(1, FP) as i:
                    pair(i, True)
                for d in range(KD):
                    dve.wait_ge(eighths, 8 * (n0 + 3 * FP - 1) + d + 1)
                    V.scalar_tensor_tensor(out=xT[:, d], in0=banks[(d + 4) % 8][:], scalar=0.5, in1=xT[:, d],
                                           op0=ALU.mult, op1=ALU.add).then_inc(x_ready, 1)

            dve.wait_ge(xT_mm, 1)
            V.tensor_copy(cols[:, 0:ROWS], banks[7][:, 0:ROWS]).then_inc(cols_ready, 1)
            dve.wait_ge(meta_act, 3)
            V.tensor_scalar(meta_in[:], meta_in[:], tiny[0:META, 2:3], None, ALU.mult).then_inc(meta_dve, 1)
            for d in range(KD):
                dve.wait_ge(xT_mm, d + 2)
                V.tensor_copy(xT[:, d], banks[d][:]).then_inc(x_ready, 1)
            dve.wait_ge(meta_mm, 1)
            dve.wait_ge(cols_ready, 1)
            V.tensor_tensor(meta_f[:], banks[0][:, 0:KD * META].rearrange("p (k m) -> p k m", k=KD),
                            cols[:, V_N2:V_N2 + KD].unsqueeze(2).to_broadcast([P, KD, META]), ALU.mult).then_inc(meta_dve, 1)
            norm(0)
            dve.wait_ge(meta_act, 4)
            dve.wait_ge(meta_dve, 2)
            V.tensor_tensor(xn_lo[:, :, 0:META], meta_f[:], xn_hi[:, :, 0:META].bitcast(F32), ALU.subtract).then_inc(meta_dve, 1)
            norm_apply(0, 0, V_FFN1)
            ffn(F1, N_FFN1)

            norm(1)
            norm_apply(1, 1, V_MIX)
            dve.wait_ge(mix_in, 80)
            dve.wait_ge(ba_split, 1)
            V.tensor_tensor(wba_lo[:], wba[:], wba_hi[:].bitcast(F32), ALU.subtract).then_inc(ba_split, 1)
            V.memset(rw[:, :, 0:3], 0.0).then_inc(conv_step, 1)
            dve.wait_ge(ws_mm, 1)
            for half in range(2):
                V.tensor_copy(wsT[:, 4 * half:4 * half + 4].rearrange("p g i -> p (g i)"), banks[6 + half][:]).then_inc(ws_done, 1)
            dve.wait_ge(ws_done, 2)
            V.memset(wsT[CH:P, :, 0:CH], 0.0).then_inc(ws_done, 1)
            for j in range(12):
                dve.wait_ge(rw_done, j + 1)
                if j >= 2:
                    dve.wait_ge(qkv_done, j - 1)
                acc = hf[:, j % 2]
                tap = lambda i: cols[:, V_CONV + 12 * i + j:V_CONV + 12 * i + j + 1]
                dve.wait_ge(conv_step, 3 * j + 1)
                V.tensor_scalar(acc, rw[:, j % 2, 0:T], tap(0), None, ALU.mult).then_inc(conv_step, 1)
                for i in range(1, 4):
                    dve.wait_ge(conv_step, 3 * j + i + 1)
                    V.scalar_tensor_tensor(out=acc, in0=rw[:, j % 2, i:i + T], scalar=tap(i), in1=acc, op0=ALU.mult, op1=ALU.add)\
                        .then_inc(conv_done if i == 3 else conv_step, 1)
            hp = lambda ap: ap.rearrange("p (h t) -> p h t", h=4)
            head4 = lambda ap: ap.unsqueeze(2).to_broadcast([P, 4, 4])
            ba = banks[4][:, 0:32].rearrange("p (t c) -> p c t", c=8)
            dve.wait_ge(act_sm, 1)
            V.tensor_tensor(hp(s_a), ba[:, 4:8], head4(hvec[:, 0]), ALU.add).then_inc(dve_sm, 1)
            V.tensor_scalar(s_e, s_e, 1.0, None, ALU.add).then_inc(dve_sm, 1)
            dve.wait_ge(dve_sm, 2)
            V.reciprocal(s_beta, s_e).then_inc(dve_sm, 1)
            dve.wait_ge(act_sm, 5)
            V.scalar_tensor_tensor(out=s_t, in0=s_a, scalar=0.0, in1=s_t, op0=ALU.max, op1=ALU.add).then_inc(dve_sm, 1)
            dve.wait_ge(dve_sm, 4)
            V.scalar_tensor_tensor(out=hp(s_g), in0=hp(s_t), scalar=-1.0, in1=head4(s_ea[:, 0:4]), op0=ALU.mult, op1=ALU.mult).then_inc(dve_sm, 1)
            dve.wait_ge(cum_mm, 1)
            V.tensor_copy(s_c.rearrange("p a b -> p (a b)"), banks[5][:, 0:64]).then_inc(dve_sm, 1)
            dve.wait_ge(dve_sm, 6)
            V.tensor_scalar(s_ngc, s_c[:, 0], -1.0, None, ALU.mult).then_inc(dve_sm, 1)
            V.tensor_tensor(s_kd, s_c[:, 1], s_c[:, 0], ALU.subtract).then_inc(dve_sm, 1)
            dve.wait_ge(act_sm, 6)
            V.tensor_tensor(s_be, s_beta, s_eg, ALU.mult).then_inc(dve_sm, 1)
            for j in range(8):
                dve.wait_ge(l2rn, 2 * j + 2)
                V.scalar_tensor_tensor(out=qkv[:, j], in0=qkv[:, j], scalar=P ** -0.5 if j < 4 else 1.0, in1=gs[:, j % 2],
                                       op0=ALU.mult, op1=ALU.mult).then_inc(l2n, 1)
            dve.wait_ge(act_sm, 8)
            dve.wait_ge(dve_sm, 9)
            for h in range(H):
                at = slice(4 * h, 4 * h + 4)
                dve.wait_ge(rs_done, h + 1)
                if h:
                    dve.wait_ge(at_done, h)
                    dve.wait_ge(l_done, h)
                V.tensor_tensor(quarters(sq[:, 0]), quarters(gs[:, 0]), over4(neg_incl), ALU.add).then_inc(arg_done, 1)
                V.tensor_tensor(quarters(sq[:, 1]), over4(neg_strict), quarters(gs[:, 0]), ALU.subtract).then_inc(arg_done, 1)
                dve.wait_ge(kt_mm, h + 1)
                V.tensor_tensor(quarters(kb[:, h]), quarters(banks[5][:]), per_block(s_be[:, at]), ALU.mult).then_inc(tok_done, 1)
                V.tensor_tensor(quarters(kd[:, h]), quarters(banks[5][:]), per_block(s_kd[:, at]), ALU.mult).then_inc(tok_done, 1)
                dve.wait_ge(vt_mm, h + 1)
                V.tensor_tensor(quarters(vb[:, h]), quarters(banks[6][:]), per_block(s_beta[:, at]), ALU.mult).then_inc(vb_done, 1)
                dve.wait_ge(exp_done, 8 * h + 4)
                dve.wait_ge(kq_mm, h + 1)
                V.tensor_tensor(atT(h), banks[4][:], sq[:, 0], ALU.mult).then_inc(at_done, 1)
                dve.wait_ge(er_done, h + 1)
                V.tensor_tensor(qT(h), qT(h), gs[:, 1], ALU.mult).then_inc(qd_done, 1)
                dve.wait_ge(exp_done, 8 * h + 8)
                for p in range(4):
                    c = slice(p * P, (p + 1) * P)
                    ins = V.scalar_tensor_tensor(out=Lm(h)[:, c], in0=banks[3][:, c], scalar=s_beta[:, 4 * h + p:4 * h + p + 1], in1=sq[:, 1, c],
                                                 op0=ALU.mult, op1=ALU.mult)
                ins.then_inc(l_done, 1)
            dve.wait_ge(va_done, 4)
            for t in range(TT):
                V.bn_stats(st6[:, t], vtok[:, t]).then_inc(ln_st, 1)
            dve.wait_ge(ln_st, 4)
            for t in range(TT):
                V.bn_aggr(mv[:, t], st6[:, t]).then_inc(ln_st, 1)
            for g in range(2):
                for hh in range(2):
                    h = 2 * g + hh
                    dve.wait_ge(l_done, h + 1)
                    if g:
                        dve.wait_ge(zt_mm, 2 * (LEVELS - 1) - 1 + hh)
                    V.tensor_tensor(quarters(Mm[:, hh]), quarters(Lm(h)), over4(mixm[:, 6]), ALU.mult).then_inc(m_done, 1)
                    dve.wait_ge(m_done, (g * LEVELS) * 2 + hh + 1)
                    V.tensor_tensor(quarters(Tm[:, hh]), over4(ident), quarters(Mm[:, hh]), ALU.subtract).then_inc(t_init, 1)
                for hh in range(2):
                    h = 2 * g + hh
                    dve.wait_ge(z_mm0, h + 1)
                    V.tensor_tensor(quarters(Z[:, h]), over4(ident), quarters(banks[2 + hh][:]), ALU.subtract).then_inc(z_sub, 1)
                for level in range(1, LEVELS):
                    for hh in range(2):
                        h = 2 * g + hh
                        n = (g * (LEVELS - 1) + level - 1) * 2 + hh
                        if level == 1:
                            dve.wait_ge(z_mm0, h + 1)
                            dve.wait_ge(t_init, h + 1)
                        else:
                            dve.wait_ge(pp_mm, n - 1)
                        V.tensor_tensor(quarters(Mm[:, hh]), quarters(Lm(h)), over4(mixm[:, 6 + level]), ALU.mult).then_inc(m_done, 1)
                    for hh in range(2):
                        h = 2 * g + hh
                        n = (g * (LEVELS - 1) + level - 1) * 2 + hh
                        dve.wait_ge(zt_mm, n + 1)
                        if level == 1:
                            dve.wait_ge(z_sub, g * 2 * LEVELS + hh + 1)
                        V.tensor_tensor(Z[:, h], Z[:, h], banks[2 + hh][:], ALU.subtract).then_inc(z_sub, 1)
                        if level < LEVELS - 1:
                            V.tensor_tensor(Tm[:, hh], Tm[:, hh], banks[4 + hh][:], ALU.subtract).then_inc(t_sub, 1)
            dve.wait_ge(ln_act, 2)
            dve.wait_ge(ln_st, 8)
            dve.wait_ge(lnc_in, 32)
            for t in range(TT):
                V.tensor_scalar(vtok[:, t], vtok[:, t], mv[:, t, 0:1], rln[:, t:t + 1], ALU.subtract, ALU.mult).then_inc(ln_app, 1)
            for step, op in ((0, ALU.mult), (1, ALU.add)):
                for t in range(TT):
                    dve.wait_ge(ln_app, 4 * step + t + 1)
                    V.tensor_tensor(vtok[:, t], vtok[:, t], lnc[:, step], op).then_inc(ln_app, 1)
            for m in range(4):
                dve.wait_ge(sgu_mm, m + 1)
                V.tensor_tensor(quarters(ya[:, m]), quarters(banks[m][:]), over4(bs[:, m]), ALU.add).then_inc(ya_done, 1)
            for c in range(NC):
                r = slice(CH * (c % 2), CH * (c % 2) + CH)
                dve.wait_ge(vn_mm, c + 1)
                V.tensor_copy(vnew[r], banks[4][r]).then_inc(vn_done, 1)
                if c < NC - 1:
                    dve.wait_ge(su_mm, c + 1)
                    if c == 0:
                        V.tensor_copy(S[:, 1], banks[5][:]).then_inc(s_done, 1)
                    else:
                        dve.wait_ge(s_done, c)
                        for h in range(H):
                            hc = slice(h * P, (h + 1) * P)
                            ins = V.scalar_tensor_tensor(out=S[:, (c + 1) % 2, hc], in0=S[:, c % 2, hc],
                                                         scalar=egl[:, c % 2, 4 * h + c // 2:4 * h + c // 2 + 1], in1=banks[5][:, hc],
                                                         op0=ALU.mult, op1=ALU.add)
                        ins.then_inc(s_done, 1)
                if c < 4:
                    dve.wait_ge(f_ev, c + 1)
                    dve.wait_ge(ya_done, c + 1)
                    V.tensor_tensor(ya[:, c], ya[:, c], gs[:, c % 2], ALU.mult).then_inc(ya_mul, 1)
            dve.wait_ge(o_mm, NC)
            for h in range(H):
                V.tensor_copy(vb[:, h], banks[h][:]).then_inc(ob_done, 1)
            for m in range(4):
                dve.wait_ge(y_hi, m + 1)
                V.tensor_tensor(xn_lo[:, m, META:TM], ya[:, m], xn_hi[:, m, META:TM].bitcast(F32), ALU.subtract).then_inc(y_lo, 1)
            for h in range(H):
                dve.wait_ge(ob_rn, 2 * h + 2)
                V.scalar_tensor_tensor(out=vb[:, h], in0=vb[:, h], scalar=cols[:, V_DN:V_DN + 1], in1=gs[:, h % 2],
                                       op0=ALU.mult, op1=ALU.mult).then_inc(ob_nrm, 1)
                dve.wait_ge(ob_nrm, h + 1)
                dve.wait_ge(f_ev, 4 + h + 1)
                V.tensor_tensor(vb[:, h], vb[:, h], zT[:, h], ALU.mult).then_inc(yb_done, 1)
            for h in range(H):
                dve.wait_ge(y_hi, 4 + h + 1)
                dve.wait_ge(yb_done, h + 1)
                V.tensor_tensor(xn_lo[:, 4 + h, META:TM], vb[:, h], xn_hi[:, 4 + h, META:TM].bitcast(F32), ALU.subtract).then_inc(y_lo, 1)
            for m in range(KD):
                dve.wait_ge(eighths, 8 * N_OUT1 + 4 * m + 4)
                V.tensor_tensor(xT[:, m], xT[:, m], banks[m % 4][:], ALU.add).then_inc(x_ready, 1)

            norm(2)
            norm_apply(2, 2, V_FFN2)
            ffn(F2, N_FFN2)
            norm(3)
            dve.wait_ge(rstd_done, 4)
            for d in range(KD):
                V.scalar_tensor_tensor(out=xT[:, d], in0=xT[:, d], scalar=cols[:, V_FIN1 + d:V_FIN1 + d + 1], in1=rstd[:],
                                       op0=ALU.mult, op1=ALU.mult).then_inc(x_ready, 1)

            norm(4)
            norm_apply(4, 3, V_N2)

            def rope_k(g):
                dve.wait_ge(kr_mm, g + 1)
                if g:
                    dve.wait_ge(kr_done, 2)
                    dve.wait_ge(rope_done, 1)
                for half in range(2):
                    hc = slice(264 * half, 264 * half + 264)
                    V.tensor_tensor(hf[:, half, 0:264], banks[(5, 7)[half]][:, 0:264], sinT[:, hc], ALU.mult).then_inc(kr_st, 1)
                    V.tensor_tensor(Kw[:, g, hc], banks[2 + half][:, 0:264], cosT[:, hc], ALU.mult).then_inc(kr_st, 1)
                for half in range(2):
                    hc = slice(264 * half, 264 * half + 264)
                    dve.wait_ge(kr_st, 4 * g + 2 * half + 2)
                    V.tensor_tensor(Kw[:, g, hc], Kw[:, g, hc], hf[:, half, 0:264], ALU.add).then_inc(kr_done, 1)

            dve.wait_ge(att_in, 32)
            rope_k(0)
            for j in range(8):
                dve.wait_ge(rot_mm, j + 1)
                if j < 2:
                    dve.wait_ge(kr_done, 2 + 2 * j)
                else:
                    dve.wait_ge(rope_done, j - 1)
                V.tensor_tensor(hf[:, j % 2], banks[(6, 4)[j % 2]][:], sinT[:, META:], ALU.mult).then_inc(rp_st, 1)
                V.tensor_tensor(Qw[:, j], gs[:, j % 2], cosT[:, META:], ALU.mult).then_inc(rp_st, 1)
                dve.wait_ge(rp_st, 2 * j + 2)
                V.tensor_tensor(Qw[:, j], Qw[:, j], hf[:, j % 2], ALU.add).then_inc(rope_done, 1)
                if j == 0:
                    rope_k(1)

            dve.wait_ge(am_st, 4)
            dve.wait_ge(rope_done, 8)
            for half in range(2):
                c = slice(256 * half, 256 * half + 256)
                V.scalar_tensor_tensor(out=hf[:, 0, c], in0=banks[2 + half][:, 0:256], scalar=0.0, in1=sq[:, 0, c], op0=ALU.max, op1=ALU.add).then_inc(gm_st, 1)
            dve.wait_ge(gm_st, 2)
            V.tensor_tensor_scan(gs[:, 0, ::-1], meta_mask[:, ::-1], hf[:, 0, ::-1], 0.0, ALU.mult, ALU.add).then_inc(gm_st, 1)
            dve.wait_ge(gm_st, 3)
            for half in range(2):
                c = slice(256 * half, 256 * half + 256)
                V.tensor_tensor(argm[:, c], banks[2 + half][:, 0:256], gs[:, 0, c], ALU.subtract).then_inc(gm_st, 1)
            dve.wait_ge(gm_st, 5)
            for u in range(32 + 4):
                if u < 32:
                    n = (u % 4 + 1) * P
                    bank = banks[u % 2]
                    dve.wait_ge(a_st, 3 * u + 3)
                    if u >= 1:
                        dve.wait_ge(d_st, 4 * u)
                    V.scalar_tensor_tensor(out=hf[:, 1, 0:n], in0=bank[:, 0:n], scalar=0.0, in1=sq[:, u % 2, 0:n], op0=ALU.max, op1=ALU.add).then_inc(d_st, 1)
                    dve.wait_ge(d_st, 4 * u + 1)
                    if u >= 3:
                        dve.wait_ge(x_mm, u - 2)
                    w = w3(u)[:, 0:n]
                    V.tensor_tensor_scan(w[:, ::-1], hf[:, 1, 0:n][:, ::-1], scan_mask[:, T - n:T][:, ::-1], 0.0, ALU.add, ALU.mult).then_inc(d_st, 1)
                    dve.wait_ge(d_st, 4 * u + 2)
                    V.tensor_copy(ctok[:, u:u + 1], w[:, 0:1]).then_inc(d_st, 1)
                    dve.wait_ge(d_st, 4 * u + 3)
                    V.tensor_tensor(w, bank[:, 0:n], w, ALU.subtract).then_inc(d_st, 1)
                    dve.wait_ge(d_st, 4 * u + 4)
                    V.tensor_tensor(w[:, n - P:n], w[:, n - P:n], neg_diag, ALU.add).then_inc(g_done, 1)
                    if u % 4 == 3:
                        h = u // 4
                        if h >= 2:
                            dve.wait_ge(xm_mm, h - 1)
                        V.tensor_tensor(wm[:, h % 2].rearrange("p (a b) -> p a b", a=4), argm[:, 256 * (h % 2) + 64 * (h // 2):256 * (h % 2) + 64 * (h // 2) + 64].rearrange("p (a b) -> p a b", a=4),
                                        ctok[:, 4 * h:4 * h + 4].unsqueeze(2).to_broadcast([P, 4, META]), ALU.subtract).then_inc(tm_done, 1)
                if u >= 10 and u % 8 == 2:
                    j = (u - 10) // 8
                    dve.wait_ge(pvm_mm, 2 * j + 2)
                    V.tensor_copy(Qs[:, j], banks[4][:]).then_inc(o1_done, 1)
            V.tensor_scalar(tiny[:, 32:48], sinks[:], -1.0, None, ALU.mult).then_inc(s_st, 1)
            for j in range(4):
                dve.wait_ge(zsilu, j + 1)
                dve.wait_ge(o1_done, j + 1)
                V.tensor_tensor(zs[:, j], zs[:, j], Qs[:, j], ALU.mult).then_inc(bz_done, 1)
            for step in range(32 + 4):
                v = step
                if v < 32:
                    o = 112 if v % 4 == 0 else 0
                    j = v // 4
                    s2 = w3(v).rearrange("p (a b) -> p a b", a=2)[:, :, o:]
                    b2 = banks[v % 2][:].rearrange("p (a b) -> p a b", a=2)[:, :, o:]
                    c = 8 * (v % 2)
                    dve.wait_ge(z2_mm, 2 * v + 2)
                    if v >= 3:
                        dve.wait_ge(x2_mm, v - 2)
                    elif v == 0:
                        dve.wait_ge(x_mm, 32)
                    V.tensor_tensor(s2, b2, win_mask[:, o:].unsqueeze(1).to_broadcast([P, 2, 256 - o]), ALU.add).then_inc(s_st, 1)
                    dve.wait_ge(s_st, 1 + 3 * v + 1)
                    if v >= 2:
                        dve.wait_ge(p2_done, 3 * (v - 1))
                    V.tensor_reduce(tiny[:, c:c + 2], s2, AX_X, ALU.max).then_inc(s_st, 1)
                    dve.wait_ge(s_st, 1 + 3 * v + 2)
                    V.scalar_tensor_tensor(out=tiny[:, c + 2:c + 4], in0=tiny[:, c:c + 2], scalar=-1.0, in1=tiny[:, 32 + 2 * j:34 + 2 * j],
                                           op0=ALU.mult, op1=ALU.min).then_inc(s_st, 1)
                    dve.wait_ge(s_st, 1 + 3 * v + 3)
                    V.tensor_tensor(tiny[:, c + 4:c + 6], tiny[:, c + 2:c + 4], tiny[:, 32 + 2 * j:34 + 2 * j], ALU.subtract).then_inc(s2_done, 1)
                v = step - 1
                if 0 <= v < 32:
                    o = 112 if v % 4 == 0 else 0
                    e = 16 + 4 * (v % 2)
                    s2 = w3(v).rearrange("p (a b) -> p a b", a=2)
                    dve.wait_ge(p2_done, 3 * v + 3)
                    if v >= 1:
                        dve.wait_ge(pn_done, v)
                    V.tensor_tensor(tiny[:, 24:26], tiny[:, e:e + 2], tiny[:, e + 2:e + 4], ALU.add).then_inc(n_st, 1)
                    dve.wait_ge(n_st, 2 * v + 1)
                    V.reciprocal(tiny[:, 26:28], tiny[:, 24:26]).then_inc(n_st, 1)
                    dve.wait_ge(n_st, 2 * v + 2)
                    for i in range(2):
                        ins = V.tensor_scalar(s2[:, i, o:], s2[:, i, o:], tiny[:, 26 + i:27 + i], None, ALU.mult)
                    ins.then_inc(pn_done, 1)
                if step >= 7 and step % 4 == 3:
                    j = (step - 7) // 4
                    dve.wait_ge(pv2_mm, 4 * j + 4)
                    dve.wait_ge(zsilu, 5 + j)
                    V.tensor_tensor(zs[:, 4 + j], zs[:, 4 + j], banks[4 + j % 2][:], ALU.mult).then_inc(o2_done, 1)
            for j in range(4):
                dve.wait_ge(a_hi, j + 1)
                V.tensor_tensor(asb_lo[:, j], zs[:, j], asb_hi[:, j].bitcast(F32), ALU.subtract).then_inc(a_lo, 1)
            for j in range(8):
                dve.wait_ge(a_hi, 4 + j + 1)
                dve.wait_ge(o2_done, j + 1)
                V.tensor_tensor(xn_lo[:, j, META:TM], zs[:, 4 + j], xn_hi[:, j, META:TM].bitcast(F32), ALU.subtract).then_inc(a_lo, 1)
            dve.wait_ge(f2_ev, 28)
            for half in range(2):
                for m in range(4 * half, 4 * half + 4):
                    dve.wait_ge(eighths, 8 * (N_BR + 3 * half) + 2 * (m % 4) + 2)
                    V.scalar_tensor_tensor(out=gt(m), in0=gt(m), scalar=1.0, in1=banks[m % 2][:], op0=ALU.add, op1=ALU.mult).then_inc(sb_ev, 1)
                for m in range(4 * half, 4 * half + 4):
                    dve.wait_ge(eighths, 8 * (N_BR + 3 * half + 1) + 4 * (m % 4) + 4)
                    if m >= 2:
                        dve.wait_ge(mg_done, m - 1)
                    V.scalar_tensor_tensor(out=hf[:, m % 2], in0=gt(8 + m), scalar=1.0, in1=banks[2 + m % 2][:], op0=ALU.add, op1=ALU.mult).then_inc(sw_st, 1)
                    dve.wait_ge(sw_st, m + 1)
                    dve.wait_ge(sb_ev, m + 1)
                    V.tensor_tensor(gt(m), gt(m), hf[:, m % 2], ALU.add).then_inc(mg_done, 1)
                    dve.wait_ge(mghi_done, m + 1)
                    dve.wait_ge(mg_done, m + 1)
                    V.tensor_tensor(mg_lo[:, m], gt(m), mg_hi[:, m].bitcast(F32), ALU.subtract).then_inc(mglo_done, 1)
            for m in range(KD):
                dve.wait_ge(eighths, 8 * N_OUT2 + 4 * m + 4)
                V.scalar_tensor_tensor(out=xT[:, m], in0=banks[4 + m % 4][:], scalar=0.5, in1=xT[:, m], op0=ALU.mult, op1=ALU.add).then_inc(x_ready, 1)
            norm(5)
            dve.wait_ge(rstd_done, 6)
            for d in range(KD):
                V.scalar_tensor_tensor(out=xT[:, d], in0=xT[:, d], scalar=cols[:, V_FIN2 + d:V_FIN2 + d + 1], in1=rstd[:],
                                       op0=ALU.mult, op1=ALU.mult).then_inc(fin_done, 1)
            for t in range(TT):
                dve.wait_ge(ft_mm, t + 1)
                V.tensor_copy(ost[:, t, 0:512], banks[(0, 2, 6, 0)[t]][:]).then_inc(ost_v, 1)

        @block.tensor
        def _(pe):
            mm1 = nc.tensor.matmul

            def three(bank, hi, lo, rhi, rlo, start, stop):
                mm1(bank, hi, rhi, start=start, stop=False)
                mm1(bank, hi, rlo, start=False, stop=False)
                return mm1(bank, lo, rhi, start=False, stop=stop)

            def feature_steps(n, f, k0, k1, bank):
                slot = n % 2
                if k0 == 0 and f == 0:
                    pe.wait_ge(split_done, n + 1)
                for k in range(k0, k1):
                    c = k * SC + f * P
                    ins = three(bank[:], w_hi[:, slot, c:c + P], w_lo[:, slot, c:c + P], xn_hi[:, k, META:TM], xn_lo[:, k, META:TM], k == 0, k == KD - 1)
                    if k % 2:
                        ins.then_inc(eighths, 1)

            def stat(q):
                pe.wait_ge(acc_done, 8 * q + 8)
                mm1(banks[4][:], ones, sumsq[:], start=True, stop=True).then_inc(stat_mm, 1)

            def ffn(S_, n0, q):
                def pair(i, first):
                    for part, freed in ((0, S_.silu), (1, S_.hmul)):
                        slot = (n0 + part) % 2
                        pe.wait_ge(split_done, n0 + 2 * i + part + 1)
                        for f in range(2):
                            if not first:
                                pe.wait_ge(freed, 2 * i + f - 1)
                            for k in range(KD):
                                if first and part == 0 and f == 0:
                                    pe.wait_ge(xlo_done, 8 * q + k + 1)
                                c = k * SC + f * P
                                ins = three(banks[2 * part + f][:], w_hi[:, slot, c:c + P], w_lo[:, slot, c:c + P],
                                            xn_hi[:, k, META:TM], xn_lo[:, k, META:TM], k == 0, k == KD - 1)
                                if k % 2:
                                    ins.then_inc(eighths, 1)
                pair(0, True)
                with pe.Fori(1, FP) as i:
                    pair(i, False)
                n1 = n0 + 2 * FP

                def down(m, slot, first, last):
                    pe.wait_ge(split_done, n1 + m + 1)
                    pe.wait_ge(S_.h_lo, 2 * m + 2)
                    for d in range(KD):
                        if first and d == 4:
                            pe.wait_ge(S_.silu, 2 * FP)
                            pe.wait_ge(S_.hmul, 2 * FP)
                        for kk in range(2):
                            c = kk * D + d * P
                            at = slice(2 * m + kk, 2 * m + kk + 1) if isinstance(m, int) else bass.ds(2 * m + kk, 1)
                            ins = three(banks[(d + 4) % 8][:], w_hi[:, slot, c:c + P], w_lo[:, slot, c:c + P],
                                        h_hi[:, at, :].rearrange("p a t -> p (a t)"), h_lo[:, at, :].rearrange("p a t -> p (a t)"),
                                        first and kk == 0, last and kk == 1)
                        ins.then_inc(eighths, 1)
                down(0, n1 % 2, True, False)
                with pe.Fori(0, (FP - 3) // 2) as j:
                    down(2 * j + 1, (n1 + 1) % 2, False, False)
                    down(2 * j + 2, n1 % 2, False, False)
                down(FP - 2, (n1 + 1) % 2, False, False)
                down(FP - 1, n1 % 2, False, True)

            pe.wait_ge(consts, 64)
            pe.wait_ge(rows_in, 128)
            nc.tensor.transpose(banks[7][:, 0:ROWS], rows[0:ROWS, :], ident[0:ROWS, 0:ROWS]).then_inc(xT_mm, 1)
            pe.wait_ge(x_loaded, 64)
            for d in range(KD):
                if d == 7:
                    pe.wait_ge(cols_ready, 1)
                for t in range(TT):
                    ins = nc.tensor.transpose(banks[d][:, t * P:(t + 1) * P], xload[:, t, d * P:(d + 1) * P], ident)
                ins.then_inc(xT_mm, 1)
            pe.wait_ge(meta_dve, 1)
            pe.wait_ge(x_ready, 1)
            for d in range(KD):
                ins = nc.tensor.transpose(banks[0][:, d * META:(d + 1) * META], meta_in[:, d * P:(d + 1) * P], ident[0:META, 0:META])
            ins.then_inc(meta_mm, 1)
            stat(0)
            pe.wait_ge(meta_dve, 2)
            ffn(F1, N_FFN1, 0)

            pe.wait_ge(mix_in, 80)
            pe.wait_ge(x_ready, 16)
            for g in range(GG):
                ins = nc.tensor.transpose(banks[6 + g // 4][:, (g % 4) * P:(g % 4 + 1) * P], wsraw[:, g], ident)
            ins.then_inc(ws_mm, 1)
            stat(1)
            for j in range(12):
                n, f = N_MIX + j // 2, j % 2
                if j >= 4:
                    pe.wait_ge(rw_done, j - 3)
                if j == 0:
                    pe.wait_ge(split_done, n + 1)
                    for k in range(KD):
                        pe.wait_ge(xlo_done, 8 + k + 1)
                        feature_steps(n, 0, k, k + 1, banks[0])
                else:
                    feature_steps(n, f, 0, KD, banks[j % 4])
                if j == 1:
                    pe.wait_ge(ba_split, 2)
                    pe.wait_ge(rstd_done, 2)
                    for t in range(TT):
                        c = slice(META + t * P, META + (t + 1) * P)
                        for k in range(KD):
                            o = banks[4][:, 8 * t:8 * t + 8]
                            mm1(o, xn_hi[:, k, c], wba_hi[:, k], start=k == 0, stop=False)
                            mm1(o, xn_hi[:, k, c], wba_lo[:, k], start=False, stop=False)
                            ins = mm1(o, xn_lo[:, k, c], wba_hi[:, k], start=False, stop=k == KD - 1)
                    ins.then_inc(ba_mm, 1)
            pe.wait_ge(dve_sm, 5)
            for n, w in enumerate((cumT, same, half0, half1)):
                ins = mm1(banks[5][:, 16 * n:16 * n + 16], w, s_g, start=True, stop=True)
            ins.then_inc(cum_mm, 1)

            def token_tile(n, t, bank, c0):
                c = slice(META + t * P, META + (t + 1) * P)
                for k in range(KD):
                    w = slice(k * SC, (k + 1) * SC)
                    o = bank[:, c0:c0 + SC]
                    mm1(o, xn_hi[:, k, c], w_hi[:, n % 2, w], start=k == 0, stop=False)
                    mm1(o, xn_hi[:, k, c], w_lo[:, n % 2, w], start=False, stop=False)
                    ins = mm1(o, xn_lo[:, k, c], w_hi[:, n % 2, w], start=False, stop=k == KD - 1)
                    if k % 4 == 3:
                        ins.then_inc(eighths, 1)
            for j in range(8):
                pe.wait_ge(l2sq, j + 1)
                if j < 2:
                    pe.wait_ge(dve_sm, 6)
                else:
                    pe.wait_ge(l2rn, 2 * j - 3)
                mm1(banks[4 + j % 2][:], ones, sq[:, j % 2], start=True, stop=True).then_inc(l2mm, 1)
                n, t = N_MIX + 6 + j // 4, j % 4
                if t == 0:
                    pe.wait_ge(split_done, n + 1)
                    pe.wait_ge(ws_done, 2) if j == 0 else pe.wait_ge(rw_done, 12)
                token_tile(n, t, banks[(6, 7, 0, 1)[j // 2]], SC * (j % 2))
            pe.wait_ge(l2n, 8)
            pe.wait_ge(va_done, 2)
            for h in range(H):
                if h:
                    pe.wait_ge(rs_done, h)
                for p in range(4):
                    ins = mm1(banks[2][:, p * P:(p + 1) * P], s_g[:, 4 * h + p:4 * h + p + 1].to_broadcast([P, P]), cumT, start=True, stop=True)
                ins.then_inc(r_mm, 1)
                pair = [slice(p * P, (p + 1) * P) for p in range(4)]
                if h:
                    pe.wait_ge(tok_done, 2 * h)
                for c in pair:
                    ins = nc.tensor.transpose(banks[5][:, c], kT(h)[:, c], ident)
                ins.then_inc(kt_mm, 1)
                if h:
                    pe.wait_ge(vb_done, h)
                for c in pair:
                    ins = nc.tensor.transpose(banks[6][:, c], vT(h)[:, c], ident)
                ins.then_inc(vt_mm, 1)
                if h:
                    pe.wait_ge(l_done, h)
                for c in pair:
                    ins = mm1(banks[3][:, c], kT(h)[:, c], kT(h)[:, c], start=True, stop=True)
                ins.then_inc(kk_mm, 1)
                for c in pair:
                    ins = mm1(banks[4][:, c], kT(h)[:, c], qT(h)[:, c], start=True, stop=True)
                ins.then_inc(kq_mm, 1)
            for g in range(2):
                for hh in range(2):
                    h = 2 * g + hh
                    pe.wait_ge(m_done, g * LEVELS * 2 + hh + 1)
                    if g:
                        pe.wait_ge(z_sub, 2 * LEVELS - 1 + hh)
                    for c in pair:
                        ins = nc.tensor.transpose(banks[2 + hh][:, c], Mm[:, hh, c], ident)
                    ins.then_inc(z_mm0, 1)
                for level in range(1, LEVELS):
                    last = level == LEVELS - 1
                    for hh in range(2):
                        h = 2 * g + hh
                        n = (g * (LEVELS - 1) + level - 1) * 2 + hh
                        pe.wait_ge(m_done, (g * LEVELS + level) * 2 + hh + 1)
                        pe.wait_ge(z_sub, (g * LEVELS + level - 1) * 2 + hh + 1)
                        if n >= 2:
                            pe.wait_ge(pp_copy, n - 1)
                        for c in pair:
                            ins = mm1(banks[hh][:, c], Mm[:, hh, c], Z[:, h, c], start=True, stop=True)
                        ins.then_inc(pp_mm, 1)
                    for hh in range(2):
                        h = 2 * g + hh
                        n = (g * (LEVELS - 1) + level - 1) * 2 + hh
                        pe.wait_ge(pp_copy, n + 1)
                        if level > 1:
                            pe.wait_ge(t_sub, (g * (LEVELS - 2) + level - 2) * 2 + hh + 1)
                        elif g:
                            pe.wait_ge(t_sub, 2 * (LEVELS - 2))
                            pe.wait_ge(t_init, 2 * g + hh + 1)
                        else:
                            pe.wait_ge(t_init, hh + 1)
                        for c in pair:
                            ins = mm1(banks[2 + hh][:, c], Tm[:, hh, c], Pp[:, hh, c], start=True, stop=True)
                        if not last:
                            for c in pair:
                                ins = mm1(banks[4 + hh][:, c], Pp[:, hh, c], Tm[:, hh, c], start=True, stop=True)
                        ins.then_inc(zt_mm, 1)
            for h in range(H):
                pe.wait_ge(z_sub, 2 * LEVELS * (h // 2 + 1) - 1 + h % 2)
                if h >= 2:
                    pe.wait_ge(nw_done, h - 1)
                for c in pair:
                    ins = mm1(banks[6 + h % 2][:, c], kb[:, h, c], Z[:, h, c], start=True, stop=True)
                ins.then_inc(nw_mm, 1)
            pe.wait_ge(ln_app, 12)
            pe.wait_ge(ws_done, 3)
            pe.wait_ge(z_sub, 4 * LEVELS)
            for m in range(4):
                for t in range(TT):
                    for half in range(2):
                        r = slice(CH * half, CH * half + CH)
                        ins = mm1(banks[m][r, t * P:(t + 1) * P], vtok[:, t, m * P + CH * half:m * P + CH * half + CH], wsT[:, 2 * m + half], start=True, stop=True)
                ins.then_inc(sgu_mm, 1)
            pe.wait_ge(nw_done, 4)
            for c in range(NC):
                p, r = c // 2, slice(CH * (c % 2), CH * (c % 2) + CH)
                cc = slice(c * CH, (c + 1) * CH)
                if c:
                    pe.wait_ge(s_done, c)
                    pe.wait_ge(vn_done, c)
                else:
                    pe.wait_ge(t_sub, 4 * (LEVELS - 2))
                for h in range(H):
                    hc = slice(h * P, (h + 1) * P)
                    ins = mm1(banks[4][:, hc], Z[:, h, p * P:(p + 1) * P], vb[:, h, p * P:(p + 1) * P], start=True, stop=c == 0)
                    if c:
                        ins = mm1(banks[4][:, hc], kb[:, h, p * P:(p + 1) * P], S[:, c % 2, hc], start=False, stop=True)
                ins.then_inc(vn_mm, 1)
                if c:
                    for h in range(H):
                        mm1(banks[h][:, cc], S[:, c % 2, h * P:(h + 1) * P], qT(h)[:, cc], start=True, stop=False)
                else:
                    pe.wait_ge(ya_done, 4)
                n, f = N_MIX + 8 + c // 2, c % 2
                if c >= 2:
                    pe.wait_ge(f_ev, c - 1)
                feature_steps(n, f, 0, 4, banks[6 + c % 2])
                pe.wait_ge(vn_done, c + 1)
                if c < NC - 1:
                    for h in range(H):
                        ins = mm1(banks[5][:, h * P:(h + 1) * P], kd[r, h, p * P:(p + 1) * P], vnew[r, h * P:(h + 1) * P], start=True, stop=True)
                    ins.then_inc(su_mm, 1)
                for h in range(H):
                    ins = mm1(banks[h][:, cc], vnew[r, h * P:(h + 1) * P], atT(h)[r, cc], start=c == 0, stop=True)
                ins.then_inc(o_mm, 1)
                feature_steps(n, f, 4, KD, banks[6 + c % 2])
            for h in range(H):
                pe.wait_ge(ob_sq, h + 1)
                if h >= 2:
                    pe.wait_ge(ob_rn, 2 * h - 3)
                mm1(banks[4 + h % 2][:], ones, sq[:, h % 2], start=True, stop=True).then_inc(ob_mm, 1)
            for m in range(KD):
                n, f = N_OUT1 + m // 2, m % 2
                if m >= 4:
                    pe.wait_ge(x_ready, 16 + m - 3)
                if m == 0:
                    for k in range(KD):
                        pe.wait_ge(y_lo, k + 1)
                        feature_steps(n, 0, k, k + 1, banks[0])
                else:
                    feature_steps(n, f, 0, KD, banks[m % 4])

            stat(2)
            ffn(F2, N_FFN2, 2)
            stat(3)

            stat(4)
            for j in range(4):
                n, f = N_P2 + j // 2, j % 2
                if j >= 2:
                    pe.wait_ge(p_ev, j - 1)
                if j == 0:
                    for k in range(KD):
                        pe.wait_ge(xlo_done, 24 + k + 1)
                        feature_steps(n, 0, k, k + 1, banks[0])
                else:
                    feature_steps(n, f, 0, KD, banks[j % 2])

            def key_tile(n, f, b):
                for half in range(2):
                    hc = slice(264 * half, 264 * half + 264)
                    for k in range(KD):
                        c = k * SC + f * P
                        ins = three(banks[b + half][:, 0:264], w_hi[:, n % 2, c:c + P], w_lo[:, n % 2, c:c + P], xn_hi[:, k, hc], xn_lo[:, k, hc], k == 0, k == KD - 1)
                        if half and k % 2:
                            ins.then_inc(eighths, 1)

            def value_tile(n, t, o, f0, width, incs):
                c = slice(0, P) if t is None else slice(META + t * P, META + (t + 1) * P)
                for k in range(KD):
                    w = slice(k * SC + f0, k * SC + f0 + width)
                    mm1(o, xn_hi[:, k, c], w_hi[:, n % 2, w], start=k == 0, stop=False)
                    mm1(o, xn_hi[:, k, c], w_lo[:, n % 2, w], start=False, stop=False)
                    ins = mm1(o, xn_lo[:, k, c], w_hi[:, n % 2, w], start=False, stop=k == KD - 1)
                    if incs and (k + 1) % (KD // incs) == 0:
                        ins.then_inc(eighths, 1)

            for j in range(4):
                n = N_P2 + 2 + j // 2
                if j % 2 == 0:
                    pe.wait_ge(split_done, n + 1)
                if j != 1:
                    pe.wait_ge(p_ev, (4, 0, 6, 8)[j])
                key_tile(n, j % 2, 2 * (j % 2))
            for s in range(2):
                n = N_P2 + 4 + s
                pe.wait_ge(split_done, n + 1)
                if s:
                    pe.wait_ge(p_ev, EV_V + 3)
                value_tile(n, None, banks[6][:, 0:SC], 0, SC, 0)
                for t in range(TT):
                    value_tile(n, t, banks[4 + t // 2][:, SC * (t % 2):SC * (t % 2) + SC], 0, SC, 2)
            n = N_P2 + 6
            pe.wait_ge(split_done, n + 1)
            pe.wait_ge(p_ev, EV_K + 6)
            key_tile(n, 0, 0)
            pe.wait_ge(p_ev, EV_V + 6)
            value_tile(n, None, banks[6][:, 0:P], P, P, 0)
            for t in range(TT):
                value_tile(n, t, banks[4][:, t * P:(t + 1) * P], P, P, 1)

            def rotate_k(g):
                for w, bb in ((dup_k[g], (2, 3)), (rot_k[g], (5, 7))):
                    for half in range(2):
                        ins = mm1(banks[bb[half]][:, 0:264], w, kraw[:, 264 * half:264 * half + 264], start=True, stop=True)
                ins.then_inc(kr_mm, 1)

            def rotate_q(j):
                pe.wait_ge(p_ev, EV_QW + j + 1)
                if j >= 2:
                    pe.wait_ge(rope_done, j - 1)
                mm1(banks[(6, 4)[j % 2]][:], rot_q, gs[:, j % 2], start=True, stop=True).then_inc(rot_mm, 1)
            pe.wait_ge(p_ev, EV_KW + 2)
            pe.wait_ge(att_in, 32)
            rotate_k(0)
            for j in range(8):
                if j >= 2:
                    pe.wait_ge(p_ev, EV_QW + j - 1)
                feature_steps(N_P2 + 7 + j // 2, j % 2, 0, KD, banks[j % 2])
                if j:
                    rotate_q(j - 1)
                if j == 1:
                    pe.wait_ge(kr_done, 2)
                    rotate_k(1)
            rotate_q(7)

            gate_at = [0]

            def gate_steps(count):
                for i in range(gate_at[0], gate_at[0] + count):
                    t, k = i // KD, i % KD
                    if k == 0:
                        if t >= 2:
                            pe.wait_ge(f2_ev, t - 1)
                        else:
                            pe.wait_ge(rope_done, 8)
                    feature_steps(N_P2 + 11 + t // 2, t % 2, k, k + 1, banks[6 + t % 2])
                gate_at[0] += count

            pe.wait_ge(kr_done, 4)
            for half in range(2):
                r = slice(HD * half, HD * half + HD)
                for j in range(4):
                    for t in range(TT):
                        c = (4 * j + t) * META
                        ins = mm1(banks[2 + half][:, c:c + META], Qs[r, j, t * P:(t + 1) * P], Ks[r, j, 0:META], start=True, stop=True)
                ins.then_inc(zm_mm, 1)
            for step in range(32 + 3):
                u = step
                if u < 32:
                    h, t = u // 4, u % 4
                    r, j, n = slice(HD * (h % 2), HD * (h % 2) + HD), h // 2, (t + 1) * P
                    if u >= 2:
                        pe.wait_ge(g_done, u - 1)
                    else:
                        pe.wait_ge(p_ev, EV_QW + 8)
                    mm1(banks[u % 2][:, 0:n], Qs[r, j, t * P:(t + 1) * P], Ks[r, j, META:META + n], start=True, stop=True).then_inc(z_mm, 1)
                    gate_steps(1)
                u = step - 2
                if 0 <= u < 32:
                    h, t = u // 4, u % 4
                    pe.wait_ge(w_done, u + 1)
                    if u >= 2:
                        pe.wait_ge(e_done, u - 1)
                    for b in range(t + 1):
                        ins = nc.tensor.transpose(banks[2 + u % 2][:, b * P:(b + 1) * P], w3(u)[:, b * P:(b + 1) * P], ident)
                    ins.then_inc(x_mm, 1)
                    if t == 3:
                        pe.wait_ge(wm_done, h + 1)
                        if h:
                            pe.wait_ge(em_done, h)
                        for b in range(TT):
                            ins = nc.tensor.transpose(banks[5][0:META, b * P:(b + 1) * P], wm[:, h % 2, b * META:(b + 1) * META], ident)
                        ins.then_inc(xm_mm, 1)
                if step < 32:
                    gate_steps(1)
                u = step - 3
                if 0 <= u < 32:
                    h, t = u // 4, u % 4
                    r, hc = slice(HD * (h % 2), HD * (h % 2) + HD), slice(HD * h, HD * h + HD)
                    pe.wait_ge(e_done, u + 1)
                    if u % 8 == 0:
                        if u:
                            pe.wait_ge(o1_done, u // 8)
                        else:
                            pe.wait_ge(rope_done, 8)
                    for b in range(t + 1):
                        ins = mm1(banks[4][r, t * P:(t + 1) * P], Vs[:, b, hc], wT[:, u % 2, b * P:(b + 1) * P],
                                  start=t == 0 and b == 0, stop=False, skip_group_check=True)
                    ins.then_inc(pv_mm, 1)
                    if t == 3:
                        pe.wait_ge(em_done, h + 1)
                        mm1(banks[4][r, :], Vm[:, hc], wTm[:], start=False, stop=True, skip_group_check=True).then_inc(pvm_mm, 1)
                if step < 32:
                    gate_steps(1)
            for step in range(32 + 3):
                v = step
                if v < 32:
                    j, t = v // 4, v % 4
                    if v >= 2:
                        pe.wait_ge(s2_done, v - 1)
                    else:
                        pe.wait_ge(g_done, 32)
                    for i in range(2):
                        r = slice(HD * i, HD * i + HD)
                        keys = slice(0, META + P) if t == 0 else slice(META + (t - 1) * P, META + (t + 1) * P)
                        n = keys.stop - keys.start
                        if i:
                            gate_steps(1)
                            pe.wait_ge(z2_mm, 2 * v + 1)
                        mm1(banks[v % 2][:, 256 * (i + 1) - n:256 * (i + 1)], Qw[r, j, t * P:(t + 1) * P], Kw[r, j // 4, keys], start=True, stop=True).then_inc(z2_mm, 1)
                v = step - 2
                if 0 <= v < 32:
                    t = v % 4
                    pe.wait_ge(pn_done, v + 1)
                    if v >= 2:
                        pe.wait_ge(e2_done, 2 * (v - 1))
                    else:
                        pe.wait_ge(e_done, 31 + v)
                    for i in range(2):
                        o = 256 * i
                        bank = banks[2 + v % 2]
                        if t:
                            nc.tensor.transpose(bank[:, o:o + P], w3(v)[:, o:o + P], ident)
                        else:
                            nc.tensor.transpose(bank[0:META, o:o + P], w3(v)[:, o + 112:o + P], ident)
                        ins = nc.tensor.transpose(bank[:, o + P:o + 2 * P], w3(v)[:, o + P:o + 2 * P], ident)
                    ins.then_inc(x2_mm, 1)
                if step < 32:
                    gate_steps(1)
                v = step - 3
                if 0 <= v < 32:
                    j, t = v // 4, v % 4
                    pe.wait_ge(e2_done, 2 * v + 2)
                    if t == 0:
                        if j >= 2:
                            pe.wait_ge(o2_done, j - 1)
                        else:
                            pe.wait_ge(o1_done, 4)
                    vc = slice(HD * (j // 4), HD * (j // 4) + HD)
                    for i in range(2):
                        o = banks[4 + j % 2][HD * i:HD * i + HD, t * P:(t + 1) * P]
                        w = wT[:, v % 2, 256 * i:256 * i + 256]
                        if t:
                            mm1(o, Vw[:, t - 1, vc], w[:, 0:P], start=True, stop=False)
                        else:
                            mm1(o, Vwm[:, vc], w[0:META, 0:P], start=True, stop=False)
                        ins = mm1(o, Vw[:, t, vc], w[:, P:2 * P], start=False, stop=True)
                    ins.then_inc(pv2_mm, 1)
                if step < 32:
                    gate_steps(1)
            gate_steps(32)

            for half in range(2):
                n = N_BR + 3 * half
                pe.wait_ge(split_done, n + 1)
                for m in range(4 * half, 4 * half + 4):
                    if m >= 2:
                        pe.wait_ge(sb_ev, m - 1)
                    for k in range(4):
                        if m == 0:
                            pe.wait_ge(a_lo, k + 1)
                        c = k * 512 + (m % 4) * P
                        ins = three(banks[m % 2][:], w_hi[:, n % 2, c:c + P], w_lo[:, n % 2, c:c + P], asb_hi[:, k], asb_lo[:, k], k == 0, k == 3)
                        if k % 2:
                            ins.then_inc(eighths, 1)
                for m in range(4 * half, 4 * half + 4):
                    if m >= 2:
                        pe.wait_ge(sw_st, m - 1)
                    for k in range(KD):
                        if m == 0:
                            pe.wait_ge(a_lo, 4 + k + 1)
                        feature_steps(n + 1 + m % 4 // 2, m % 2, k, k + 1, banks[2 + m % 2])
            pe.wait_ge(f2_ev, 28)
            pe.wait_ge(o2_done, 8)
            for m in range(KD):
                n, f = N_OUT2 + m // 2, m % 2
                if f == 0:
                    pe.wait_ge(split_done, n + 1)
                if m >= 4:
                    pe.wait_ge(x_ready, 40 + m - 3)
                for k in range(KD):
                    if m == 0:
                        pe.wait_ge(mglo_done, k + 1)
                    c = k * SC + f * P
                    ins = three(banks[4 + m % 4][:], w_hi[:, n % 2, c:c + P], w_lo[:, n % 2, c:c + P], mg_hi[:, k], mg_lo[:, k], k == 0, k == KD - 1)
                    if k % 2:
                        ins.then_inc(eighths, 1)
            stat(5)
            for t in range(TT):
                if t == 3:
                    pe.wait_ge(ost_a, 1)
                    pe.wait_ge(ost_v, 1)
                for d in range(KD):
                    if t == 0:
                        pe.wait_ge(fin_done, d + 1)
                    ins = nc.tensor.transpose(banks[(0, 2, 6, 0)[t] + d // 4][:, (d % 4) * P:(d % 4 + 1) * P], xT[:, d, t * P:(t + 1) * P], ident)
                ins.then_inc(ft_mm, 1)


INPUTS = ("x", "ffn1_norm", "ffn1_w_gate", "ffn1_w_up", "ffn1_w_down", "mix_norm", "w_in", "gm_ln_g", "gm_ln_b", "gm_w_s",
          "gm_b_s", "dn_conv_w", "dn_a_log", "dn_dt_bias", "dn_norm", "w_out", "ffn2_norm", "ffn2_w_gate", "ffn2_w_up",
          "ffn2_w_down", "final_norm", "meta_tokens_2", "norm_gain_2", "w_in_2", "w_branch_sb_2", "w_branch_swa_2",
          "w_out_2", "attn_sinks_2", "final_norm_gain_2")


def kernel(**inputs):
    import concourse.bacc as bacc
    from concourse.bass_utils import run_bass_kernel_spmd

    nc = bacc.Bacc("TRN2", target_bir_lowering=False, num_devices=1)
    arrays, aps = {}, {}
    given = {name: inputs[name] for name in INPUTS}
    given.update(constants())
    for name, value in given.items():
        value = np.ascontiguousarray(value)
        arrays[f"in_{name}_dram"] = value
        aps[name] = nc.dram_tensor(f"in_{name}_dram", value.shape, mybir.dt.from_np(value.dtype), kind="ExternalInput").ap()
    out = nc.dram_tensor("out_0_dram", (1, T, D), F32, kind="ExternalOutput").ap()
    program(nc, aps, out)
    result = run_bass_kernel_spmd(nc, [arrays], core_ids=[0])
    return result.results[0]["out_0_dram"]
```

```python
from contextlib import ExitStack

import numpy as np

import concourse.bass as bass
from concourse import mybir

P = 128
F32 = mybir.dt.float32
F32R = mybir.dt.float32r
ALU = mybir.AluOpType
ACT = mybir.ActivationFunctionType
AX_X = mybir.AxisListType.X

T = 512
D = 1024
KD = D // P
TT = T // P
FF = 2816
FP = FF // (2 * P)
SLAB = 2048
SC = SLAB // KD
META = 16
TM = META + T
CH = 64
NC = T // CH
H = 4
LEVELS = 6
GG = 8
HD = 64
NEG = -1e30

V_FFN1, V_MIX, V_FFN2, V_FIN1, V_N2, V_DN, V_CONV = 0, 8, 16, 24, 32, 40, 41
ROWS = V_CONV + 48
V_FG2 = ROWS

N_FFN1 = 0
N_MIX = N_FFN1 + 3 * FP
MIX_SLABS = (4, 5, 6, 7, 8, 9, 2, 3, 0, 1, 10, 11)
N_OUT1 = N_MIX + len(MIX_SLABS)
N_FFN2 = N_OUT1 + 4
N_P2 = N_FFN2 + 3 * FP
P2_SLABS = (0, 1, 2, 3, 4, 5, 10, 6, 7, 8, 9) + tuple(range(11, 25))
N_BR = N_P2 + len(P2_SLABS)
N_OUT2 = N_BR + 6
N_SLABS = N_OUT2 + 4


def constants():
    i, j = np.arange(P)[:, None], np.arange(P)[None, :]
    same = i // CH == j // CH
    f = lambda m: np.asarray(m, np.float32)
    ones = np.ones((P, P))
    base = [np.eye(P), ones, np.full((P, 8), 1e-6)]
    neg = lambda keep: np.where(keep, 0.0, NEG)
    mix = [same & (i <= j), same, (i // CH == 0) * ones, (i // CH == 1) * ones, neg(same & (i <= j)), neg(same & (j < i))]
    mix += [(i // (2 << s) == j // (2 << s)) & ((i >> s) % 2 == 1) & ((j >> s) % 2 == 0) for s in range(LEVELS)]
    prev = neg(j > i)
    own = neg(j <= i)
    att = [np.ones((P, 384)), j < i, neg(j < i), prev, own, (np.arange(T)[None, :] % META != META - 1) * np.ones((P, T))]
    half = HD // 2
    rot = np.zeros((P, P))
    for m in range(P):
        if m % HD < half:
            rot[m + half, m] = -1.0
        else:
            rot[m - half, m] = 1.0
    rope = [rot]
    for g in range(2):
        dup = np.zeros((P, P))
        for m in range(P):
            dup[g * HD + m % HD, m] = 1.0
        rope += [dup, dup @ rot]
    inv = np.float32(10000.0) ** (-np.arange(half, dtype=np.float32) / np.float32(half))
    ang = np.tile(inv, 4)[:, None] * np.arange(TM, dtype=np.float32)[None, :]
    rope += [np.cos(ang), np.sin(ang)]
    cat = lambda parts: np.ascontiguousarray(np.concatenate([f(m) for m in parts], axis=1))
    return {"c_base": cat(base), "c_mix": cat(mix), "c_att": cat(att), "c_rope": cat(rope)}


def program(nc, a, out):
    with ExitStack() as ctx:
        sem = lambda name: ctx.enter_context(nc.semaphore(name))
        cursor = [(nc.sbuf_base + 31) // 32 * 32]

        def sb(name, shape, dt=F32):
            t = nc.alloc_sbuf_tensor_at(name, shape, dt, offset=cursor[0])
            cursor[0] += (4 * int(np.prod(shape[1:])) + 31) // 32 * 32
            return t

        raw = sb("raw", [P, 2, SLAB])
        w_hi = sb("w_hi", [P, 2, SLAB], F32R)
        w_lo = sb("w_lo", [P, 2, SLAB], F32R)
        xT = sb("xT", [P, KD, T])
        xn_hi = sb("xn_hi", [P, KD, TM], F32R)
        xn_lo = sb("xn_lo", [P, KD, TM], F32R)
        base_c = sb("base_c", [P, 2 * P + 8])
        ident, ones, epsc = base_c[:, 0:P], base_c[:, P:2 * P], base_c[:, 2 * P:2 * P + 1]
        rows_at = cursor[0]
        rows = sb("rows", [P, P])
        cols = sb("cols", [P, P])
        rstd = sb("rstd", [P, T])
        hvec = sb("hvec", [P, 2, 4])
        sinks = sb("sinks", [P, 16])
        tiny = sb("tiny", [P, 48])
        rtok = sb("rtok", [P, TT])
        sq = sb("sq", [P, 2, T])
        smalls_at = cursor[0]
        sumsq = sb("sumsq", [P, TM])
        gs = sb("gs", [P, 2, T])
        hf = sb("hf", [P, 2, T])
        region = cursor[0]

        sums = sumsq[:, 0:T]
        sums2 = gs[:, 0]
        factor, factor_t = sumsq, sumsq[:, META:TM]

        h_hi = sb("h_hi", [P, 2 * FP, T], F32R)
        h_lo = sb("h_lo", [P, 2 * FP, T], F32R)
        assert cursor[0] <= nc.sbuf_usable_end
        cursor[0] = region
        xload = sb("xload", [P, TT, D])
        meta_in = sb("meta_in", [META, D])
        meta_sq = sb("meta_sq", [META, D])
        meta_f = sb("meta_f", [P, KD, META])

        cursor[0] = region
        mixm = sb("mixm", [P, 12, P])
        cumT, same, half0, half1 = (mixm[:, n] for n in range(4))
        neg_incl, neg_strict = mixm[:, 4], mixm[:, 5]
        here, cursor[0] = cursor[0], rows_at
        wba = sb("wba", [P, KD, 8])
        cursor[0] = here
        qkv = sb("qkv", [P, 12, T])
        cursor[0] -= 4 * T * 4
        ya = sb("ya", [P, 4, T])
        rw_at = cursor[0]
        rw = sb("rw", [P, 2, T + 8])
        cursor[0] = rw_at
        lnc = sb("lnc", [P, 2, T])
        cursor[0] = rw_at
        vnew = sb("vnew", [P, T])
        cursor[0] = rw_at + 2 * 4 * (T + 8)
        vb = sb("vb", [P, H, T])
        kb_at = cursor[0]
        kb = sb("kb", [P, H, T])
        kd = sb("kd", [P, H, T])
        Z = sb("Z", [P, H, T])
        tmp_at = cursor[0]
        Tm = sb("Tm", [P, 2, T])
        Mm = sb("Mm", [P, 2, T])
        Pp = sb("Pp", [P, 2, T])
        cursor[0] = tmp_at
        wsraw = sb("wsraw", [P, GG, P])
        cursor[0] = tmp_at
        zT = sb("zT", [P, 4, T])
        S = sb("S", [P, 2, T])
        vtok_at = cursor[0]
        vtok = sb("vtok", [P, TT, T])
        wsT_at = cursor[0]
        wsT = sb("wsT", [P, GG, P])
        bs = sb("bs", [P, 4, P])
        wba_w = KD * 8 + P - 8
        cursor[0] = vtok_at
        wba_hi = sb("wba_hi", [P, wba_w], F32R)
        wba_lo = sb("wba_lo", [P, wba_w], F32R)
        baf = sb("baf", [8, T])
        cursor[0] = wsT_at + 4 * (GG * P + 4 * P)
        assert cursor[0] <= nc.sbuf_usable_end
        cursor[0] = vtok_at
        ya_hi = sb("ya_hi", [P, 4, T], F32R)
        cursor[0] = rw_at + 4 * T
        ya_lo0 = sb("ya_lo0", [P, T], F32R)
        cursor[0] = wsT_at
        ya_lo1 = sb("ya_lo1", [P, 3, T], F32R)
        cursor[0] = kb_at
        yb_hi = sb("yb_hi", [P, 4, T], F32R)
        yb_lo = sb("yb_lo", [P, 4, T], F32R)
        yh = lambda k: ya_hi[:, k] if k < 4 else yb_hi[:, k - 4]
        yl = lambda k: ya_lo0[:] if k < 1 else ya_lo1[:, k - 1] if k < 4 else yb_lo[:, k - 4]
        cursor[0] = smalls_at
        sm = sb("sm", [P, 14, 16])
        s_e, s_beta, s_a, s_t, s_g, s_ea = (sm[:, n] for n in range(6))
        s_c = sm[:, 6:10]
        s_ngc, s_kd, s_eg, s_be = (sm[:, n] for n in range(10, 14))
        egl = sb("egl", [P, 2, 16])
        st6 = sb("st6", [P, 4, 6])
        mv = sb("mv", [P, 4, 2])
        rln = sb("rln", [P, 4])

        cursor[0] = region
        Qs = sb("Qs", [P, 4, T])
        Ks = sb("Ks", [P, 4, TM])
        Vs = sb("Vs", [P, TT, T])
        Vm = sb("Vm", [META, T])
        zs = sb("zs", [P, 12, T])
        qw_at = cursor[0]
        Qw = sb("Qw", [P, 8, T])
        Kw = sb("Kw", [P, 2, TM])
        Vw = sb("Vw", [P, TT, P])
        Vwm = sb("Vwm", [META, P])
        attm = sb("attm", [P, 1408])
        scan_mask, neg_diag, win_mask, meta_mask = attm[:, 0:512], attm[:, 512:640], attm[:, 640:896], attm[:, 896:1408]
        kblk = sb("kblk", [P, 4, 2 * META])
        work_at = cursor[0]
        ropec = sb("ropec", [P, 5 * P + 2 * TM])
        rot_q = ropec[:, 0:P]
        dup_k = [ropec[:, (1 + 2 * g) * P:(2 + 2 * g) * P] for g in range(2)]
        rot_k = [ropec[:, (2 + 2 * g) * P:(3 + 2 * g) * P] for g in range(2)]
        cosT, sinT = ropec[:, 5 * P:5 * P + TM], ropec[:, 5 * P + TM:]
        kraw = sb("kraw", [P, TM])
        cursor[0] = work_at
        wT = sb("wT", [P, 2, T])
        argm = sb("argm", [P, T])
        ctok = sb("ctok", [P, 32])
        wm = sb("wm", [P, 2, HD])
        wTm = sb("wTm", [META, T])
        assert cursor[0] <= nc.sbuf_usable_end
        cursor[0] = region
        g_lowt = sb("g_lowt", [P, 12, T])
        ost_at = region
        cursor[0] = qw_at
        g_hight = sb("g_hight", [P, 4, T])
        asb_hi = sb("asb_hi", [P, 4, T], F32R)
        asb_lo = sb("asb_lo", [P, 4, T], F32R)
        mg_lo = sb("mg_lo", [P, KD, T], F32R)
        assert cursor[0] <= nc.sbuf_usable_end
        cursor[0] = qw_at - 8 * T * 4
        mg_hi = sb("mg_hi", [P, KD, T], F32R)
        cursor[0] = ost_at
        ost = sb("ost", [P, TT, D])
        gain_row = sb("gain_row", [P, D])
        gt = lambda t: g_lowt[:, t] if t < 12 else g_hight[:, t - 12]

        banks = [ctx.enter_context(nc.psum_tensor(f"bank{i}", [P, 512], F32)) for i in range(8)]

        def quarters(ap):
            return ap.rearrange("p (a b) -> p a b", a=4)

        def over4(ap):
            return ap.unsqueeze(1).to_broadcast([P, 4, P])

        def per_block(ap):
            return ap.unsqueeze(2).to_broadcast([P, 4, P])

        x_loaded = [sem(f"x_loaded{t}") for t in range(TT)]
        consts, hvec_in, rows_in, row0_in = sem("consts"), sem("hvec_in"), sem("rows_in"), sem("row0_in")
        slab_loaded = [sem("slab_loaded0"), sem("slab_loaded1")]
        hi_done, split_done = sem("hi_done"), sem("split_done")
        eighths = sem("eighths")
        xT_mm, x_ready, cols_ready = sem("xT_mm"), sem("x_ready"), sem("cols_ready")
        sq_done, acc_done, stat_mm, ln_done, rstd_done = (
            sem(s) for s in ("sq_done", "acc_done", "stat_mm", "ln_done", "rstd_done"))
        xhi_done, xlo_done, gain_done = sem("xhi_done"), sem("xlo_done"), sem("gain_done")
        rt_mm, rt_done, r4_st, r4_ln, f_done = sem("rt_mm"), sem("rt_done"), sem("r4_st"), sem("r4_ln"), sem("f_done")
        meta_act, meta_dve, meta_mm, meta_loaded = sem("meta_act"), sem("meta_dve"), sem("meta_mm"), sem("meta_loaded")
        out_done = sem("out_done")

        f_gate, f_up, f_silu, f_mul, f_hi, f_lo = (sem(s) for s in ("f_gate", "f_up", "f_silu", "f_mul", "f_hi", "f_lo"))

        mix_in, lnc_in = sem("mix_in"), sem("lnc_in")
        rw_done, conv_step, conv_done, qkv_done = sem("rw_done"), sem("conv_step"), sem("conv_done"), sem("qkv_done")
        ba_split, ba_mm, act_sm, dve_sm, cum_mm = sem("ba_split"), sem("ba_mm"), sem("act_sm"), sem("dve_sm"), sem("cum_mm")
        ws_mm, ws_done = sem("ws_mm"), sem("ws_done")
        l2sq, l2mm, l2rn, l2n, va_done = sem("l2sq"), sem("l2mm"), sem("l2rn"), sem("l2n"), sem("va_done")
        r_mm, kq_mm, kt_mm, vt_mm = sem("r_mm"), sem("kq_mm"), sem("kt_mm"), sem("vt_mm")
        rs_done, er_done, exp_done = sem("rs_done"), sem("er_done"), sem("exp_done")
        arg_done, at_done, qd_done, l_done, tok_done, vb_done = (
            sem(s) for s in ("arg_done", "at_done", "qd_done", "l_done", "tok_done", "vb_done"))
        ln_st, ln_act, ln_app = sem("ln_st"), sem("ln_act"), sem("ln_app")
        m_done, t_init, z_mm0, pp_mm, pp_copy, zt_mm, z_sub, t_sub = (
            sem(s) for s in ("m_done", "t_init", "z_mm0", "pp_mm", "pp_copy", "zt_mm", "z_sub", "t_sub"))
        nw_mm, nw_done, sgu_mm, ya_done = sem("nw_mm"), sem("nw_done"), sem("sgu_mm"), sem("ya_done")
        fz_ev = sem("fz_ev")
        vn_mm, vn_done, su_mm, s_done, o_mm, f_ev, ya_mul = (
            sem(s) for s in ("vn_mm", "vn_done", "su_mm", "s_done", "o_mm", "f_ev", "ya_mul"))
        ob_done, ob_sq, ob_mm, ob_rn, ob_nrm, yb_done, y_hi, y_lo = (
            sem(s) for s in ("ob_done", "ob_sq", "ob_mm", "ob_rn", "ob_nrm", "yb_done", "y_hi", "y_lo"))
        att_in, kr_mm, kr_st, kr_done, rot_mm, rp_st, rope_done = (
            sem(s) for s in ("att_in", "kr_mm", "kr_st", "kr_done", "rot_mm", "rp_st", "rope_done"))
        zm_mm, am_st, gm_st, z_mm, a_st, d_st, g_done, w_done, x_mm, e_done, pv_mm = (
            sem(s) for s in ("zm_mm", "am_st", "gm_st", "z_mm", "a_st", "d_st", "g_done", "w_done", "x_mm", "e_done", "pv_mm"))
        tm_done, wm_done, xm_mm, em_done, pvm_mm, o1_done, f2_ev = (
            sem(s) for s in ("tm_done", "wm_done", "xm_mm", "em_done", "pvm_mm", "o1_done", "f2_ev"))
        zsilu, bz_done = sem("zsilu"), sem("bz_done")
        z2_mm, s_st, s2_done, p2_done, n_st, pn_done, x2_mm, e2_done, pv2_mm, o2_done = (
            sem(s) for s in ("z2_mm", "s_st", "s2_done", "p2_done", "n_st", "pn_done", "x2_mm", "e2_done", "pv2_mm", "o2_done"))
        a_hi, a_lo, sb_ev, sw_st, mg_done, mghi_done, mglo_done = (
            sem(s) for s in ("a_hi", "a_lo", "sb_ev", "sw_st", "mg_done", "mghi_done", "mglo_done"))
        vw_mm, vg_done, kb_done = sem("vw_mm"), sem("vg_done"), sem("kb_done")
        pq_ev, pt_ev, th_done = sem("pq_ev"), sem("pt_ev"), sem("th_done")
        fsq_done, fsum_done, fln_done, ost_v = sem("fsq_done"), sem("fsum_done"), sem("fln_done"), sem("ost_v")

        def out_bank(s, t):
            return banks[(4 if s < 2 else 0) + t][:, SC * (s % 2):SC * (s % 2) + SC]

        def gain(q, d):
            at = (V_FFN1, V_MIX, V_FFN2, V_FG2)[q] + d
            return cols[:, at:at + 1]
        qT = lambda h: qkv[:, h]
        kT = lambda h: qkv[:, 4 + h]
        vT = lambda h: qkv[:, 8 + h]
        atT, Lm = kT, vT
        vwf = gs[:].rearrange("p a b -> p (a b)")[:, 0:TM]
        w3 = lambda u: (gs[:, 0], gs[:, 1], hf[:, 0])[u % 3]

        block = ctx.enter_context(nc.Block())

        @block.sync
        def _(sp):
            def load(n, src, slot=None):
                slot = n % 2 if slot is None else slot
                if not isinstance(n, int) or n >= 2:
                    sp.wait_ge(split_done, n - 1)
                sp.dma_start(raw[:, slot, :].rearrange("p (k c) -> p k c", k=src.shape[1]), src).then_inc(slab_loaded[slot], 16)

            def ffn(n0, wg, wu, wd):
                g = wg.rearrange("(k p) f -> p k f", p=P)
                u = wu.rearrange("(k p) f -> p k f", p=P)
                d = wd.rearrange("(k p) c -> p k c", p=P)
                if n0:
                    load(n0, g[:, :, 0:SC])
                load(n0 + 1, u[:, :, 0:SC])
                with sp.Fori(1, FP) as i:
                    load(n0 + 2 * i, g[:, :, bass.ds(i * SC, SC)], n0 % 2)
                    load(n0 + 2 * i + 1, u[:, :, bass.ds(i * SC, SC)], (n0 + 1) % 2)
                n1 = n0 + 2 * FP
                with sp.Fori(0, FP // 2) as j:
                    load(n1 + 2 * j, d[:, bass.ds(j * 4, 2), :], n1 % 2)
                    load(n1 + 2 * j + 1, d[:, bass.ds(j * 4 + 2, 2), :], (n1 + 1) % 2)
                load(n1 + FP - 1, d[:, 2 * FP - 2:2 * FP, :])

            def columns(n0, w, slabs):
                v = w.rearrange("(k p) c -> p k c", p=P)
                for i, s in enumerate(slabs):
                    load(n0 + i, v[:, :, s * SC:(s + 1) * SC])

            xv = a["x"].rearrange("b (t p) d -> (b p) t d", p=P)
            wg1 = a["ffn1_w_gate"][0].rearrange("(k p) f -> p k f", p=P)
            load(0, wg1[:, :, 0:SC])
            sp.dma_start(rows[V_FFN1:V_FFN1 + 8, :], a["ffn1_norm"].rearrange("b (k p) -> (b k) p", p=P)).then_inc(row0_in, 16)
            sp.dma_start(base_c[:], a["c_base"]).then_inc(consts, 16)
            for t in range(TT):
                sp.dma_start(xload[:, t, :], xv[:, t, :]).then_inc(x_loaded[t], 16)
            ffn(N_FFN1, a["ffn1_w_gate"][0], a["ffn1_w_up"][0], a["ffn1_w_down"][0])
            columns(N_MIX, a["w_in"][0], MIX_SLABS[0:2])
            sp.wait_ge(eighths, 8 * N_MIX)
            sp.dma_start(mixm[:].rearrange("p a b -> p (a b)"), a["c_mix"]).then_inc(mix_in, 16)
            with nc.allow_non_contiguous_dma(reason="eight columns of a row"):
                sp.dma_start(wba[:], a["w_in"][0].rearrange("(k p) c -> p k c", p=P)[:, :, 3072:3080]).then_inc(mix_in, 16)
            sp.dma_start(wsraw[:], a["gm_w_s"][0].rearrange("g i j -> i g j")).then_inc(mix_in, 16)
            bsv = a["gm_b_s"][0].rearrange("(m two) i -> two m i", two=2)
            for half in range(2):
                sp.dma_start(bs[64 * half:64 * half + 64], bsv[half].partition_broadcast(64)).then_inc(mix_in, 16)
            columns(N_MIX + 2, a["w_in"][0], MIX_SLABS[2:10])
            sp.wait_ge(conv_done, 12)
            sp.dma_start(lnc[:, 0, :], a["gm_ln_g"][0].partition_broadcast(P)).then_inc(lnc_in, 16)
            sp.dma_start(lnc[:, 1, :], a["gm_ln_b"][0].partition_broadcast(P)).then_inc(lnc_in, 16)
            columns(N_MIX + 10, a["w_in"][0], MIX_SLABS[10:])
            columns(N_OUT1, a["w_out"][0], range(4))
            ffn(N_FFN2, a["ffn2_w_gate"][0], a["ffn2_w_up"][0], a["ffn2_w_down"][0])
            columns(N_P2, a["w_in_2"][0], P2_SLABS[0:2])
            sp.wait_ge(eighths, 8 * N_P2)
            sp.dma_start(attm[:], a["c_att"]).then_inc(att_in, 16)
            sp.dma_start(ropec[:], a["c_rope"]).then_inc(att_in, 16)
            columns(N_P2 + 2, a["w_in_2"][0], P2_SLABS[2:])
            wsb = a["w_branch_sb_2"][0].rearrange("(k p) c -> p k c", p=P)
            for i in range(2):
                load(N_BR + 3 * i, wsb[:, :, i * 512:(i + 1) * 512])
                columns(N_BR + 3 * i + 1, a["w_branch_swa_2"][0], (2 * i, 2 * i + 1))
            columns(N_OUT2, a["w_out_2"][0], range(4))
            ov = out[0].rearrange("(t p) d -> t p d", p=P)
            sp.wait_ge(mglo_done, 8)
            sp.dma_start(gain_row[:], a["final_norm_gain_2"].partition_broadcast(P)).then_inc(gain_done, 16)
            for t in range(TT):
                sp.wait_ge(ost_v, 2 * t + 2)
                sp.dma_start(ov[t], ost[:, t]).then_inc(out_done, 16)
            sp.wait_ge(out_done, 16 * TT)

        @block.gpsimd
        def _(pool):
            parts = pool.alloc_register("high_parts")

            def split(n, slot, loads):
                pool.wait_ge(slab_loaded[slot], 16 * loads)
                if not isinstance(n, int) or n >= 2:
                    pool.wait_ge(eighths, 8 * (n - 1))
                done = n + 1
                if not isinstance(n, int):
                    pool.reg_add(parts, parts, 1)
                    done = parts
                nc.gpsimd.tensor_scalar(w_hi[:, slot], raw[:, slot], 1.0, 0.0, ALU.mult, ALU.add).then_inc(hi_done, 1)
                pool.wait_ge(hi_done, done)
                nc.gpsimd.tensor_tensor(w_lo[:, slot], raw[:, slot], w_hi[:, slot].bitcast(F32), ALU.subtract).then_inc(split_done, 1)
            pool.wait_ge(split_done, 1)
            split(1, 1, 1)
            def slabs(n0, n1):
                pool.reg_mov(parts, n0)
                with pool.Fori(n0 // 2, n1 // 2) as i:
                    split(2 * i, 0, i + 1)
                    split(2 * i + 1, 1, i + 1)
            n = N_MIX + 7
            assert N_SLABS % 2 and n % 2 == 0
            slabs(2, n)
            split(n, 0, n // 2 + 1)
            for h in range(H):
                e = (sq, hf)[h % 2]
                pool.wait_ge(rs_done, h + 1)
                if h >= 2:
                    pool.wait_ge(at_done, h - 1)
                    pool.wait_ge(l_done, h - 1)
                nc.gpsimd.tensor_tensor(quarters(e[:, 0]), quarters(gs[:, 0]), over4(neg_incl), ALU.add).then_inc(arg_done, 1)
                nc.gpsimd.tensor_tensor(quarters(e[:, 1]), over4(neg_strict), quarters(gs[:, 0]), ALU.subtract).then_inc(arg_done, 1)
                if h == 1:
                    split(n + 1, 1, n // 2 + 1)
            split(n + 2, 0, n // 2 + 2)
            pool.wait_ge(ln_act, 2)
            pool.wait_ge(ln_st, 8)
            pool.wait_ge(lnc_in, 32)
            for t in range(TT):
                nc.gpsimd.tensor_scalar(vtok[:, t], vtok[:, t], mv[:, t, 0:1], rln[:, t:t + 1], ALU.subtract, ALU.mult).then_inc(ln_app, 1)
            for step, op in ((0, ALU.mult), (1, ALU.add)):
                for t in range(TT):
                    pool.wait_ge(ln_app, 4 * step + t + 1)
                    nc.gpsimd.tensor_tensor(vtok[:, t], vtok[:, t], lnc[:, step], op).then_inc(ln_app, 1)
            split(n + 3, 1, n // 2 + 2)
            slabs(n + 4, N_SLABS - 1)
            split(N_SLABS - 1, 0, N_SLABS // 2 + 1)

        @block.scalar
        def _(act):
            A = nc.scalar.activation

            def high(q, d):
                act.wait_ge(x_ready, 8 * q + d + 1)
                nc.scalar.mul(xn_hi[:, d, META:TM], xT[:, d], gain(q, d)).then_inc(xhi_done, 1)

            def square(q, d):
                if 8 * q + d >= 2:
                    act.wait_ge(acc_done, 8 * q + d - 1)
                A(sq[:, d % 2], xT[:, d], ACT.Square).then_inc(sq_done, 1)

            def root(q):
                act.preload_act_table_set("natural_log_exp_and_others")
                act.wait_ge(stat_mm, q + 1)
                A(rstd[:], banks[4][:], ACT.Ln, bias=epsc, scale=1.0 / D).then_inc(ln_done, 1)
                act.wait_ge(ln_done, q + 1)
                A(rstd[:], rstd[:], ACT.Exp, scale=-0.5).then_inc(rstd_done, 1)

            def norm(q):
                for d in range(KD):
                    high(q, d)
                    square(q, d)
                root(q)

            def ffn(base):
                def pair(i, guard):
                    for f in range(2):
                        act.wait_ge(f_gate, base + 2 * i + f + 1)
                        A(gs[:, f], gs[:, f], ACT.Silu).then_inc(f_silu, 1)
                    for f in range(2):
                        act.wait_ge(f_mul, base + 2 * i + f + 1)
                        dst = h_hi[:, bass.ds(2 * i + f, 1), :] if guard else h_hi[:, f:f + 1, :]
                        nc.scalar.copy(dst.rearrange("p a t -> p (a t)"), hf[:, f]).then_inc(f_hi, 1)
                pair(0, False)
                if base == 0:
                    act.wait_ge(meta_dve, 2)
                    nc.scalar.copy(xn_hi[:, :, 0:META], meta_f[:]).then_inc(meta_act, 1)
                with act.Fori(1, FP) as i:
                    pair(i, True)

            act.preload_act_table_set("natural_log_exp_and_others")
            act.wait_ge(slab_loaded[0], 16)
            nc.scalar.copy(w_hi[:, 0], raw[:, 0]).then_inc(hi_done, 1)
            for name, r, n in (("mix_norm", V_MIX, 8), ("ffn2_norm", V_FFN2, 8), ("norm_gain_2", V_N2, 8), ("dn_norm", V_DN, 1)):
                act.dma_start(rows[r:r + n, :], a[name].rearrange("b (k p) -> (b k) p", p=P)).then_inc(rows_in, 16)
            act.dma_start(rows[V_FIN1:V_FIN1 + 8, :], a["final_norm"].rearrange("(k p) -> k p", p=P)).then_inc(rows_in, 16)
            act.dma_start(rows[V_CONV:V_CONV + 48, :], a["dn_conv_w"][0].rearrange("j (c p) -> (j c) p", p=P)).then_inc(rows_in, 16)
            act.dma_start(meta_in[:], a["meta_tokens_2"]).then_inc(meta_loaded, 16)
            act.dma_start(hvec[:, 0, :], a["dn_dt_bias"][0].partition_broadcast(P)).then_inc(hvec_in, 16)
            act.dma_start(hvec[:, 1, :], a["dn_a_log"][0].partition_broadcast(P)).then_inc(hvec_in, 16)
            act.dma_start(sinks[:], a["attn_sinks_2"][0].partition_broadcast(P)).then_inc(hvec_in, 16)
            act.wait_ge(cols_ready, 1)
            for d in range(KD):
                high(0, d)
            for d in range(KD):
                square(0, d)
            root(0)
            act.wait_ge(meta_loaded, 16)
            A(meta_sq[:], meta_in[:], ACT.Square, accum_out=tiny[0:META, 0:1]).then_inc(meta_act, 1)
            act.wait_ge(meta_act, 1)
            A(tiny[0:META, 1:2], tiny[0:META, 0:1], ACT.Ln, bias=epsc[0:META], scale=1.0 / D).then_inc(meta_act, 1)
            act.wait_ge(meta_act, 2)
            A(tiny[0:META, 2:3], tiny[0:META, 1:2], ACT.Exp, scale=-0.5).then_inc(meta_act, 1)
            act.wait_ge(hvec_in, 48)
            ffn(0)

            norm(1)
            act.wait_ge(mix_in, 80)
            nc.scalar.copy(wba_hi[:, 0:KD * 8], wba[:].rearrange("p k c -> p (k c)")).then_inc(ba_split, 1)
            act.preload_act_table(ACT.Silu)
            for j in range(12):
                if j == 8:
                    act.preload_act_table_set("natural_log_exp_and_others")
                    hp = lambda ap: ap.rearrange("p (h t) -> p h t", h=4)
                    ba = banks[5][:, 0:32].rearrange("p (t c) -> p c t", c=8)
                    act.wait_ge(ba_mm, 2)
                    A(hp(s_e), ba[:, 0:4], ACT.Exp, scale=-1.0).then_inc(act_sm, 1)
                    act.wait_ge(dve_sm, 2)
                    A(s_t, s_a, ACT.Abs).then_inc(act_sm, 1)
                    act.wait_ge(act_sm, 2)
                    A(s_t, s_t, ACT.Exp, scale=-1.0).then_inc(act_sm, 1)
                    act.wait_ge(act_sm, 3)
                    A(s_t, s_t, ACT.Ln, bias=1.0).then_inc(act_sm, 1)
                    A(s_ea[:, 0:4], hvec[:, 1], ACT.Exp).then_inc(act_sm, 1)
                    act.wait_ge(dve_sm, 7)
                    A(s_eg, s_c[:, 0], ACT.Exp).then_inc(act_sm, 1)
                    act.wait_ge(dve_sm, 9)
                    A(s_kd, s_kd, ACT.Exp).then_inc(act_sm, 1)
                    A(egl[:], s_c[:, 2:4], ACT.Exp).then_inc(act_sm, 1)
                    def l2_root(i):
                        act.wait_ge(l2mm, i + 1)
                        if i >= 2:
                            act.wait_ge(l2n, i - 1)
                        A(gs[:, i % 2], banks[4 + i % 2][:], ACT.Ln, bias=epsc).then_inc(l2rn, 1)
                        act.wait_ge(l2rn, 2 * i + 1)
                        A(gs[:, i % 2], gs[:, i % 2], ACT.Exp, scale=-0.5).then_inc(l2rn, 1)
                    for i in range(9):
                        if i < 8:
                            act.wait_ge(qkv_done, i + 1)
                            if i >= 2:
                                act.wait_ge(l2mm, i - 1)
                            A(sq[:, i % 2], qkv[:, i], ACT.Square).then_inc(l2sq, 1)
                        if i:
                            l2_root(i - 1)
                    act.preload_act_table(ACT.Silu)
                act.wait_ge(conv_done, j + 1)
                A(qkv[:, j], hf[:, j % 2], ACT.Silu).then_inc(qkv_done, 1)
            act.preload_act_table_set("natural_log_exp_and_others")

            def gate_ev(j):
                t = j % 4
                act.wait_ge(eighths, 8 * (N_MIX + 6) + 4 * (j // 2) + 4)
                nc.scalar.mul(vtok[:, t, (j // 4) * SC:(j // 4 + 1) * SC], banks[(7, 0, 1, 7)[j // 2]][:, (j % 2) * SC:(j % 2 + 1) * SC],
                              rtok[:, t:t + 1]).then_inc(va_done, 1)
            for h in range(H):
                act.wait_ge(r_mm, h + 1)
                if h:
                    act.wait_ge(arg_done, 2 * h)
                    act.wait_ge(er_done, h)
                else:
                    act.wait_ge(l2n, 8)
                nc.scalar.copy(gs[:, 0], banks[2][:]).then_inc(rs_done, 1)
                act.wait_ge(rs_done, h + 1)
                if h:
                    act.wait_ge(qd_done, h)
                A(gs[:, 1], gs[:, 0], ACT.Exp).then_inc(er_done, 1)
                for part, bias in ((0, s_ngc), (1, s_c[:, 0])):
                    act.wait_ge(arg_done, 2 * h + part + 1)
                    for p in range(4):
                        e = (sq, hf)[h % 2][:, part, p * P:(p + 1) * P]
                        A(e, e, ACT.Exp,
                          bias=bias[:, 4 * h + p:4 * h + p + 1]).then_inc(exp_done, 1)
                for j in ((0, 1), (2, 3), (), (4, 5, 6, 7))[h]:
                    gate_ev(j)
            act.wait_ge(va_done, 8)
            for t in range(TT):
                A(vtok[:, t], vtok[:, t], ACT.Gelu_apprx_tanh).then_inc(vg_done, 1)
            for g in range(2):
                if g:
                    act.wait_ge(ln_st, 8)
                    A(rln[:], mv[:, :, 1], ACT.Ln, bias=epsc).then_inc(ln_act, 1)
                    act.wait_ge(ln_act, 1)
                    A(rln[:], rln[:], ACT.Exp, scale=-0.5).then_inc(ln_act, 1)
                for level in range(1, LEVELS):
                    for hh in range(2):
                        n = (g * (LEVELS - 1) + level - 1) * 2 + hh
                        act.wait_ge(pp_mm, n + 1)
                        if n >= 2:
                            act.wait_ge(zt_mm, n - 1)
                        nc.scalar.copy(Pp[:, hh], banks[hh][:]).then_inc(pp_copy, 1)
            for h in range(H):
                act.wait_ge(nw_mm, h + 1)
                nc.scalar.mul(kb[:, h], banks[6 + h % 2][:], -1.0).then_inc(nw_done, 1)
            for c in range(NC):
                if c >= 4:
                    act.wait_ge(ya_mul, 4)
                    nc.scalar.copy(yh(c - 4), ya[:, c - 4]).then_inc(y_hi, 1)
                act.wait_ge(fz_ev, c + 1)
                if c < 4:
                    A(gs[:, c % 2], gs[:, c % 2], ACT.Gelu_apprx_tanh).then_inc(f_ev, 1)
                else:
                    A(zT[:, c - 4], zT[:, c - 4], ACT.Silu).then_inc(f_ev, 1)
            act.preload_act_table_set("natural_log_exp_and_others")
            for h in range(H + 2):
                if h < H:
                    act.wait_ge(ob_done, h + 1)
                    if h >= 2:
                        act.wait_ge(ob_mm, h - 1)
                    A(sq[:, h % 2], vb[:, h], ACT.Square).then_inc(ob_sq, 1)
                e = h - 1
                if 0 <= e < H:
                    act.wait_ge(ob_mm, e + 1)
                    if e >= 2:
                        act.wait_ge(ob_nrm, e - 1)
                    A(gs[:, e % 2], banks[4 + e % 2][:], ACT.Ln, bias=epsc, scale=1.0 / P).then_inc(ob_rn, 1)
                    act.wait_ge(ob_rn, 2 * e + 1)
                    A(gs[:, e % 2], gs[:, e % 2], ACT.Exp, scale=-0.5).then_inc(ob_rn, 1)
                e = h - 2
                if e >= 0:
                    act.wait_ge(yb_done, e + 1)
                    nc.scalar.copy(yh(4 + e), vb[:, e]).then_inc(y_hi, 1)

            norm(2)
            ffn(2 * FP)

            for d in range(KD):
                high(3, d)
            for d in range(KD):
                act.wait_ge(acc_done, 24 + 2 * d)
                A(sq[:, 0], xT[:, d], ACT.Square).then_inc(sq_done, 1)
                A(sq[:, 1], xT[:, d], ACT.Square, scale=cols[:, V_FIN1 + d:V_FIN1 + d + 1]).then_inc(sq_done, 1)
            root(3)
            act.wait_ge(r4_st, 2)
            A(gs[:, 1], gs[:, 1], ACT.Ln, bias=epsc, scale=1.0 / D).then_inc(r4_ln, 1)
            act.wait_ge(r4_ln, 1)
            A(gs[:, 1], gs[:, 1], ACT.Exp, scale=-0.5).then_inc(r4_ln, 1)
            act.wait_ge(rt_done, 2)
            for s in range(2):
                for t in range(TT):
                    if t % 2 == 0:
                        act.wait_ge(eighths, 8 * (N_P2 + 4 + s) + 2 * t + 4)
                    nc.scalar.mul(Vs[:, t, s * SC:(s + 1) * SC], banks[4 + t // 2][:, SC * (t % 2):SC * (t % 2) + SC], rtok[:, t:t + 1]).then_inc(pt_ev, 1)
                nc.scalar.copy(Vm[:, s * SC:(s + 1) * SC], banks[6][0:META, 0:SC]).then_inc(pt_ev, 1)
            act.wait_ge(vw_mm, 2)
            nc.scalar.copy(Vw[:].rearrange("p a b -> p (a b)"), banks[4][:]).then_inc(pt_ev, 1)
            nc.scalar.copy(Vwm[:], banks[6][0:META, 0:P]).then_inc(pt_ev, 1)

            act.preload_act_table_set("natural_log_exp_and_others")
            act.wait_ge(zm_mm, 1)
            A(sq[:, 0], banks[2][:], ACT.Abs).then_inc(am_st, 1)
            act.wait_ge(am_st, 1)
            A(sq[:, 0], sq[:, 0], ACT.Exp, scale=-1.0).then_inc(am_st, 1)
            act.wait_ge(am_st, 2)
            A(sq[:, 0], sq[:, 0], ACT.Ln, bias=1.0).then_inc(am_st, 1)
            act.wait_ge(gm_st, 1)
            for step in range(32 + 3):
                u = step
                if u < 32:
                    n = (u % 4 + 1) * P
                    act.wait_ge(z_mm, u + 1)
                    if u >= 2:
                        act.wait_ge(g_done, u - 1)
                    A(sq[:, u % 2, 0:n], banks[u % 2][:, 0:n], ACT.Abs).then_inc(a_st, 1)
                    act.wait_ge(a_st, 3 * u + 1)
                    A(sq[:, u % 2, 0:n], sq[:, u % 2, 0:n], ACT.Exp, scale=-1.0).then_inc(a_st, 1)
                    act.wait_ge(a_st, 3 * u + 2)
                    A(sq[:, u % 2, 0:n], sq[:, u % 2, 0:n], ACT.Ln, bias=1.0).then_inc(a_st, 1)
                u = step - 1
                if 0 <= u < 32:
                    n = (u % 4 + 1) * P
                    act.wait_ge(g_done, u + 1)
                    A(w3(u)[:, 0:n], w3(u)[:, 0:n], ACT.Exp).then_inc(w_done, 1)
                    if u % 4 == 3:
                        h = u // 4
                        act.wait_ge(tm_done, h + 1)
                        A(wm[:, h % 2], wm[:, h % 2], ACT.Exp).then_inc(wm_done, 1)
                u = step - 2
                if 0 <= u < 32:
                    n = (u % 4 + 1) * P
                    act.wait_ge(x_mm, u + 1)
                    if u >= 2:
                        act.wait_ge(pv_mm, u - 1)
                    nc.scalar.copy(wT[:, u % 2, 0:n], banks[2 + u % 2][:, 0:n]).then_inc(e_done, 1)
                    if u % 4 == 3:
                        h = u // 4
                        act.wait_ge(xm_mm, h + 1)
                        if h:
                            act.wait_ge(pvm_mm, h)
                        nc.scalar.copy(wTm[:], banks[5][0:META, :]).then_inc(em_done, 1)
            act.preload_act_table(ACT.Silu)
            for t in range(12):
                act.wait_ge(f2_ev, t + 1)
                A(zs[:, t], zs[:, t], ACT.Silu).then_inc(zsilu, 1)
            act.preload_act_table_set("exp_and_others")

            def tanh(m):
                act.wait_ge(f2_ev, 12 + m + 1)
                A(gt(m), gt(m), ACT.Tanh, scale=0.5).then_inc(th_done, 1)
            for step in range(32 + 3):
                v = step
                if v < 32:
                    o = 112 if v % 4 == 0 else 0
                    s2 = w3(v).rearrange("p (a b) -> p a b", a=2)
                    act.wait_ge(s2_done, v + 1)
                    if v >= 2:
                        act.wait_ge(pn_done, v - 1)
                    for i in range(2):
                        A(s2[:, i, o:], s2[:, i, o:], ACT.Exp, bias=tiny[:, 8 * (v % 2) + 2 + i:8 * (v % 2) + 3 + i],
                          accum_out=tiny[:, 16 + 4 * (v % 2) + i:17 + 4 * (v % 2) + i]).then_inc(p2_done, 1)
                    A(tiny[:, 18 + 4 * (v % 2):20 + 4 * (v % 2)], tiny[:, 8 * (v % 2) + 4:8 * (v % 2) + 6], ACT.Exp).then_inc(p2_done, 1)
                v = step - 2
                if 0 <= v < 32:
                    act.wait_ge(x2_mm, v + 1)
                    if v >= 2:
                        act.wait_ge(pv2_mm, v - 1)
                    if v % 4:
                        nc.scalar.copy(wT[:, v % 2, 0:256], banks[2 + v % 2][:, 0:256]).then_inc(e2_done, 1)
                        nc.scalar.copy(wT[:, v % 2, 256:512], banks[2 + v % 2][:, 256:512]).then_inc(e2_done, 1)
                    else:
                        w2 = wT[:, v % 2].rearrange("p (a b c) -> p a b c", a=2, b=2)
                        b2 = banks[2 + v % 2][:].rearrange("p (a b c) -> p a b c", a=2, b=2)
                        nc.scalar.copy(w2[:, :, 1], b2[:, :, 1]).then_inc(e2_done, 1)
                        nc.scalar.copy(w2[0:META, :, 0], b2[0:META, :, 0]).then_inc(e2_done, 1)
                if step < 32 and (3 * step + 3) // 8 > 3 * step // 8:
                    tanh(3 * step // 8)
            act.wait_ge(pv2_mm, 32)
            for j in range(4):
                act.wait_ge(bz_done, j + 1)
                nc.scalar.copy(asb_hi[:, j], zs[:, j]).then_inc(a_hi, 1)
            for m in range(12, 16):
                tanh(m)
            act.wait_ge(eighths, 8 * N_BR)
            for j in range(8):
                act.wait_ge(o2_done, j + 1)
                nc.scalar.copy(xn_hi[:, j, META:TM], zs[:, 4 + j]).then_inc(a_hi, 1)
            act.wait_ge(a_lo, 12)
            for m in range(KD):
                act.wait_ge(mg_done, m + 1)
                nc.scalar.mul(mg_hi[:, m], gt(m), 0.5).then_inc(mghi_done, 1)
            for half in range(2):
                for t in range(TT):
                    act.wait_ge(eighths, 8 * (N_OUT2 + 2 * half + 1) + 2 * t + 2)
                    if half or t:
                        act.wait_ge(fsq_done, 4 * half + t)
                    A(sq[:, 0], banks[(4, 0)[half] + t][:], ACT.Square, accum_out=tiny[:, 2 * t + half:2 * t + half + 1]).then_inc(fsq_done, 1)
                    if half:
                        if t == 0:
                            act.preload_act_table_set("natural_log_exp_and_others")
                        act.wait_ge(fsum_done, t + 1)
                        A(tiny[:, 20 + t:21 + t], tiny[:, 16 + t:17 + t], ACT.Ln, bias=epsc, scale=1.0 / D).then_inc(fln_done, 1)
                        act.wait_ge(fln_done, 2 * t + 1)
                        A(tiny[:, 24 + t:25 + t], tiny[:, 20 + t:21 + t], ACT.Exp, scale=-0.5).then_inc(fln_done, 1)

        @block.vector
        def _(dve):
            V = nc.vector

            def low(q, d):
                dve.wait_ge(xhi_done, 8 * q + d + 1)
                V.scalar_tensor_tensor(out=xn_lo[:, d, META:TM], in0=xT[:, d], scalar=gain(q, d), in1=xn_hi[:, d, META:TM].bitcast(F32),
                                       op0=ALU.mult, op1=ALU.subtract).then_inc(xlo_done, 1)

            def add_square(q, d):
                dve.wait_ge(sq_done, 8 * q + d + 1)
                if d == 0:
                    V.tensor_copy(sums, sq[:, 0]).then_inc(acc_done, 1)
                else:
                    dve.wait_ge(acc_done, 8 * q + d)
                    V.tensor_tensor(sums, sums, sq[:, d % 2], ALU.add).then_inc(acc_done, 1)

            def add_squares(d):
                for i, total in enumerate((sums, sums2)):
                    n = 24 + 2 * d + i
                    dve.wait_ge(sq_done, n + 1)
                    if d == 0:
                        V.tensor_copy(total, sq[:, i]).then_inc(acc_done, 1)
                    else:
                        dve.wait_ge(acc_done, n - 1)
                        V.tensor_tensor(total, total, sq[:, i], ALU.add).then_inc(acc_done, 1)

            def norm_step(q, d):
                dve.wait_ge(x_ready, 8 * q + d + 1)
                low(q, d)
                if q < 3:
                    add_square(q, d)

            def token_factor(n):
                dve.wait_ge(rt_mm, n)
                V.tensor_copy(rtok[:], banks[7][:, 0:TT]).then_inc(rt_done, 1)

            def ffn(base, n0, q):
                def pair(i, guard):
                    for f in range(2):
                        dve.wait_ge(eighths, 8 * (n0 + 2 * i) + 4 * f + 4)
                        if guard:
                            dve.wait_ge(f_mul, base + 2 * i + f - 1)
                        V.tensor_tensor(gs[:, f], banks[f][:], rstd[:], ALU.mult).then_inc(f_gate, 1)
                    for f in range(2):
                        dve.wait_ge(eighths, 8 * (n0 + 2 * i + 1) + 4 * f + 4)
                        if guard:
                            dve.wait_ge(f_lo, base + 2 * i + f - 1)
                        V.tensor_tensor(hf[:, f], banks[2 + f][:], rstd[:], ALU.mult).then_inc(f_up, 1)
                        dve.wait_ge(f_silu, base + 2 * i + f + 1)
                        dve.wait_ge(f_up, base + 2 * i + f + 1)
                        V.tensor_tensor(hf[:, f], hf[:, f], gs[:, f], ALU.mult).then_inc(f_mul, 1)
                    for f in range(2):
                        dve.wait_ge(f_mul, base + 2 * i + f + 1)
                        dve.wait_ge(f_hi, base + 2 * i + f + 1)
                        at = bass.ds(2 * i + f, 1) if guard else slice(f, f + 1)
                        V.tensor_tensor(h_lo[:, at, :].rearrange("p a t -> p (a t)"), hf[:, f],
                                        h_hi[:, at, :].bitcast(F32).rearrange("p a t -> p (a t)"), ALU.subtract).then_inc(f_lo, 1)
                dve.wait_ge(rstd_done, q + 1)
                pair(0, False)
                if q == 0:
                    meta_split()
                with dve.Fori(1, FP) as i:
                    pair(i, True)
                for d in range(KD + 1):
                    if d < KD:
                        dve.wait_ge(eighths, 8 * (n0 + 3 * FP - 1) + d + 1)
                        V.scalar_tensor_tensor(out=xT[:, d], in0=banks[(d + 4) % 8][:], scalar=0.5, in1=xT[:, d],
                                               op0=ALU.mult, op1=ALU.add).then_inc(x_ready, 1)
                    if d:
                        norm_step(q + 1, d - 1)

            dve.wait_ge(hi_done, 1)
            V.tensor_tensor(w_lo[:, 0], raw[:, 0], w_hi[:, 0].bitcast(F32), ALU.subtract).then_inc(split_done, 1)
            dve.wait_ge(xT_mm, 1)
            V.tensor_copy(cols[:, 0:KD], banks[7][:, 0:KD]).then_inc(cols_ready, 1)
            dve.wait_ge(cols_ready, 1)
            for d in range(KD + 1):
                if d < KD:
                    dve.wait_ge(xT_mm, d + 2)
                    V.tensor_copy(xT[:, d], banks[d][:]).then_inc(x_ready, 1)
                if d:
                    dve.wait_ge(x_ready, d)
                    low(0, d - 1)
            for d in range(KD):
                add_square(0, d)
            dve.wait_ge(meta_act, 3)
            V.tensor_scalar(meta_in[:], meta_in[:], tiny[0:META, 2:3], None, ALU.mult).then_inc(meta_dve, 1)

            def meta_split():
                dve.wait_ge(meta_mm, 1)
                V.tensor_copy(cols[:, KD:ROWS], banks[6][:, KD:ROWS]).then_inc(cols_ready, 1)
                dve.wait_ge(cols_ready, 2)
                V.tensor_tensor(cols[:, V_FG2:V_FG2 + KD], cols[:, V_FIN1:V_FIN1 + KD], cols[:, V_N2:V_N2 + KD], ALU.mult).then_inc(cols_ready, 1)
                V.tensor_tensor(meta_f[:], banks[5][:, 0:KD * META].rearrange("p (k m) -> p k m", k=KD),
                                cols[:, V_N2:V_N2 + KD].unsqueeze(2).to_broadcast([P, KD, META]), ALU.mult).then_inc(meta_dve, 1)
                dve.wait_ge(meta_act, 4)
                dve.wait_ge(meta_dve, 2)
                V.tensor_tensor(xn_lo[:, :, 0:META], meta_f[:], xn_hi[:, :, 0:META].bitcast(F32), ALU.subtract).then_inc(meta_dve, 1)
            ffn(0, N_FFN1, 0)

            dve.wait_ge(mix_in, 80)
            dve.wait_ge(ba_split, 1)
            V.tensor_tensor(wba_lo[:, 0:KD * 8], wba[:].rearrange("p k c -> p (k c)"), wba_hi[:, 0:KD * 8].bitcast(F32), ALU.subtract).then_inc(ba_split, 1)
            for w in (wba_hi, wba_lo):
                V.memset(w[:, KD * 8:wba_w].bitcast(F32), 0.0).then_inc(ba_split, 1)
            V.memset(rw[:, :, 0:3], 0.0).then_inc(conv_step, 1)
            for j in range(12):
                dve.wait_ge(eighths, 8 * N_MIX + 4 * j + 4)
                if j >= 2:
                    dve.wait_ge(conv_done, j - 1)
                V.tensor_tensor(rw[:, j % 2, 3:3 + T], banks[j % 4][:], rstd[:], ALU.mult).then_inc(rw_done, 1)
                dve.wait_ge(rw_done, j + 1)
                if j >= 2:
                    dve.wait_ge(qkv_done, j - 1)
                acc = hf[:, j % 2]
                tap = lambda i: cols[:, V_CONV + 12 * i + j:V_CONV + 12 * i + j + 1]
                dve.wait_ge(conv_step, 3 * j + 1)
                V.tensor_scalar(acc, rw[:, j % 2, 0:T], tap(0), None, ALU.mult).then_inc(conv_step, 1)
                for i in range(1, 4):
                    dve.wait_ge(conv_step, 3 * j + i + 1)
                    V.scalar_tensor_tensor(out=acc, in0=rw[:, j % 2, i:i + T], scalar=tap(i), in1=acc, op0=ALU.mult, op1=ALU.add)\
                        .then_inc(conv_done if i == 3 else conv_step, 1)
                if j == 3:
                    token_factor(1)
                if j == 5:
                    dve.wait_ge(ws_mm, 1)
                    for half in range(2):
                        V.tensor_copy(wsT[:, 4 * half:4 * half + 4].rearrange("p g i -> p (g i)"), banks[6 + half][:]).then_inc(ws_done, 1)
                    dve.wait_ge(ws_done, 2)
                    V.memset(wsT[CH:P, :, 0:CH], 0.0).then_inc(ws_done, 1)
                if j == 4:
                    dve.wait_ge(ba_mm, 1)
                    V.tensor_tensor(baf[:], banks[4][0:8, :], rstd[0:8, :], ALU.mult).then_inc(dve_sm, 1)
                if j == 7:
                    hp = lambda ap: ap.rearrange("p (h t) -> p h t", h=4)
                    head4 = lambda ap: ap.unsqueeze(2).to_broadcast([P, 4, 4])
                    ba = banks[5][:, 0:32].rearrange("p (t c) -> p c t", c=8)
                    dve.wait_ge(ba_mm, 2)
                    dve.wait_ge(act_sm, 1)
                    V.tensor_tensor(hp(s_a), ba[:, 4:8], head4(hvec[:, 0]), ALU.add).then_inc(dve_sm, 1)
                    V.tensor_scalar(s_e, s_e, 1.0, None, ALU.add).then_inc(dve_sm, 1)
                    dve.wait_ge(dve_sm, 3)
                    V.reciprocal(s_beta, s_e).then_inc(dve_sm, 1)
                    dve.wait_ge(act_sm, 5)
                    V.scalar_tensor_tensor(out=s_t, in0=s_a, scalar=0.0, in1=s_t, op0=ALU.max, op1=ALU.add).then_inc(dve_sm, 1)
                    dve.wait_ge(dve_sm, 5)
                    V.scalar_tensor_tensor(out=hp(s_g), in0=hp(s_t), scalar=-1.0, in1=head4(s_ea[:, 0:4]), op0=ALU.mult, op1=ALU.mult).then_inc(dve_sm, 1)
                    dve.wait_ge(cum_mm, 1)
                    V.tensor_copy(s_c.rearrange("p a b -> p (a b)"), banks[5][:, 0:64]).then_inc(dve_sm, 1)
                    dve.wait_ge(dve_sm, 7)
                    V.tensor_scalar(s_ngc, s_c[:, 0], -1.0, None, ALU.mult).then_inc(dve_sm, 1)
                    V.tensor_tensor(s_kd, s_c[:, 1], s_c[:, 0], ALU.subtract).then_inc(dve_sm, 1)
                    dve.wait_ge(act_sm, 6)
                    V.tensor_tensor(s_be, s_beta, s_eg, ALU.mult).then_inc(dve_sm, 1)
                if j == 9:
                    for i in range(8):
                        dve.wait_ge(l2rn, 2 * i + 2)
                        V.scalar_tensor_tensor(out=qkv[:, i], in0=qkv[:, i], scalar=P ** -0.5 if i < 4 else 1.0, in1=gs[:, i % 2],
                                               op0=ALU.mult, op1=ALU.mult).then_inc(l2n, 1)
            dve.wait_ge(act_sm, 8)
            dve.wait_ge(dve_sm, 10)
            for h in range(H):
                at = slice(4 * h, 4 * h + 4)
                e = (sq, hf)[h % 2]
                dve.wait_ge(kt_mm, h + 1)
                V.tensor_tensor(quarters(kb[:, h]), quarters(banks[5][:]), per_block(s_be[:, at]), ALU.mult).then_inc(tok_done, 1)
                V.tensor_tensor(quarters(kd[:, h]), quarters(banks[5][:]), per_block(s_kd[:, at]), ALU.mult).then_inc(tok_done, 1)
                dve.wait_ge(vt_mm, h + 1)
                V.tensor_tensor(quarters(vb[:, h]), quarters(banks[6][:]), per_block(s_beta[:, at]), ALU.mult).then_inc(vb_done, 1)
                dve.wait_ge(exp_done, 8 * h + 4)
                dve.wait_ge(kq_mm, h + 1)
                V.tensor_tensor(atT(h), banks[4][:], e[:, 0], ALU.mult).then_inc(at_done, 1)
                dve.wait_ge(er_done, h + 1)
                V.tensor_tensor(qT(h), qT(h), gs[:, 1], ALU.mult).then_inc(qd_done, 1)
                dve.wait_ge(exp_done, 8 * h + 8)
                for p in range(4):
                    c = slice(p * P, (p + 1) * P)
                    ins = V.scalar_tensor_tensor(out=Lm(h)[:, c], in0=banks[3][:, c], scalar=s_beta[:, 4 * h + p:4 * h + p + 1], in1=e[:, 1, c],
                                                 op0=ALU.mult, op1=ALU.mult)
                ins.then_inc(l_done, 1)
            for g in range(2):
                for hh in range(2):
                    h = 2 * g + hh
                    dve.wait_ge(l_done, h + 1)
                    if g:
                        dve.wait_ge(zt_mm, 2 * (LEVELS - 1) - 1 + hh)
                    V.tensor_tensor(quarters(Mm[:, hh]), quarters(Lm(h)), over4(mixm[:, 6]), ALU.mult).then_inc(m_done, 1)
                    dve.wait_ge(m_done, (g * LEVELS) * 2 + hh + 1)
                    V.tensor_tensor(quarters(Tm[:, hh]), over4(ident), quarters(Mm[:, hh]), ALU.subtract).then_inc(t_init, 1)
                for hh in range(2):
                    h = 2 * g + hh
                    dve.wait_ge(z_mm0, h + 1)
                    V.tensor_tensor(quarters(Z[:, h]), over4(ident), quarters(banks[2 + hh][:]), ALU.subtract).then_inc(z_sub, 1)
                for level in range(LEVELS):
                    for hh in range(2 if level < LEVELS - 1 else 0):
                        h = 2 * g + hh
                        if level == 0:
                            dve.wait_ge(z_mm0, h + 1)
                            dve.wait_ge(t_init, h + 1)
                        else:
                            dve.wait_ge(pp_mm, (g * (LEVELS - 1) + level - 1) * 2 + hh + 1)
                        V.tensor_tensor(quarters(Mm[:, hh]), quarters(Lm(h)), over4(mixm[:, 7 + level]), ALU.mult).then_inc(m_done, 1)
                    for hh in range(2 if level else 0):
                        h = 2 * g + hh
                        n = (g * (LEVELS - 1) + level - 1) * 2 + hh
                        dve.wait_ge(zt_mm, n + 1)
                        if level == 1:
                            dve.wait_ge(z_sub, g * 2 * LEVELS + hh + 1)
                        V.tensor_tensor(Z[:, h], Z[:, h], banks[2 + hh][:], ALU.subtract).then_inc(z_sub, 1)
                        if level < LEVELS - 1:
                            V.tensor_tensor(Tm[:, hh], Tm[:, hh], banks[4 + hh][:], ALU.subtract).then_inc(t_sub, 1)
                    if g == 0 and level in (2, 3):
                        dve.wait_ge(vg_done, TT)
                        for t in range(2 * level - 4, 2 * level - 2):
                            V.bn_stats(st6[:, t], vtok[:, t]).then_inc(ln_st, 1)
                    if g == 0 and level == 4:
                        dve.wait_ge(ln_st, 4)
                        for t in range(TT):
                            V.bn_aggr(mv[:, t], st6[:, t]).then_inc(ln_st, 1)
            for m in range(4):
                dve.wait_ge(sgu_mm, m + 1)
                V.tensor_tensor(quarters(ya[:, m]), quarters(banks[m][:]), over4(bs[:, m]), ALU.add).then_inc(ya_done, 1)
            def ya_low(m):
                dve.wait_ge(y_hi, m + 1)
                V.tensor_tensor(yl(m), ya[:, m], yh(m).bitcast(F32), ALU.subtract).then_inc(y_lo, 1)

            for c in range(NC):
                r = slice(CH * (c % 2), CH * (c % 2) + CH)
                dve.wait_ge(vn_mm, c + 1)
                V.tensor_copy(vnew[r], banks[4][r]).then_inc(vn_done, 1)
                if c < NC - 1:
                    dve.wait_ge(su_mm, c + 1)
                    if c == 0:
                        V.tensor_copy(S[:, 1], banks[5][:]).then_inc(s_done, 1)
                    else:
                        dve.wait_ge(s_done, c)
                        for h in range(H):
                            hc = slice(h * P, (h + 1) * P)
                            ins = V.scalar_tensor_tensor(out=S[:, (c + 1) % 2, hc], in0=S[:, c % 2, hc],
                                                         scalar=egl[:, c % 2, 4 * h + c // 2:4 * h + c // 2 + 1], in1=banks[5][:, hc],
                                                         op0=ALU.mult, op1=ALU.add)
                        ins.then_inc(s_done, 1)
                if 1 <= c <= 4:
                    dve.wait_ge(f_ev, c)
                    dve.wait_ge(ya_done, c)
                    V.tensor_tensor(ya[:, c - 1], ya[:, c - 1], gs[:, (c - 1) % 2], ALU.mult).then_inc(ya_mul, 1)
                if c > 4:
                    ya_low(c - 5)
                if c == NC - 1:
                    ya_low(3)
                    dve.wait_ge(o_mm, NC)
                    for h in range(H):
                        V.tensor_copy(vb[:, h], banks[h][:]).then_inc(ob_done, 1)
                dve.wait_ge(eighths, 8 * (N_MIX + 8) + 4 * c + 4)
                if 2 <= c < 4:
                    dve.wait_ge(ya_mul, c - 1)
                V.tensor_tensor(gs[:, c % 2] if c < 4 else zT[:, c - 4], banks[6 + c % 2][:], rstd[:], ALU.mult).then_inc(fz_ev, 1)
            for h in range(H + 1):
                if h < H:
                    dve.wait_ge(ob_rn, 2 * h + 2)
                    V.scalar_tensor_tensor(out=vb[:, h], in0=vb[:, h], scalar=cols[:, V_DN:V_DN + 1], in1=gs[:, h % 2],
                                           op0=ALU.mult, op1=ALU.mult).then_inc(ob_nrm, 1)
                    dve.wait_ge(ob_nrm, h + 1)
                    dve.wait_ge(f_ev, 4 + h + 1)
                    V.tensor_tensor(vb[:, h], vb[:, h], zT[:, h], ALU.mult).then_inc(yb_done, 1)
                e = h - 1
                if e >= 0:
                    dve.wait_ge(y_hi, 4 + e + 1)
                    dve.wait_ge(yb_done, e + 1)
                    V.tensor_tensor(yl(4 + e), vb[:, e], yh(4 + e).bitcast(F32), ALU.subtract).then_inc(y_lo, 1)
            for m in range(KD + 1):
                if m < KD:
                    dve.wait_ge(eighths, 8 * N_OUT1 + 4 * m + 4)
                    V.tensor_tensor(xT[:, m], xT[:, m], banks[m % 4][:], ALU.add).then_inc(x_ready, 1)
                if m:
                    norm_step(2, m - 1)

            ffn(2 * FP, N_FFN2, 2)

            for d in range(KD):
                add_squares(d)
            dve.wait_ge(rstd_done, 4)
            V.tensor_tensor(gs[:, 1], banks[5][:], rstd[:], ALU.mult).then_inc(r4_st, 1)
            dve.wait_ge(r4_st, 1)
            V.tensor_tensor(gs[:, 1], gs[:, 1], rstd[:], ALU.mult).then_inc(r4_st, 1)
            V.memset(factor[:, 0:META], 1.0).then_inc(f_done, 1)
            dve.wait_ge(r4_ln, 2)
            V.tensor_tensor(factor_t, rstd[:], gs[:, 1], ALU.mult).then_inc(f_done, 1)
            dve.wait_ge(f_done, 2)
            for j in range(4):
                dve.wait_ge(eighths, 8 * N_P2 + 4 * j + 4)
                V.scalar_tensor_tensor(out=Qs[:, j], in0=banks[j][:], scalar=0.125, in1=factor_t, op0=ALU.mult, op1=ALU.mult).then_inc(pq_ev, 1)
                if j == 0:
                    token_factor(2)
            for j in range(6):
                dst = Ks[:, j] if j < 4 else kraw[:] if j == 4 else vwf
                dve.wait_ge(eighths, 8 * (N_P2 + 2) + 4 * j + 4 if j < 4 else 8 * (N_P2 + 6) + 4 * (j - 4) + 4)
                if j == 4:
                    dve.wait_ge(sq_done, 40)
                    for d in range(KD):
                        V.scalar_tensor_tensor(out=xT[:, d], in0=xT[:, d], scalar=cols[:, V_FIN1 + d:V_FIN1 + d + 1], in1=rstd[:],
                                               op0=ALU.mult, op1=ALU.mult).then_inc(x_ready, 1)
                    dve.wait_ge(att_in, 32)
                for half in range(2):
                    hc = slice(264 * half, 264 * half + 264)
                    V.tensor_tensor(dst[:, hc], banks[2 * (j % 2) + half][:, 0:264], factor[:, hc], ALU.mult).then_inc(pq_ev, 1)

            def rope_k(g):
                dve.wait_ge(kr_mm, g + 1)
                if g:
                    dve.wait_ge(kr_done, 2)
                    dve.wait_ge(rope_done, 1)
                for half in range(2):
                    hc = slice(264 * half, 264 * half + 264)
                    V.tensor_tensor(hf[:, half, 0:264], banks[(5, 7)[half]][:, 0:264], sinT[:, hc], ALU.mult).then_inc(kr_st, 1)
                    V.tensor_tensor(Kw[:, g, hc], banks[2 + half][:, 0:264], cosT[:, hc], ALU.mult).then_inc(kr_st, 1)
                for half in range(2):
                    hc = slice(264 * half, 264 * half + 264)
                    dve.wait_ge(kr_st, 4 * g + 2 * half + 2)
                    V.tensor_tensor(Kw[:, g, hc], Kw[:, g, hc], hf[:, half, 0:264], ALU.add).then_inc(kr_done, 1)

            def q_ev(j):
                dve.wait_ge(eighths, 8 * (N_P2 + 7) + 4 * j + 4)
                if j >= 2:
                    dve.wait_ge(rot_mm, j - 1)
                    dve.wait_ge(rp_st, 2 * (j - 1))
                else:
                    dve.wait_ge(vw_mm, 2)
                V.scalar_tensor_tensor(out=gs[:, j % 2], in0=banks[j % 2][:], scalar=0.125, in1=factor_t, op0=ALU.mult, op1=ALU.mult).then_inc(pq_ev, 1)

            V.memset(kblk[:], 0.0).then_inc(kb_done, 1)
            dve.wait_ge(kb_done, 1)
            dve.wait_ge(pq_ev, 12)
            for half in range(2):
                r = slice(HD * half, HD * half + HD)
                V.tensor_copy(kblk[r, :, META * half:META * half + META], Ks[r, :, 0:META]).then_inc(kb_done, 1)
            rope_k(0)
            q_ev(0)
            for j in range(8):
                if j < 7:
                    q_ev(j + 1)
                dve.wait_ge(rot_mm, j + 1)
                dve.wait_ge(pq_ev, 16 + j + 1)
                if j < 2:
                    dve.wait_ge(kr_done, 2 + 2 * j)
                else:
                    dve.wait_ge(rope_done, j - 1)
                V.tensor_tensor(hf[:, j % 2], banks[(6, 4)[j % 2]][:], sinT[:, META:], ALU.mult).then_inc(rp_st, 1)
                V.tensor_tensor(Qw[:, j], gs[:, j % 2], cosT[:, META:], ALU.mult).then_inc(rp_st, 1)
                dve.wait_ge(rp_st, 2 * j + 2)
                V.tensor_tensor(Qw[:, j], Qw[:, j], hf[:, j % 2], ALU.add).then_inc(rope_done, 1)
                if j == 0:
                    rope_k(1)

            def gate_ev(t):
                dve.wait_ge(eighths, 8 * (N_P2 + 11) + 4 * t + 4)
                V.tensor_tensor(zs[:, t] if t < 12 else gt(t - 12), banks[6 + t % 2][:], factor_t, ALU.mult).then_inc(f2_ev, 1)

            dve.wait_ge(am_st, 3)
            dve.wait_ge(rope_done, 8)
            V.scalar_tensor_tensor(out=hf[:, 0], in0=banks[2][:], scalar=0.0, in1=sq[:, 0], op0=ALU.max, op1=ALU.add).then_inc(gm_st, 1)
            dve.wait_ge(gm_st, 1)
            V.tensor_tensor_scan(gs[:, 0, ::-1], meta_mask[:, ::-1], hf[:, 0, ::-1], 0.0, ALU.mult, ALU.add).then_inc(gm_st, 1)
            dve.wait_ge(gm_st, 2)
            V.tensor_tensor(argm[:], banks[2][:], gs[:, 0], ALU.subtract).then_inc(gm_st, 1)
            dve.wait_ge(gm_st, 3)
            for u in range(32 + 4):
                if u < 32:
                    n = (u % 4 + 1) * P
                    bank = banks[u % 2]
                    dve.wait_ge(a_st, 3 * u + 3)
                    if u >= 1:
                        dve.wait_ge(d_st, 4 * u)
                    V.scalar_tensor_tensor(out=hf[:, 1, 0:n], in0=bank[:, 0:n], scalar=0.0, in1=sq[:, u % 2, 0:n], op0=ALU.max, op1=ALU.add).then_inc(d_st, 1)
                    dve.wait_ge(d_st, 4 * u + 1)
                    if u >= 3:
                        dve.wait_ge(x_mm, u - 2)
                    w = w3(u)[:, 0:n]
                    V.tensor_tensor_scan(w[:, ::-1], hf[:, 1, 0:n][:, ::-1], scan_mask[:, T - n:T][:, ::-1], 0.0, ALU.add, ALU.mult).then_inc(d_st, 1)
                    dve.wait_ge(d_st, 4 * u + 2)
                    V.tensor_copy(ctok[:, u:u + 1], w[:, 0:1]).then_inc(d_st, 1)
                    dve.wait_ge(d_st, 4 * u + 3)
                    V.tensor_tensor(w, bank[:, 0:n], w, ALU.subtract).then_inc(d_st, 1)
                    dve.wait_ge(d_st, 4 * u + 4)
                    V.tensor_tensor(w[:, n - P:n], w[:, n - P:n], neg_diag, ALU.add).then_inc(g_done, 1)
                    if u % 4 == 3:
                        h = u // 4
                        if h >= 2:
                            dve.wait_ge(xm_mm, h - 1)
                        V.tensor_tensor(wm[:, h % 2].rearrange("p (a b) -> p a b", a=4), argm[:].rearrange("p (j t h m) -> p j h t m", j=4, t=4, h=2)[:, h // 2, h % 2],
                                        ctok[:, 4 * h:4 * h + 4].unsqueeze(2).to_broadcast([P, 4, META]), ALU.subtract).then_inc(tm_done, 1)
                if u < 32 and (3 * u + 3) // 8 > 3 * u // 8:
                    gate_ev(3 * u // 8)
                if u >= 10 and u % 8 == 2:
                    j = (u - 10) // 8
                    dve.wait_ge(pvm_mm, 2 * j + 2)
                    V.tensor_copy(Qs[:, j], banks[4][:]).then_inc(o1_done, 1)
            V.tensor_scalar(tiny[:, 32:48], sinks[:], -1.0, None, ALU.mult).then_inc(s_st, 1)
            for j in range(4):
                dve.wait_ge(zsilu, j + 1)
                dve.wait_ge(o1_done, j + 1)
                V.tensor_tensor(zs[:, j], zs[:, j], Qs[:, j], ALU.mult).then_inc(bz_done, 1)
            for step in range(32 + 4):
                v = step
                if v < 32:
                    o = 112 if v % 4 == 0 else 0
                    j = v // 4
                    s2 = w3(v).rearrange("p (a b) -> p a b", a=2)[:, :, o:]
                    b2 = banks[v % 2][:].rearrange("p (a b) -> p a b", a=2)[:, :, o:]
                    c = 8 * (v % 2)
                    dve.wait_ge(z2_mm, 2 * v + 2)
                    if v >= 3:
                        dve.wait_ge(x2_mm, v - 2)
                    elif v == 0:
                        dve.wait_ge(x_mm, 32)
                    V.tensor_tensor(s2, b2, win_mask[:, o:].unsqueeze(1).to_broadcast([P, 2, 256 - o]), ALU.add).then_inc(s_st, 1)
                    dve.wait_ge(s_st, 1 + 3 * v + 1)
                    if v >= 2:
                        dve.wait_ge(p2_done, 3 * (v - 1))
                    V.tensor_reduce(tiny[:, c:c + 2], s2, AX_X, ALU.max).then_inc(s_st, 1)
                    dve.wait_ge(s_st, 1 + 3 * v + 2)
                    V.scalar_tensor_tensor(out=tiny[:, c + 2:c + 4], in0=tiny[:, c:c + 2], scalar=-1.0, in1=tiny[:, 32 + 2 * j:34 + 2 * j],
                                           op0=ALU.mult, op1=ALU.min).then_inc(s_st, 1)
                    dve.wait_ge(s_st, 1 + 3 * v + 3)
                    V.tensor_tensor(tiny[:, c + 4:c + 6], tiny[:, c + 2:c + 4], tiny[:, 32 + 2 * j:34 + 2 * j], ALU.subtract).then_inc(s2_done, 1)
                v = step - 1
                if 0 <= v < 32:
                    o = 112 if v % 4 == 0 else 0
                    e = 16 + 4 * (v % 2)
                    s2 = w3(v).rearrange("p (a b) -> p a b", a=2)
                    dve.wait_ge(p2_done, 3 * v + 3)
                    if v >= 1:
                        dve.wait_ge(pn_done, v)
                    V.tensor_tensor(tiny[:, 24:26], tiny[:, e:e + 2], tiny[:, e + 2:e + 4], ALU.add).then_inc(n_st, 1)
                    dve.wait_ge(n_st, 2 * v + 1)
                    V.reciprocal(tiny[:, 26:28], tiny[:, 24:26]).then_inc(n_st, 1)
                    dve.wait_ge(n_st, 2 * v + 2)
                    for i in range(2):
                        ins = V.tensor_scalar(s2[:, i, o:], s2[:, i, o:], tiny[:, 26 + i:27 + i], None, ALU.mult)
                    ins.then_inc(pn_done, 1)
                if step < 32 and (3 * step + 3) // 8 > 3 * step // 8:
                    if step < 3:
                        dve.wait_ge(bz_done, 4)
                    gate_ev(12 + 3 * step // 8)
                if step >= 7 and step % 4 == 3:
                    j = (step - 7) // 4
                    dve.wait_ge(pv2_mm, 4 * j + 4)
                    dve.wait_ge(zsilu, 5 + j)
                    V.tensor_tensor(zs[:, 4 + j], zs[:, 4 + j], banks[4 + j % 2][:], ALU.mult).then_inc(o2_done, 1)
            for j in range(4):
                dve.wait_ge(a_hi, j + 1)
                V.tensor_tensor(asb_lo[:, j], zs[:, j], asb_hi[:, j].bitcast(F32), ALU.subtract).then_inc(a_lo, 1)
            for t in range(24, 28):
                gate_ev(t)
            for j in range(8):
                dve.wait_ge(a_hi, 4 + j + 1)
                dve.wait_ge(o2_done, j + 1)
                V.tensor_tensor(xn_lo[:, j, META:TM], zs[:, 4 + j], xn_hi[:, j, META:TM].bitcast(F32), ALU.subtract).then_inc(a_lo, 1)
            dve.wait_ge(th_done, 16)
            for half in range(2):
                for m in range(4 * half, 4 * half + 4):
                    dve.wait_ge(eighths, 8 * (N_BR + 3 * half) + 2 * (m % 4) + 2)
                    V.scalar_tensor_tensor(out=gt(m), in0=gt(m), scalar=1.0, in1=banks[m % 2][:], op0=ALU.add, op1=ALU.mult).then_inc(sb_ev, 1)
                for m in range(4 * half, 4 * half + 4):
                    dve.wait_ge(eighths, 8 * (N_BR + 3 * half + 1) + 4 * (m % 4) + 4)
                    if m >= 2:
                        dve.wait_ge(mg_done, m - 1)
                    V.scalar_tensor_tensor(out=hf[:, m % 2], in0=gt(8 + m), scalar=1.0, in1=banks[2 + m % 2][:], op0=ALU.add, op1=ALU.mult).then_inc(sw_st, 1)
                    dve.wait_ge(sw_st, m + 1)
                    dve.wait_ge(sb_ev, m + 1)
                    V.tensor_tensor(gt(m), gt(m), hf[:, m % 2], ALU.add).then_inc(mg_done, 1)
                    dve.wait_ge(mghi_done, m + 1)
                    dve.wait_ge(mg_done, m + 1)
                    V.scalar_tensor_tensor(out=mg_lo[:, m], in0=gt(m), scalar=0.5, in1=mg_hi[:, m].bitcast(F32), op0=ALU.mult, op1=ALU.subtract).then_inc(mglo_done, 1)
            dve.wait_ge(gain_done, 16)
            for t in range(TT):
                dve.wait_ge(fsq_done, 4 + t + 1)
                V.tensor_tensor(tiny[:, 16 + t:17 + t], tiny[:, 2 * t:2 * t + 1], tiny[:, 2 * t + 1:2 * t + 2], ALU.add).then_inc(fsum_done, 1)
                dve.wait_ge(fln_done, 2 * t + 2)
                for half in range(2):
                    c = slice(512 * half, 512 * half + 512)
                    V.scalar_tensor_tensor(out=ost[:, t, c], in0=banks[(4, 0)[half] + t][:], scalar=tiny[:, 24 + t:25 + t], in1=gain_row[:, c],
                                           op0=ALU.mult, op1=ALU.mult).then_inc(ost_v, 1)

        @block.tensor
        def _(pe):
            mm1 = nc.tensor.matmul

            def three(bank, hi, lo, rhi, rlo, start, stop):
                mm1(bank, hi, rhi, start=start, stop=False)
                mm1(bank, hi, rlo, start=False, stop=False)
                return mm1(bank, lo, rhi, start=False, stop=stop)

            def feature_steps(n, f, k0, k1, bank):
                slot = n % 2
                if k0 == 0 and f == 0:
                    pe.wait_ge(split_done, n + 1)
                for k in range(k0, k1):
                    c = k * SC + f * P
                    ins = three(bank[:], w_hi[:, slot, c:c + P], w_lo[:, slot, c:c + P], xn_hi[:, k, META:TM], xn_lo[:, k, META:TM], k == 0, k == KD - 1)
                    if k % 2:
                        ins.then_inc(eighths, 1)

            def stat(q):
                pe.wait_ge(acc_done, 8 * q + 8 if q < 3 else 40)
                ins = mm1(banks[4][:], ones, sums, start=True, stop=True)
                if q == 3:
                    ins = mm1(banks[5][:], ones, sums2, start=True, stop=True)
                ins.then_inc(stat_mm, 1)

            def token_factor(from_):
                for t in range(TT):
                    ins = mm1(banks[7][:, t:t + 1], from_[:, t * P:(t + 1) * P], ident[:, 0:1], start=True, stop=True)
                ins.then_inc(rt_mm, 1)

            def first_tiles(q, n):
                pe.wait_ge(split_done, n + 1)
                pe.wait_ge(x_ready, 8 * q + 6 if q else 2)
                for k in range(KD):
                    pe.wait_ge(xlo_done, 8 * q + k + 1)
                    for f in range(2):
                        c = k * SC + f * P
                        ins = three(banks[f][:], w_hi[:, n % 2, c:c + P], w_lo[:, n % 2, c:c + P], xn_hi[:, k, META:TM], xn_lo[:, k, META:TM],
                                    k == 0, k == KD - 1)
                        if k == KD - 1:
                            ins.then_inc(eighths, 4)

            def ffn(base, n0, q):
                def pair(i, first):
                    for part, freed in ((0, f_gate), (1, f_up)):
                        slot = (n0 + part) % 2
                        pe.wait_ge(split_done, n0 + 2 * i + part + 1)
                        if first and part == 0:
                            first_tiles(q, n0)
                            continue
                        for f in range(2):
                            if first:
                                pe.wait_ge(x_ready, 8 * q + 5 + 2 * part + f)
                            else:
                                pe.wait_ge(freed, base + 2 * i + f - 1)
                            for k in range(KD):
                                c = k * SC + f * P
                                ins = three(banks[2 * part + f][:], w_hi[:, slot, c:c + P], w_lo[:, slot, c:c + P],
                                            xn_hi[:, k, META:TM], xn_lo[:, k, META:TM], k == 0, k == KD - 1)
                                if k % 2:
                                    ins.then_inc(eighths, 1)
                            if first and f == 0:
                                stat(q)
                pair(0, True)
                if q == 0:
                    meta_turn()
                with pe.Fori(1, FP) as i:
                    pair(i, False)
                n1 = n0 + 2 * FP

                def down(m, slot, first, last):
                    pe.wait_ge(split_done, n1 + m + 1)
                    pe.wait_ge(f_lo, base + 2 * m + 2)
                    for d in range(KD):
                        if first and d == 4:
                            pe.wait_ge(f_gate, base + 2 * FP)
                            pe.wait_ge(f_up, base + 2 * FP)
                        for kk in range(2):
                            c = kk * D + d * P
                            at = slice(2 * m + kk, 2 * m + kk + 1) if isinstance(m, int) else bass.ds(2 * m + kk, 1)
                            ins = three(banks[(d + 4) % 8][:], w_hi[:, slot, c:c + P], w_lo[:, slot, c:c + P],
                                        h_hi[:, at, :].rearrange("p a t -> p (a t)"), h_lo[:, at, :].rearrange("p a t -> p (a t)"),
                                        first and kk == 0, last and kk == 1)
                        ins.then_inc(eighths, 1)
                down(0, n1 % 2, True, False)
                with pe.Fori(0, (FP - 3) // 2) as j:
                    down(2 * j + 1, (n1 + 1) % 2, False, False)
                    down(2 * j + 2, n1 % 2, False, False)
                down(FP - 2, (n1 + 1) % 2, False, False)
                down(FP - 1, n1 % 2, False, True)

            pe.wait_ge(consts, 16)

            def turn(t, d, done):
                ins = nc.tensor.transpose(banks[d][:, t * P:(t + 1) * P], xload[:, t, d * P:(d + 1) * P], ident)
                if done:
                    ins.then_inc(xT_mm, 1)
            for t in range(TT - 1):
                pe.wait_ge(x_loaded[t], 16)
                for d in range(KD - 1):
                    turn(t, d, False)
            pe.wait_ge(row0_in, 16)
            nc.tensor.transpose(banks[7][:, 0:KD], rows[0:KD, :], ident[0:KD, 0:KD]).then_inc(xT_mm, 1)
            pe.wait_ge(x_loaded[TT - 1], 16)
            for d in range(KD - 1):
                turn(TT - 1, d, True)
            pe.wait_ge(cols_ready, 1)
            for t in range(TT):
                turn(t, KD - 1, t == TT - 1)

            def meta_turn():
                pe.wait_ge(rows_in, 96)
                nc.tensor.transpose(banks[6][:, 0:ROWS], rows[0:ROWS, :], ident[0:ROWS, 0:ROWS])
                pe.wait_ge(meta_dve, 1)
                for d in range(KD):
                    ins = nc.tensor.transpose(banks[5][:, d * META:(d + 1) * META], meta_in[:, d * P:(d + 1) * P], ident[0:META, 0:META])
                ins.then_inc(meta_mm, 1)
            ffn(0, N_FFN1, 0)

            def lengths(i0):
                for i in range(i0, min(i0 + 2, 8)):
                    pe.wait_ge(l2sq, i + 1)
                    if i < 2:
                        pe.wait_ge(dve_sm, 7)
                    else:
                        pe.wait_ge(l2rn, 2 * i - 3)
                    mm1(banks[4 + i % 2][:], ones, sq[:, i % 2], start=True, stop=True).then_inc(l2mm, 1)

            for j in range(12):
                n, f = N_MIX + j // 2, j % 2
                if j < 2:
                    if j == 0:
                        first_tiles(1, n)
                        stat(1)
                    continue
                if j >= 4:
                    pe.wait_ge(rw_done, j - 3)
                else:
                    pe.wait_ge(x_ready, 8 + 5 + j)
                feature_steps(n, f, 0, 4, banks[j % 4])
                if j == 9:
                    pe.wait_ge(dve_sm, 6)
                    for i, w in enumerate((cumT, same, half0, half1)):
                        ins = mm1(banks[5][:, 16 * i:16 * i + 16], w, s_g, start=True, stop=True)
                    ins.then_inc(cum_mm, 1)
                if j >= 10:
                    lengths(4 * j - 38)
                feature_steps(n, f, 4, KD, banks[j % 4])
                if j >= 9:
                    lengths(4 * j - 36)
                if j == 3:
                    pe.wait_ge(rstd_done, 2)
                    token_factor(rstd)
                if j == 4:
                    pe.wait_ge(mix_in, 80)
                    pe.wait_ge(rt_done, 1)
                    for g in range(GG):
                        ins = nc.tensor.transpose(banks[6 + g // 4][:, (g % 4) * P:(g % 4 + 1) * P], wsraw[:, g], ident)
                    ins.then_inc(ws_mm, 1)
                if j == 3:
                    pe.wait_ge(ba_split, 4)
                    for k in range(KD):
                        c = slice(8 * k, 8 * k + P)
                        ins = three(banks[4][:], wba_hi[:, c], wba_lo[:, c], xn_hi[:, k, META:TM], xn_lo[:, k, META:TM], k == 0, k == KD - 1)
                    ins.then_inc(ba_mm, 1)
                if j == 6:
                    pe.wait_ge(dve_sm, 1)
                    for t in range(TT):
                        ins = nc.tensor.transpose(banks[5][:, 8 * t:8 * t + 8], baf[:, t * P:(t + 1) * P], ident[0:8, 0:8])
                    ins.then_inc(ba_mm, 1)

            def token_tile(n, t, bank, c0):
                c = slice(META + t * P, META + (t + 1) * P)
                for k in range(KD):
                    w = slice(k * SC, (k + 1) * SC)
                    o = bank[:, c0:c0 + SC]
                    mm1(o, xn_hi[:, k, c], w_hi[:, n % 2, w], start=k == 0, stop=False)
                    mm1(o, xn_hi[:, k, c], w_lo[:, n % 2, w], start=False, stop=False)
                    ins = mm1(o, xn_lo[:, k, c], w_hi[:, n % 2, w], start=False, stop=k == KD - 1)
                    if k % 4 == 3:
                        ins.then_inc(eighths, 1)
            def gate_tile(j):
                n, t = N_MIX + 6 + j // 4, j % 4
                if t == 0:
                    pe.wait_ge(split_done, n + 1)
                if j == 0:
                    pe.wait_ge(ws_done, 2)
                elif j == 6:
                    pe.wait_ge(va_done, 2)
                token_tile(n, t, banks[(7, 0, 1, 7)[j // 2]], SC * (j % 2))

            pair = [slice(p * P, (p + 1) * P) for p in range(4)]
            gate_tile(0)
            gate_tile(1)
            pe.wait_ge(l2n, 8)
            pe.wait_ge(rw_done, 12)
            for h in range(H):
                if h:
                    pe.wait_ge(rs_done, h)
                for p in range(4):
                    ins = mm1(banks[2][:, p * P:(p + 1) * P], s_g[:, 4 * h + p:4 * h + p + 1].to_broadcast([P, P]), cumT, start=True, stop=True)
                ins.then_inc(r_mm, 1)
                if h:
                    pe.wait_ge(tok_done, 2 * h)
                for c in pair:
                    ins = nc.tensor.transpose(banks[5][:, c], kT(h)[:, c], ident)
                ins.then_inc(kt_mm, 1)
                pe.wait_ge(qkv_done, 8 + h + 1)
                if h:
                    pe.wait_ge(vb_done, h)
                for c in pair:
                    ins = nc.tensor.transpose(banks[6][:, c], vT(h)[:, c], ident)
                ins.then_inc(vt_mm, 1)
                if h:
                    pe.wait_ge(l_done, h)
                for c in pair:
                    ins = mm1(banks[3][:, c], kT(h)[:, c], kT(h)[:, c], start=True, stop=True)
                for c in pair:
                    ins = mm1(banks[4][:, c], kT(h)[:, c], qT(h)[:, c], start=True, stop=True)
                ins.then_inc(kq_mm, 1)
                for j in ((2, 3), (4,), (5,), (6, 7))[h]:
                    gate_tile(j)
            pe.wait_ge(va_done, 8)
            for g in range(2):
                for hh in range(2):
                    h = 2 * g + hh
                    pe.wait_ge(m_done, g * LEVELS * 2 + hh + 1)
                    if g:
                        pe.wait_ge(z_sub, 2 * LEVELS - 1 + hh)
                    for c in pair:
                        ins = nc.tensor.transpose(banks[2 + hh][:, c], Mm[:, hh, c], ident)
                    ins.then_inc(z_mm0, 1)
                for level in range(1, LEVELS):
                    last = level == LEVELS - 1
                    for hh in range(2):
                        h = 2 * g + hh
                        n = (g * (LEVELS - 1) + level - 1) * 2 + hh
                        pe.wait_ge(m_done, (g * LEVELS + level) * 2 + hh + 1)
                        pe.wait_ge(z_sub, (g * LEVELS + level - 1) * 2 + hh + 1)
                        if n >= 2:
                            pe.wait_ge(pp_copy, n - 1)
                        for c in pair:
                            ins = mm1(banks[hh][:, c], Mm[:, hh, c], Z[:, h, c], start=True, stop=True)
                        ins.then_inc(pp_mm, 1)
                    for hh in range(2):
                        h = 2 * g + hh
                        n = (g * (LEVELS - 1) + level - 1) * 2 + hh
                        pe.wait_ge(pp_copy, n + 1)
                        if level > 1:
                            pe.wait_ge(t_sub, (g * (LEVELS - 2) + level - 2) * 2 + hh + 1)
                        elif g:
                            pe.wait_ge(t_sub, 2 * (LEVELS - 2))
                            pe.wait_ge(t_init, 2 * g + hh + 1)
                        else:
                            pe.wait_ge(t_init, hh + 1)
                        for c in pair:
                            ins = mm1(banks[2 + hh][:, c], Tm[:, hh, c], Pp[:, hh, c], start=True, stop=True)
                        if not last:
                            for c in pair:
                                ins = mm1(banks[4 + hh][:, c], Pp[:, hh, c], Tm[:, hh, c], start=True, stop=True)
                        ins.then_inc(zt_mm, 1)
            for h in range(H):
                pe.wait_ge(z_sub, 2 * LEVELS * (h // 2 + 1) - 1 + h % 2)
                if h >= 2:
                    pe.wait_ge(nw_done, h - 1)
                for c in pair:
                    ins = mm1(banks[6 + h % 2][:, c], kb[:, h, c], Z[:, h, c], start=True, stop=True)
                ins.then_inc(nw_mm, 1)
            pe.wait_ge(ln_app, 12)
            pe.wait_ge(ws_done, 3)
            pe.wait_ge(z_sub, 4 * LEVELS)
            for m in range(4):
                for t in range(TT):
                    for half in range(2):
                        r = slice(CH * half, CH * half + CH)
                        ins = mm1(banks[m][r, t * P:(t + 1) * P], vtok[:, t, m * P + CH * half:m * P + CH * half + CH], wsT[:, 2 * m + half], start=True, stop=True)
                ins.then_inc(sgu_mm, 1)
            pe.wait_ge(nw_done, 4)
            for c in range(NC):
                p, r = c // 2, slice(CH * (c % 2), CH * (c % 2) + CH)
                cc = slice(c * CH, (c + 1) * CH)
                if c:
                    pe.wait_ge(s_done, c)
                    pe.wait_ge(vn_done, c)
                else:
                    pe.wait_ge(t_sub, 4 * (LEVELS - 2))
                for h in range(H):
                    hc = slice(h * P, (h + 1) * P)
                    ins = mm1(banks[4][:, hc], Z[:, h, p * P:(p + 1) * P], vb[:, h, p * P:(p + 1) * P], start=True, stop=c == 0)
                    if c:
                        ins = mm1(banks[4][:, hc], kb[:, h, p * P:(p + 1) * P], S[:, c % 2, hc], start=False, stop=True)
                ins.then_inc(vn_mm, 1)
                if c:
                    for h in range(H):
                        mm1(banks[h][:, cc], S[:, c % 2, h * P:(h + 1) * P], qT(h)[:, cc], start=True, stop=False)
                else:
                    pe.wait_ge(ya_done, 4)
                n, f = N_MIX + 8 + c // 2, c % 2
                if c >= 2:
                    pe.wait_ge(fz_ev, c - 1)
                feature_steps(n, f, 0, 4, banks[6 + c % 2])
                pe.wait_ge(vn_done, c + 1)
                if c < NC - 1:
                    for h in range(H):
                        ins = mm1(banks[5][:, h * P:(h + 1) * P], kd[r, h, p * P:(p + 1) * P], vnew[r, h * P:(h + 1) * P], start=True, stop=True)
                    ins.then_inc(su_mm, 1)
                for h in range(H):
                    ins = mm1(banks[h][:, cc], vnew[r, h * P:(h + 1) * P], atT(h)[r, cc], start=c == 0, stop=True)
                ins.then_inc(o_mm, 1)
                feature_steps(n, f, 4, KD, banks[6 + c % 2])
            def out_steps(m, k0, k1):
                n, f = N_OUT1 + m // 2, m % 2
                for k in range(k0, k1):
                    if m == 0:
                        pe.wait_ge(y_lo, k + 1)
                    c = k * SC + f * P
                    ins = three(banks[m % 4][:], w_hi[:, n % 2, c:c + P], w_lo[:, n % 2, c:c + P], yh(k), yl(k), k == 0, k == KD - 1)
                if k1 == KD:
                    ins.then_inc(eighths, 4)
            for m in range(4):
                if m % 2 == 0:
                    pe.wait_ge(split_done, N_OUT1 + m // 2 + 1)
                pe.wait_ge(ob_done, m + 1)
                out_steps(m, 0, 4)
                for h in ((0, 1), (2, 3), (), ())[m]:
                    pe.wait_ge(ob_sq, h + 1)
                    if h >= 2:
                        pe.wait_ge(ob_rn, 2 * h - 3)
                    mm1(banks[4 + h % 2][:], ones, sq[:, h % 2], start=True, stop=True).then_inc(ob_mm, 1)
            for m in range(4):
                out_steps(m, 4, KD)
            for m in range(4, KD):
                if m % 2 == 0:
                    pe.wait_ge(split_done, N_OUT1 + m // 2 + 1)
                pe.wait_ge(x_ready, 16 + m - 3)
                out_steps(m, 0, KD)

            ffn(2 * FP, N_FFN2, 2)

            for j in range(4):
                if j < 2:
                    if j == 0:
                        first_tiles(3, N_P2)
                    continue
                pe.wait_ge(x_ready, 24 + 5 + j)
                feature_steps(N_P2 + j // 2, j % 2, 0, KD, banks[j])
                if j == 2:
                    stat(3)
            pe.wait_ge(f_done, 2)
            token_factor(factor_t)

            def key_tile(n, f, b):
                for half in range(2):
                    hc = slice(264 * half, 264 * half + 264)
                    for k in range(KD):
                        c = k * SC + f * P
                        ins = three(banks[b + half][:, 0:264], w_hi[:, n % 2, c:c + P], w_lo[:, n % 2, c:c + P], xn_hi[:, k, hc], xn_lo[:, k, hc], k == 0, k == KD - 1)
                        if half and k % 2:
                            ins.then_inc(eighths, 1)

            def value_tile(n, t, o, f0, width, incs):
                c = slice(0, P) if t is None else slice(META + t * P, META + (t + 1) * P)
                for k in range(KD):
                    w = slice(k * SC + f0, k * SC + f0 + width)
                    mm1(o, xn_hi[:, k, c], w_hi[:, n % 2, w], start=k == 0, stop=False)
                    mm1(o, xn_hi[:, k, c], w_lo[:, n % 2, w], start=False, stop=False)
                    ins = mm1(o, xn_lo[:, k, c], w_hi[:, n % 2, w], start=False, stop=k == KD - 1)
                    if incs and (k + 1) % (KD // incs) == 0:
                        ins.then_inc(eighths, 1)

            for j in range(4):
                n = N_P2 + 2 + j // 2
                if j % 2 == 0:
                    pe.wait_ge(split_done, n + 1)
                pe.wait_ge(pq_ev, (2, 4, 6, 8)[j])
                key_tile(n, j % 2, 2 * (j % 2))
            for s in range(2):
                n = N_P2 + 4 + s
                pe.wait_ge(split_done, n + 1)
                if s:
                    pe.wait_ge(pt_ev, 5)
                value_tile(n, None, banks[6][:, 0:SC], 0, SC, 0)
                for t in range(TT):
                    value_tile(n, t, banks[4 + t // 2][:, SC * (t % 2):SC * (t % 2) + SC], 0, SC, 2)
            n = N_P2 + 6
            pe.wait_ge(split_done, n + 1)
            pe.wait_ge(pq_ev, 10)
            key_tile(n, 0, 0)
            pe.wait_ge(pt_ev, 10)
            pe.wait_ge(pq_ev, 12)
            key_tile(n, 1, 2)

            def turn_values():
                nc.tensor.transpose(banks[6][0:META, 0:P], vwf[:, 0:META], ident).then_inc(vw_mm, 1)
                for t in range(TT):
                    ins = nc.tensor.transpose(banks[4][:, t * P:(t + 1) * P], vwf[:, META + t * P:META + (t + 1) * P], ident)
                ins.then_inc(vw_mm, 1)

            def rotate_k(g):
                for w, bb in ((dup_k[g], (2, 3)), (rot_k[g], (5, 7))):
                    for half in range(2):
                        ins = mm1(banks[bb[half]][:, 0:264], w, kraw[:, 264 * half:264 * half + 264], start=True, stop=True)
                ins.then_inc(kr_mm, 1)

            def rotate_q(j):
                pe.wait_ge(pq_ev, 16 + j + 1)
                if j >= 2:
                    pe.wait_ge(rope_done, j - 1)
                else:
                    pe.wait_ge(pt_ev, 12)
                mm1(banks[(6, 4)[j % 2]][:], rot_q, gs[:, j % 2], start=True, stop=True).then_inc(rot_mm, 1)
            pe.wait_ge(pq_ev, 16)
            pe.wait_ge(att_in, 32)
            rotate_k(0)
            turn_values()
            for j in range(8):
                if j >= 2:
                    pe.wait_ge(pq_ev, 16 + j - 1)
                feature_steps(N_P2 + 7 + j // 2, j % 2, 0, KD, banks[j % 2])
                if j:
                    rotate_q(j - 1)
                if j == 1:
                    pe.wait_ge(kr_done, 2)
                    rotate_k(1)
            rotate_q(7)

            gate_at = [0]

            def gate_steps(count):
                for i in range(gate_at[0], gate_at[0] + count):
                    t, k = i // KD, i % KD
                    if k == 0:
                        if t >= 2:
                            pe.wait_ge(f2_ev, t - 1)
                        else:
                            pe.wait_ge(rope_done, 8)
                    feature_steps(N_P2 + 11 + t // 2, t % 2, k, k + 1, banks[6 + t % 2])
                gate_at[0] += count

            pe.wait_ge(kr_done, 4)
            pe.wait_ge(kb_done, 3)
            for i in range(4 * TT):
                j, t, c = i // TT, i % TT, i * 2 * META
                ins = mm1(banks[2][:, c:c + 2 * META], Qs[:, j, t * P:(t + 1) * P], kblk[:, j], start=True, stop=True)
            ins.then_inc(zm_mm, 1)
            for step in range(32 + 3):
                u = step
                if u < 32:
                    h, t = u // 4, u % 4
                    r, j, n = slice(HD * (h % 2), HD * (h % 2) + HD), h // 2, (t + 1) * P
                    if u >= 2:
                        pe.wait_ge(g_done, u - 1)
                    else:
                        pe.wait_ge(pq_ev, 24)
                    mm1(banks[u % 2][:, 0:n], Qs[r, j, t * P:(t + 1) * P], Ks[r, j, META:META + n], start=True, stop=True).then_inc(z_mm, 1)
                    gate_steps(1)
                u = step - 2
                if 0 <= u < 32:
                    h, t = u // 4, u % 4
                    pe.wait_ge(w_done, u + 1)
                    if u >= 2:
                        pe.wait_ge(e_done, u - 1)
                    for b in range(t + 1):
                        ins = nc.tensor.transpose(banks[2 + u % 2][:, b * P:(b + 1) * P], w3(u)[:, b * P:(b + 1) * P], ident)
                    ins.then_inc(x_mm, 1)
                    if t == 3:
                        pe.wait_ge(wm_done, h + 1)
                        if h:
                            pe.wait_ge(em_done, h)
                        for b in range(TT):
                            ins = nc.tensor.transpose(banks[5][0:META, b * P:(b + 1) * P], wm[:, h % 2, b * META:(b + 1) * META], ident)
                        ins.then_inc(xm_mm, 1)
                if step < 32:
                    gate_steps(1)
                u = step - 3
                if 0 <= u < 32:
                    h, t = u // 4, u % 4
                    r, hc = slice(HD * (h % 2), HD * (h % 2) + HD), slice(HD * h, HD * h + HD)
                    pe.wait_ge(e_done, u + 1)
                    if u % 8 == 0:
                        if u:
                            pe.wait_ge(o1_done, u // 8)
                        else:
                            pe.wait_ge(rope_done, 8)
                    for b in range(t + 1):
                        ins = mm1(banks[4][r, t * P:(t + 1) * P], Vs[:, b, hc], wT[:, u % 2, b * P:(b + 1) * P],
                                  start=t == 0 and b == 0, stop=False, skip_group_check=True)
                    ins.then_inc(pv_mm, 1)
                    if t == 3:
                        pe.wait_ge(em_done, h + 1)
                        mm1(banks[4][r, :], Vm[:, hc], wTm[:], start=False, stop=True, skip_group_check=True).then_inc(pvm_mm, 1)
                if step < 32:
                    gate_steps(1)
            for step in range(32 + 3):
                v = step
                if v < 32:
                    j, t = v // 4, v % 4
                    if v >= 2:
                        pe.wait_ge(s2_done, v - 1)
                    else:
                        pe.wait_ge(g_done, 32)
                    for i in range(2):
                        r = slice(HD * i, HD * i + HD)
                        keys = slice(0, META + P) if t == 0 else slice(META + (t - 1) * P, META + (t + 1) * P)
                        n = keys.stop - keys.start
                        if i:
                            gate_steps(1)
                            pe.wait_ge(z2_mm, 2 * v + 1)
                        mm1(banks[v % 2][:, 256 * (i + 1) - n:256 * (i + 1)], Qw[r, j, t * P:(t + 1) * P], Kw[r, j // 4, keys], start=True, stop=True).then_inc(z2_mm, 1)
                v = step - 2
                if 0 <= v < 32:
                    t = v % 4
                    pe.wait_ge(pn_done, v + 1)
                    if v >= 2:
                        pe.wait_ge(e2_done, 2 * (v - 1))
                    else:
                        pe.wait_ge(e_done, 31 + v)
                    for i in range(2):
                        o = 256 * i
                        bank = banks[2 + v % 2]
                        if t:
                            nc.tensor.transpose(bank[:, o:o + P], w3(v)[:, o:o + P], ident)
                        else:
                            nc.tensor.transpose(bank[0:META, o:o + P], w3(v)[:, o + 112:o + P], ident)
                        ins = nc.tensor.transpose(bank[:, o + P:o + 2 * P], w3(v)[:, o + P:o + 2 * P], ident)
                    ins.then_inc(x2_mm, 1)
                if step < 32:
                    gate_steps(1)
                v = step - 3
                if 0 <= v < 32:
                    j, t = v // 4, v % 4
                    pe.wait_ge(e2_done, 2 * v + 2)
                    if t == 0:
                        if j >= 2:
                            pe.wait_ge(o2_done, j - 1)
                        else:
                            pe.wait_ge(o1_done, 4)
                    vc = slice(HD * (j // 4), HD * (j // 4) + HD)
                    for i in range(2):
                        o = banks[4 + j % 2][HD * i:HD * i + HD, t * P:(t + 1) * P]
                        w = wT[:, v % 2, 256 * i:256 * i + 256]
                        if t:
                            mm1(o, Vw[:, t - 1, vc], w[:, 0:P], start=True, stop=False)
                        else:
                            mm1(o, Vwm[:, vc], w[0:META, 0:P], start=True, stop=False)
                        ins = mm1(o, Vw[:, t, vc], w[:, P:2 * P], start=False, stop=True)
                    ins.then_inc(pv2_mm, 1)
                if step < 32:
                    gate_steps(1)
            gate_steps(32)

            for half in range(2):
                n = N_BR + 3 * half
                pe.wait_ge(split_done, n + 1)
                for m in range(4 * half, 4 * half + 4):
                    if m >= 2:
                        pe.wait_ge(sb_ev, m - 1)
                    for k in range(4):
                        if m == 0:
                            pe.wait_ge(a_lo, k + 1)
                        c = k * 512 + (m % 4) * P
                        ins = three(banks[m % 2][:], w_hi[:, n % 2, c:c + P], w_lo[:, n % 2, c:c + P], asb_hi[:, k], asb_lo[:, k], k == 0, k == 3)
                        if k % 2:
                            ins.then_inc(eighths, 1)
                for m in range(4 * half, 4 * half + 4):
                    if m >= 2:
                        pe.wait_ge(sw_st, m - 1)
                    for k in range(KD):
                        if m == 0:
                            pe.wait_ge(a_lo, 4 + k + 1)
                        feature_steps(n + 1 + m % 4 // 2, m % 2, k, k + 1, banks[2 + m % 2])
            pe.wait_ge(f2_ev, 28)
            pe.wait_ge(o2_done, 8)
            pe.wait_ge(x_ready, 40)
            for s in range(4):
                n = N_OUT2 + s
                pe.wait_ge(split_done, n + 1)
                for t in range(TT):
                    o, c = out_bank(s, t), slice(t * P, (t + 1) * P)
                    for i in range(2):
                        mm1(o[:, i * P:(i + 1) * P], xT[:, 2 * s + i, c], ident, start=s % 2 == 0 and i == 0, stop=False, skip_group_check=True)
                    for k in range(KD):
                        if s == 0 and t == 0:
                            pe.wait_ge(mglo_done, k + 1)
                        w = slice(k * SC, (k + 1) * SC)
                        mm1(o, mg_hi[:, k, c], w_hi[:, n % 2, w], start=False, stop=False, skip_group_check=True)
                        mm1(o, mg_hi[:, k, c], w_lo[:, n % 2, w], start=False, stop=False, skip_group_check=True)
                        ins = mm1(o, mg_lo[:, k, c], w_hi[:, n % 2, w], start=False, stop=k == KD - 1, skip_group_check=True)
                        if k % 4 == 3:
                            ins.then_inc(eighths, 1)


INPUTS = ("x", "ffn1_norm", "ffn1_w_gate", "ffn1_w_up", "ffn1_w_down", "mix_norm", "w_in", "gm_ln_g", "gm_ln_b", "gm_w_s",
          "gm_b_s", "dn_conv_w", "dn_a_log", "dn_dt_bias", "dn_norm", "w_out", "ffn2_norm", "ffn2_w_gate", "ffn2_w_up",
          "ffn2_w_down", "final_norm", "meta_tokens_2", "norm_gain_2", "w_in_2", "w_branch_sb_2", "w_branch_swa_2",
          "w_out_2", "attn_sinks_2", "final_norm_gain_2")


def kernel(**inputs):
    import concourse.bacc as bacc
    from concourse.bass_utils import run_bass_kernel_spmd

    nc = bacc.Bacc("TRN2", target_bir_lowering=False, num_devices=1)
    arrays, aps = {}, {}
    given = {name: inputs[name] for name in INPUTS}
    given.update(constants())
    for name, value in given.items():
        value = np.ascontiguousarray(value)
        arrays[f"in_{name}_dram"] = value
        aps[name] = nc.dram_tensor(f"in_{name}_dram", value.shape, mybir.dt.from_np(value.dtype), kind="ExternalInput").ap()
    out = nc.dram_tensor("out_0_dram", (1, T, D), F32, kind="ExternalOutput").ap()
    program(nc, aps, out)
    result = run_bass_kernel_spmd(nc, [arrays], core_ids=[0])
    return result.results[0]["out_0_dram"]
```

```python
from contextlib import ExitStack

import numpy as np

import concourse.bass as bass
from concourse import mybir

P = 128
F32 = mybir.dt.float32
F32R = mybir.dt.float32r
ALU = mybir.AluOpType
ACT = mybir.ActivationFunctionType
AX_X = mybir.AxisListType.X

T = 512
D = 1024
KD = D // P
TT = T // P
FF = 2816
FP = FF // (2 * P)
SLAB = 2048
SC = SLAB // KD
META = 16
TM = META + T
CH = 64
NC = T // CH
H = 4
LEVELS = 6
GG = 8
HD = 64
NEG = -1e30

V_FFN1, V_MIX, V_FFN2, V_FIN1, V_N2, V_DN, V_CONV = 0, 8, 16, 24, 32, 40, 41
ROWS = V_CONV + 48
V_FG2 = ROWS

N_FFN1 = 0
N_MIX = N_FFN1 + 3 * FP
MIX_SLABS = (4, 5, 6, 7, 8, 9, 2, 3, 0, 1, 10, 11)
N_OUT1 = N_MIX + len(MIX_SLABS)
N_FFN2 = N_OUT1 + 4
N_P2 = N_FFN2 + 3 * FP
P2_SLABS = (0, 1, 2, 3, 4, 5, 10, 6, 7, 8, 9) + tuple(range(11, 25))
N_BR = N_P2 + len(P2_SLABS)
N_OUT2 = N_BR + 6
N_SLABS = N_OUT2 + 4


def constants():
    i, j = np.arange(P)[:, None], np.arange(P)[None, :]
    same = i // CH == j // CH
    f = lambda m: np.asarray(m, np.float32)
    ones = np.ones((P, P))
    base = [np.eye(P), ones, np.full((P, 8), 1e-6)]
    neg = lambda keep: np.where(keep, 0.0, NEG)
    mix = [same & (i <= j), same, (i // CH == 0) * ones, (i // CH == 1) * ones, neg(same & (i <= j)), neg(same & (j < i))]
    mix += [(i // (2 << s) == j // (2 << s)) & ((i >> s) % 2 == 1) & ((j >> s) % 2 == 0) for s in range(LEVELS)]
    prev = neg(j > i)
    own = neg(j <= i)
    att = [np.ones((P, 384)), j < i, neg(j < i), prev, own, (np.arange(T)[None, :] % META != META - 1) * np.ones((P, T))]
    half = HD // 2
    rot = np.zeros((P, P))
    for m in range(P):
        if m % HD < half:
            rot[m + half, m] = -1.0
        else:
            rot[m - half, m] = 1.0
    rope = [rot]
    for g in range(2):
        dup = np.zeros((P, P))
        for m in range(P):
            dup[g * HD + m % HD, m] = 1.0
        rope += [dup, dup @ rot]
    inv = np.float32(10000.0) ** (-np.arange(half, dtype=np.float32) / np.float32(half))
    ang = np.tile(inv, 4)[:, None] * np.arange(TM, dtype=np.float32)[None, :]
    rope += [np.cos(ang), np.sin(ang)]
    cat = lambda parts: np.ascontiguousarray(np.concatenate([f(m) for m in parts], axis=1))
    return {"c_base": cat(base), "c_mix": cat(mix), "c_att": cat(att), "c_rope": cat(rope)}


def program(nc, a, out):
    with ExitStack() as ctx:
        sem = lambda name: ctx.enter_context(nc.semaphore(name))
        cursor = [(nc.sbuf_base + 31) // 32 * 32]

        def sb(name, shape, dt=F32):
            t = nc.alloc_sbuf_tensor_at(name, shape, dt, offset=cursor[0])
            cursor[0] += (4 * int(np.prod(shape[1:])) + 31) // 32 * 32
            return t

        raw = sb("raw", [P, 2, SLAB])
        w_hi = sb("w_hi", [P, 2, SLAB], F32R)
        w_lo = sb("w_lo", [P, 2, SLAB], F32R)
        xT = sb("xT", [P, KD, T])
        xn_hi = sb("xn_hi", [P, KD, TM], F32R)
        xn_lo = sb("xn_lo", [P, KD, TM], F32R)
        base_c = sb("base_c", [P, 2 * P + 8])
        ident, ones, epsc = base_c[:, 0:P], base_c[:, P:2 * P], base_c[:, 2 * P:2 * P + 1]
        rows_at = cursor[0]
        rows = sb("rows", [P, P])
        cols = sb("cols", [P, P])
        rstd = sb("rstd", [P, T])
        hvec = sb("hvec", [P, 2, 4])
        sinks = sb("sinks", [P, 16])
        tiny = sb("tiny", [P, 48])
        rtok = sb("rtok", [P, TT])
        sq = sb("sq", [P, 2, T])
        smalls_at = cursor[0]
        sumsq = sb("sumsq", [P, TM])
        gs = sb("gs", [P, 2, T])
        hf = sb("hf", [P, 2, T])
        region = cursor[0]

        sums = sumsq[:, 0:T]
        sums2 = gs[:, 0]
        factor, factor_t = sumsq, sumsq[:, META:TM]

        h_hi = sb("h_hi", [P, 2 * FP, T], F32R)
        h_lo = sb("h_lo", [P, 2 * FP, T], F32R)
        assert cursor[0] <= nc.sbuf_usable_end
        cursor[0] = region
        xload = sb("xload", [P, TT, D])
        meta_in = sb("meta_in", [META, D])
        meta_sq = sb("meta_sq", [META, D])
        meta_f = sb("meta_f", [P, KD, META])

        cursor[0] = region
        mixm = sb("mixm", [P, 12, P])
        cumT, same, half0, half1 = (mixm[:, n] for n in range(4))
        neg_incl, neg_strict = mixm[:, 4], mixm[:, 5]
        here, cursor[0] = cursor[0], rows_at
        wba = sb("wba", [P, KD, 8])
        cursor[0] = here
        qkv = sb("qkv", [P, 12, T])
        cursor[0] -= 4 * T * 4
        ya = sb("ya", [P, 4, T])
        rw_at = cursor[0]
        rw = sb("rw", [P, 2, T + 8])
        cursor[0] = rw_at
        lnc = sb("lnc", [P, 2, T])
        cursor[0] = rw_at
        vnew = sb("vnew", [P, T])
        cursor[0] = rw_at + 2 * 4 * (T + 8)
        vb = sb("vb", [P, H, T])
        kb_at = cursor[0]
        kb = sb("kb", [P, H, T])
        kd = sb("kd", [P, H, T])
        Z = sb("Z", [P, H, T])
        tmp_at = cursor[0]
        Tm = sb("Tm", [P, 2, T])
        Mm = sb("Mm", [P, 2, T])
        Pp = sb("Pp", [P, 2, T])
        cursor[0] = tmp_at
        wsraw = sb("wsraw", [P, GG, P])
        cursor[0] = tmp_at
        zT = sb("zT", [P, 4, T])
        S = sb("S", [P, 2, T])
        vtok_at = cursor[0]
        vtok = sb("vtok", [P, TT, T])
        wsT_at = cursor[0]
        wsT = sb("wsT", [P, GG, P])
        bs = sb("bs", [P, 4, P])
        wba_w = KD * 8 + P - 8
        cursor[0] = vtok_at
        wba_hi = sb("wba_hi", [P, wba_w], F32R)
        wba_lo = sb("wba_lo", [P, wba_w], F32R)
        baf = sb("baf", [8, T])
        cursor[0] = wsT_at + 4 * (GG * P + 4 * P)
        assert cursor[0] <= nc.sbuf_usable_end
        cursor[0] = vtok_at
        ya_hi = sb("ya_hi", [P, 4, T], F32R)
        cursor[0] = rw_at + 4 * T
        ya_lo0 = sb("ya_lo0", [P, T], F32R)
        cursor[0] = wsT_at
        ya_lo1 = sb("ya_lo1", [P, 3, T], F32R)
        cursor[0] = kb_at
        yb_hi = sb("yb_hi", [P, 4, T], F32R)
        yb_lo = sb("yb_lo", [P, 4, T], F32R)
        yh = lambda k: ya_hi[:, k] if k < 4 else yb_hi[:, k - 4]
        yl = lambda k: ya_lo0[:] if k < 1 else ya_lo1[:, k - 1] if k < 4 else yb_lo[:, k - 4]
        cursor[0] = smalls_at
        sm = sb("sm", [P, 14, 16])
        s_e, s_beta, s_a, s_t, s_g, s_ea = (sm[:, n] for n in range(6))
        s_c = sm[:, 6:10]
        s_ngc, s_kd, s_eg, s_be = (sm[:, n] for n in range(10, 14))
        egl = sb("egl", [P, 2, 16])
        st6 = sb("st6", [P, 4, 6])
        mv = sb("mv", [P, 4, 2])
        rln = sb("rln", [P, 4])

        cursor[0] = region
        Qs = sb("Qs", [P, 4, T])
        Ks = sb("Ks", [P, 4, TM])
        Vs = sb("Vs", [P, TT, T])
        Vm = sb("Vm", [META, T])
        zs = sb("zs", [P, 12, T])
        qw_at = cursor[0]
        Qw = sb("Qw", [P, 8, T])
        Kw = sb("Kw", [P, 2, TM])
        Vw = sb("Vw", [P, TT, P])
        Vwm = sb("Vwm", [META, P])
        attm = sb("attm", [P, 1408])
        scan_mask, neg_diag, win_mask, meta_mask = attm[:, 0:512], attm[:, 512:640], attm[:, 640:896], attm[:, 896:1408]
        kblk = sb("kblk", [P, 4, 2 * META])
        work_at = cursor[0]
        ropec = sb("ropec", [P, 5 * P + 2 * TM])
        rot_q = ropec[:, 0:P]
        dup_k = [ropec[:, (1 + 2 * g) * P:(2 + 2 * g) * P] for g in range(2)]
        rot_k = [ropec[:, (2 + 2 * g) * P:(3 + 2 * g) * P] for g in range(2)]
        cosT, sinT = ropec[:, 5 * P:5 * P + TM], ropec[:, 5 * P + TM:]
        kraw = sb("kraw", [P, TM])
        cursor[0] = work_at
        wT = sb("wT", [P, 2, T])
        argm = sb("argm", [P, T])
        ctok = sb("ctok", [P, 32])
        wm = sb("wm", [P, 2, HD])
        wTm = sb("wTm", [META, T])
        assert cursor[0] <= nc.sbuf_usable_end
        cursor[0] = region
        g_lowt = sb("g_lowt", [P, 12, T])
        ost_at = region
        cursor[0] = qw_at
        g_hight = sb("g_hight", [P, 4, T])
        asb_hi = sb("asb_hi", [P, 4, T], F32R)
        asb_lo = sb("asb_lo", [P, 4, T], F32R)
        mg_lo = sb("mg_lo", [P, KD, T], F32R)
        assert cursor[0] <= nc.sbuf_usable_end
        cursor[0] = qw_at - 8 * T * 4
        mg_hi = sb("mg_hi", [P, KD, T], F32R)
        cursor[0] = ost_at
        ost = sb("ost", [P, TT, D])
        gain_row = sb("gain_row", [P, D])
        gt = lambda t: g_lowt[:, t] if t < 12 else g_hight[:, t - 12]

        banks = [ctx.enter_context(nc.psum_tensor(f"bank{i}", [P, 512], F32)) for i in range(8)]

        def quarters(ap):
            return ap.rearrange("p (a b) -> p a b", a=4)

        def over4(ap):
            return ap.unsqueeze(1).to_broadcast([P, 4, P])

        def per_block(ap):
            return ap.unsqueeze(2).to_broadcast([P, 4, P])

        x_loaded = [sem(f"x_loaded{t}") for t in range(TT)]
        consts_loaded = sem("consts_loaded")
        heads_loaded = sem("heads_loaded")
        vectors_loaded = sem("vectors_loaded")
        first_gain_loaded = sem("first_gain_loaded")
        slab_loaded = [sem("slab_loaded0"), sem("slab_loaded1")]
        slab_high = sem("slab_high")
        slab_split = sem("slab_split")
        eighths_used = sem("eighths_used")
        mix_loaded = sem("mix_loaded")
        ln_vecs_loaded = sem("ln_vecs_loaded")
        att_loaded = sem("att_loaded")
        gain_row_loaded = sem("gain_row_loaded")
        out_stored = sem("out_stored")
        meta_loaded = sem("meta_loaded")
        x_turned = sem("x_turned")
        x_ready = sem("x_ready")
        cols_ready = sem("cols_ready")
        xn_high = sem("xn_high")
        xn_split = sem("xn_split")
        sq_done = sem("sq_done")
        sq_added = sem("sq_added")
        sums_mm = sem("sums_mm")
        log_done = sem("log_done")
        rstd_done = sem("rstd_done")
        rtok_mm = sem("rtok_mm")
        rtok_done = sem("rtok_done")
        two_norms_dve = sem("two_norms_dve")
        two_norms_act = sem("two_norms_act")
        factor_done = sem("factor_done")
        meta_act = sem("meta_act")
        meta_dve = sem("meta_dve")
        meta_turned = sem("meta_turned")
        gate_out = sem("gate_out")
        up_out = sem("up_out")
        gate_silu = sem("gate_silu")
        inner_done = sem("inner_done")
        inner_high = sem("inner_high")
        inner_split = sem("inner_split")
        conv_in = sem("conv_in")
        conv_step = sem("conv_step")
        conv_done = sem("conv_done")
        qkv_done = sem("qkv_done")
        ba_split = sem("ba_split")
        ba_mm = sem("ba_mm")
        decay_act = sem("decay_act")
        decay_dve = sem("decay_dve")
        cum_mm = sem("cum_mm")
        len_sq = sem("len_sq")
        len_mm = sem("len_mm")
        len_root = sem("len_root")
        len_done = sem("len_done")
        gate_w_mm = sem("gate_w_mm")
        gate_w_done = sem("gate_w_done")
        gate_v_out = sem("gate_v_out")
        gate_v_gelu = sem("gate_v_gelu")
        ln_stats = sem("ln_stats")
        ln_root = sem("ln_root")
        ln_applied = sem("ln_applied")
        gate_mm = sem("gate_mm")
        gate_mixed = sem("gate_mixed")
        g_rows_mm = sem("g_rows_mm")
        g_rows = sem("g_rows")
        g_rows_exp = sem("g_rows_exp")
        decay_arg = sem("decay_arg")
        decay_exp = sem("decay_exp")
        k_turned = sem("k_turned")
        v_turned = sem("v_turned")
        kq_mm = sem("kq_mm")
        k_tok_done = sem("k_tok_done")
        v_beta = sem("v_beta")
        qk_decayed = sem("qk_decayed")
        q_decayed = sem("q_decayed")
        l_done = sem("l_done")
        m_done = sem("m_done")
        t_init = sem("t_init")
        m_turned = sem("m_turned")
        mz_mm = sem("mz_mm")
        mz_out = sem("mz_out")
        zt_mm = sem("zt_mm")
        z_done = sem("z_done")
        t_done = sem("t_done")
        w_mm = sem("w_mm")
        neg_w_done = sem("neg_w_done")
        vnew_mm = sem("vnew_mm")
        vnew_done = sem("vnew_done")
        state_mm = sem("state_mm")
        state_done = sem("state_done")
        chunk_out_mm = sem("chunk_out_mm")
        uz_out = sem("uz_out")
        uz_act = sem("uz_act")
        ya_done = sem("ya_done")
        o_out = sem("o_out")
        o_sq = sem("o_sq")
        o_sq_mm = sem("o_sq_mm")
        o_root = sem("o_root")
        o_normed = sem("o_normed")
        yb_done = sem("yb_done")
        y_high = sem("y_high")
        y_split = sem("y_split")
        qk_out = sem("qk_out")
        v_out = sem("v_out")
        vw_turned = sem("vw_turned")
        k_rot_mm = sem("k_rot_mm")
        k_rot_step = sem("k_rot_step")
        k_rot_done = sem("k_rot_done")
        q_rot_mm = sem("q_rot_mm")
        q_rot_step = sem("q_rot_step")
        q_rot_done = sem("q_rot_done")
        kblk_done = sem("kblk_done")
        gates_out = sem("gates_out")
        zm_mm = sem("zm_mm")
        zm_act = sem("zm_act")
        zm_dve = sem("zm_dve")
        z_mm = sem("z_mm")
        sp_act = sem("sp_act")
        arg_step = sem("arg_step")
        arg_done = sem("arg_done")
        weights_done = sem("weights_done")
        weights_mm = sem("weights_mm")
        weights_out = sem("weights_out")
        pv_mm = sem("pv_mm")
        argm_done = sem("argm_done")
        weightsm_done = sem("weightsm_done")
        weightsm_mm = sem("weightsm_mm")
        weightsm_out = sem("weightsm_out")
        pvm_mm = sem("pvm_mm")
        sb_out = sem("sb_out")
        zs_silu = sem("zs_silu")
        sb_gated = sem("sb_gated")
        z2_mm = sem("z2_mm")
        score_step = sem("score_step")
        score_done = sem("score_done")
        exp2_done = sem("exp2_done")
        norm2_step = sem("norm2_step")
        weights2_done = sem("weights2_done")
        weights2_mm = sem("weights2_mm")
        weights2_out = sem("weights2_out")
        pv2_mm = sem("pv2_mm")
        sw_gated = sem("sw_gated")
        merge_tanh = sem("merge_tanh")
        br_high = sem("br_high")
        br_split = sem("br_split")
        sb_merged = sem("sb_merged")
        sw_merged = sem("sw_merged")
        merged = sem("merged")
        merged_high = sem("merged_high")
        merged_split = sem("merged_split")
        out_sq = sem("out_sq")
        out_sum = sem("out_sum")
        out_root = sem("out_root")
        out_ready = sem("out_ready")

        def out_bank(s, t):
            return banks[(4 if s < 2 else 0) + t][:, SC * (s % 2):SC * (s % 2) + SC]

        def gain(q, d):
            at = (V_FFN1, V_MIX, V_FFN2, V_FG2)[q] + d
            return cols[:, at:at + 1]
        qT = lambda h: qkv[:, h]
        kT = lambda h: qkv[:, 4 + h]
        vT = lambda h: qkv[:, 8 + h]
        atT, Lm = kT, vT
        vwf = gs[:].rearrange("p a b -> p (a b)")[:, 0:TM]
        unit_buf = lambda u: (gs[:, 0], gs[:, 1], hf[:, 0])[u % 3]

        block = ctx.enter_context(nc.Block())

        @block.sync
        def _(sp):
            def load(n, src, slot=None):
                slot = n % 2 if slot is None else slot
                if not isinstance(n, int) or n >= 2:
                    sp.wait_ge(slab_split, n - 1)
                sp.dma_start(raw[:, slot, :].rearrange("p (k c) -> p k c", k=src.shape[1]), src).then_inc(slab_loaded[slot], 16)

            def ffn(n0, wg, wu, wd):
                g = wg.rearrange("(k p) f -> p k f", p=P)
                u = wu.rearrange("(k p) f -> p k f", p=P)
                d = wd.rearrange("(k p) c -> p k c", p=P)
                if n0:
                    load(n0, g[:, :, 0:SC])
                load(n0 + 1, u[:, :, 0:SC])
                with sp.Fori(1, FP) as i:
                    load(n0 + 2 * i, g[:, :, bass.ds(i * SC, SC)], n0 % 2)
                    load(n0 + 2 * i + 1, u[:, :, bass.ds(i * SC, SC)], (n0 + 1) % 2)
                n1 = n0 + 2 * FP
                with sp.Fori(0, FP // 2) as j:
                    load(n1 + 2 * j, d[:, bass.ds(j * 4, 2), :], n1 % 2)
                    load(n1 + 2 * j + 1, d[:, bass.ds(j * 4 + 2, 2), :], (n1 + 1) % 2)
                load(n1 + FP - 1, d[:, 2 * FP - 2:2 * FP, :])

            def columns(n0, w, slabs):
                v = w.rearrange("(k p) c -> p k c", p=P)
                for i, s in enumerate(slabs):
                    load(n0 + i, v[:, :, s * SC:(s + 1) * SC])

            xv = a["x"].rearrange("b (t p) d -> (b p) t d", p=P)
            wg1 = a["ffn1_w_gate"][0].rearrange("(k p) f -> p k f", p=P)
            load(0, wg1[:, :, 0:SC])
            sp.dma_start(rows[V_FFN1:V_FFN1 + 8, :], a["ffn1_norm"].rearrange("b (k p) -> (b k) p", p=P)).then_inc(first_gain_loaded, 16)
            sp.dma_start(base_c[:], a["c_base"]).then_inc(consts_loaded, 16)
            for t in range(TT):
                sp.dma_start(xload[:, t, :], xv[:, t, :]).then_inc(x_loaded[t], 16)
            ffn(N_FFN1, a["ffn1_w_gate"][0], a["ffn1_w_up"][0], a["ffn1_w_down"][0])
            columns(N_MIX, a["w_in"][0], MIX_SLABS[0:2])
            sp.wait_ge(eighths_used, 8 * N_MIX)
            sp.dma_start(mixm[:].rearrange("p a b -> p (a b)"), a["c_mix"]).then_inc(mix_loaded, 16)
            with nc.allow_non_contiguous_dma(reason="eight columns of a row"):
                sp.dma_start(wba[:], a["w_in"][0].rearrange("(k p) c -> p k c", p=P)[:, :, 3072:3080]).then_inc(mix_loaded, 16)
            sp.dma_start(wsraw[:], a["gm_w_s"][0].rearrange("g i j -> i g j")).then_inc(mix_loaded, 16)
            bsv = a["gm_b_s"][0].rearrange("(m two) i -> two m i", two=2)
            for half in range(2):
                sp.dma_start(bs[64 * half:64 * half + 64], bsv[half].partition_broadcast(64)).then_inc(mix_loaded, 16)
            columns(N_MIX + 2, a["w_in"][0], MIX_SLABS[2:10])
            sp.wait_ge(conv_done, 12)
            sp.dma_start(lnc[:, 0, :], a["gm_ln_g"][0].partition_broadcast(P)).then_inc(ln_vecs_loaded, 16)
            sp.dma_start(lnc[:, 1, :], a["gm_ln_b"][0].partition_broadcast(P)).then_inc(ln_vecs_loaded, 16)
            columns(N_MIX + 10, a["w_in"][0], MIX_SLABS[10:])
            columns(N_OUT1, a["w_out"][0], range(4))
            ffn(N_FFN2, a["ffn2_w_gate"][0], a["ffn2_w_up"][0], a["ffn2_w_down"][0])
            columns(N_P2, a["w_in_2"][0], P2_SLABS[0:2])
            sp.wait_ge(eighths_used, 8 * N_P2)
            sp.dma_start(attm[:], a["c_att"]).then_inc(att_loaded, 16)
            sp.dma_start(ropec[:], a["c_rope"]).then_inc(att_loaded, 16)
            columns(N_P2 + 2, a["w_in_2"][0], P2_SLABS[2:])
            wsb = a["w_branch_sb_2"][0].rearrange("(k p) c -> p k c", p=P)
            for i in range(2):
                load(N_BR + 3 * i, wsb[:, :, i * 512:(i + 1) * 512])
                columns(N_BR + 3 * i + 1, a["w_branch_swa_2"][0], (2 * i, 2 * i + 1))
            columns(N_OUT2, a["w_out_2"][0], range(4))
            ov = out[0].rearrange("(t p) d -> t p d", p=P)
            sp.wait_ge(merged_split, 8)
            sp.dma_start(gain_row[:], a["final_norm_gain_2"].partition_broadcast(P)).then_inc(gain_row_loaded, 16)
            for t in range(TT):
                sp.wait_ge(out_ready, 2 * t + 2)
                sp.dma_start(ov[t], ost[:, t]).then_inc(out_stored, 16)
            sp.wait_ge(out_stored, 16 * TT)

        @block.gpsimd
        def _(pool):
            parts = pool.alloc_register("high_parts")

            def split(n, slot, loads):
                pool.wait_ge(slab_loaded[slot], 16 * loads)
                if not isinstance(n, int) or n >= 2:
                    pool.wait_ge(eighths_used, 8 * (n - 1))
                done = n + 1
                if not isinstance(n, int):
                    pool.reg_add(parts, parts, 1)
                    done = parts
                nc.gpsimd.tensor_scalar(w_hi[:, slot], raw[:, slot], 1.0, 0.0, ALU.mult, ALU.add).then_inc(slab_high, 1)
                pool.wait_ge(slab_high, done)
                nc.gpsimd.tensor_tensor(w_lo[:, slot], raw[:, slot], w_hi[:, slot].bitcast(F32), ALU.subtract).then_inc(slab_split, 1)
            pool.wait_ge(slab_split, 1)
            split(1, 1, 1)
            def slabs(n0, n1):
                pool.reg_mov(parts, n0)
                with pool.Fori(n0 // 2, n1 // 2) as i:
                    split(2 * i, 0, i + 1)
                    split(2 * i + 1, 1, i + 1)
            n = N_MIX + 7
            assert N_SLABS % 2 and n % 2 == 0
            slabs(2, n)
            split(n, 0, n // 2 + 1)
            for h in range(H):
                e = (sq, hf)[h % 2]
                pool.wait_ge(g_rows, h + 1)
                if h >= 2:
                    pool.wait_ge(qk_decayed, h - 1)
                    pool.wait_ge(l_done, h - 1)
                nc.gpsimd.tensor_tensor(quarters(e[:, 0]), quarters(gs[:, 0]), over4(neg_incl), ALU.add).then_inc(decay_arg, 1)
                nc.gpsimd.tensor_tensor(quarters(e[:, 1]), over4(neg_strict), quarters(gs[:, 0]), ALU.subtract).then_inc(decay_arg, 1)
                if h == 1:
                    split(n + 1, 1, n // 2 + 1)
            split(n + 2, 0, n // 2 + 2)
            pool.wait_ge(ln_root, 2)
            pool.wait_ge(ln_stats, 8)
            pool.wait_ge(ln_vecs_loaded, 32)
            for t in range(TT):
                nc.gpsimd.tensor_scalar(vtok[:, t], vtok[:, t], mv[:, t, 0:1], rln[:, t:t + 1], ALU.subtract, ALU.mult).then_inc(ln_applied, 1)
            for step, op in ((0, ALU.mult), (1, ALU.add)):
                for t in range(TT):
                    pool.wait_ge(ln_applied, 4 * step + t + 1)
                    nc.gpsimd.tensor_tensor(vtok[:, t], vtok[:, t], lnc[:, step], op).then_inc(ln_applied, 1)
            split(n + 3, 1, n // 2 + 2)
            slabs(n + 4, N_SLABS - 1)
            split(N_SLABS - 1, 0, N_SLABS // 2 + 1)

        @block.scalar
        def _(act):
            A = nc.scalar.activation

            def high(q, d):
                act.wait_ge(x_ready, 8 * q + d + 1)
                nc.scalar.mul(xn_hi[:, d, META:TM], xT[:, d], gain(q, d)).then_inc(xn_high, 1)

            def square(q, d):
                if 8 * q + d >= 2:
                    act.wait_ge(sq_added, 8 * q + d - 1)
                A(sq[:, d % 2], xT[:, d], ACT.Square).then_inc(sq_done, 1)

            def root(q):
                act.preload_act_table_set("natural_log_exp_and_others")
                act.wait_ge(sums_mm, q + 1)
                A(rstd[:], banks[4][:], ACT.Ln, bias=epsc, scale=1.0 / D).then_inc(log_done, 1)
                act.wait_ge(log_done, q + 1)
                A(rstd[:], rstd[:], ACT.Exp, scale=-0.5).then_inc(rstd_done, 1)

            def norm(q):
                for d in range(KD):
                    high(q, d)
                    square(q, d)
                root(q)

            def ffn(base):
                def pair(i, guard):
                    for f in range(2):
                        act.wait_ge(gate_out, base + 2 * i + f + 1)
                        A(gs[:, f], gs[:, f], ACT.Silu).then_inc(gate_silu, 1)
                    for f in range(2):
                        act.wait_ge(inner_done, base + 2 * i + f + 1)
                        dst = h_hi[:, bass.ds(2 * i + f, 1), :] if guard else h_hi[:, f:f + 1, :]
                        nc.scalar.copy(dst.rearrange("p a t -> p (a t)"), hf[:, f]).then_inc(inner_high, 1)
                pair(0, False)
                if base == 0:
                    act.wait_ge(meta_dve, 2)
                    nc.scalar.copy(xn_hi[:, :, 0:META], meta_f[:]).then_inc(meta_act, 1)
                with act.Fori(1, FP) as i:
                    pair(i, True)

            act.preload_act_table_set("natural_log_exp_and_others")
            act.wait_ge(slab_loaded[0], 16)
            nc.scalar.copy(w_hi[:, 0], raw[:, 0]).then_inc(slab_high, 1)
            for name, r, n in (("mix_norm", V_MIX, 8), ("ffn2_norm", V_FFN2, 8), ("norm_gain_2", V_N2, 8), ("dn_norm", V_DN, 1)):
                act.dma_start(rows[r:r + n, :], a[name].rearrange("b (k p) -> (b k) p", p=P)).then_inc(vectors_loaded, 16)
            act.dma_start(rows[V_FIN1:V_FIN1 + 8, :], a["final_norm"].rearrange("(k p) -> k p", p=P)).then_inc(vectors_loaded, 16)
            act.dma_start(rows[V_CONV:V_CONV + 48, :], a["dn_conv_w"][0].rearrange("j (c p) -> (j c) p", p=P)).then_inc(vectors_loaded, 16)
            act.dma_start(meta_in[:], a["meta_tokens_2"]).then_inc(meta_loaded, 16)
            act.dma_start(hvec[:, 0, :], a["dn_dt_bias"][0].partition_broadcast(P)).then_inc(heads_loaded, 16)
            act.dma_start(hvec[:, 1, :], a["dn_a_log"][0].partition_broadcast(P)).then_inc(heads_loaded, 16)
            act.dma_start(sinks[:], a["attn_sinks_2"][0].partition_broadcast(P)).then_inc(heads_loaded, 16)
            act.wait_ge(cols_ready, 1)
            for d in range(KD):
                high(0, d)
            for d in range(KD):
                square(0, d)
            root(0)
            act.wait_ge(meta_loaded, 16)
            A(meta_sq[:], meta_in[:], ACT.Square, accum_out=tiny[0:META, 0:1]).then_inc(meta_act, 1)
            act.wait_ge(meta_act, 1)
            A(tiny[0:META, 1:2], tiny[0:META, 0:1], ACT.Ln, bias=epsc[0:META], scale=1.0 / D).then_inc(meta_act, 1)
            act.wait_ge(meta_act, 2)
            A(tiny[0:META, 2:3], tiny[0:META, 1:2], ACT.Exp, scale=-0.5).then_inc(meta_act, 1)
            act.wait_ge(heads_loaded, 48)
            ffn(0)

            norm(1)
            act.wait_ge(mix_loaded, 80)
            nc.scalar.copy(wba_hi[:, 0:KD * 8], wba[:].rearrange("p k c -> p (k c)")).then_inc(ba_split, 1)
            act.preload_act_table(ACT.Silu)
            for j in range(12):
                if j == 8:
                    act.preload_act_table_set("natural_log_exp_and_others")
                    hp = lambda ap: ap.rearrange("p (h t) -> p h t", h=4)
                    ba = banks[5][:, 0:32].rearrange("p (t c) -> p c t", c=8)
                    act.wait_ge(ba_mm, 2)
                    A(hp(s_e), ba[:, 0:4], ACT.Exp, scale=-1.0).then_inc(decay_act, 1)
                    act.wait_ge(decay_dve, 2)
                    A(s_t, s_a, ACT.Abs).then_inc(decay_act, 1)
                    act.wait_ge(decay_act, 2)
                    A(s_t, s_t, ACT.Exp, scale=-1.0).then_inc(decay_act, 1)
                    act.wait_ge(decay_act, 3)
                    A(s_t, s_t, ACT.Ln, bias=1.0).then_inc(decay_act, 1)
                    A(s_ea[:, 0:4], hvec[:, 1], ACT.Exp).then_inc(decay_act, 1)
                    act.wait_ge(decay_dve, 7)
                    A(s_eg, s_c[:, 0], ACT.Exp).then_inc(decay_act, 1)
                    act.wait_ge(decay_dve, 9)
                    A(s_kd, s_kd, ACT.Exp).then_inc(decay_act, 1)
                    A(egl[:], s_c[:, 2:4], ACT.Exp).then_inc(decay_act, 1)
                    def l2_root(i):
                        act.wait_ge(len_mm, i + 1)
                        if i >= 2:
                            act.wait_ge(len_done, i - 1)
                        A(gs[:, i % 2], banks[4 + i % 2][:], ACT.Ln, bias=epsc).then_inc(len_root, 1)
                        act.wait_ge(len_root, 2 * i + 1)
                        A(gs[:, i % 2], gs[:, i % 2], ACT.Exp, scale=-0.5).then_inc(len_root, 1)
                    for i in range(9):
                        if i < 8:
                            act.wait_ge(qkv_done, i + 1)
                            if i >= 2:
                                act.wait_ge(len_mm, i - 1)
                            A(sq[:, i % 2], qkv[:, i], ACT.Square).then_inc(len_sq, 1)
                        if i:
                            l2_root(i - 1)
                    act.preload_act_table(ACT.Silu)
                act.wait_ge(conv_done, j + 1)
                A(qkv[:, j], hf[:, j % 2], ACT.Silu).then_inc(qkv_done, 1)
            act.preload_act_table_set("natural_log_exp_and_others")

            def gate_ev(j):
                t = j % 4
                act.wait_ge(eighths_used, 8 * (N_MIX + 6) + 4 * (j // 2) + 4)
                nc.scalar.mul(vtok[:, t, (j // 4) * SC:(j // 4 + 1) * SC], banks[(7, 0, 1, 7)[j // 2]][:, (j % 2) * SC:(j % 2 + 1) * SC],
                              rtok[:, t:t + 1]).then_inc(gate_v_out, 1)
            for h in range(H):
                act.wait_ge(g_rows_mm, h + 1)
                if h:
                    act.wait_ge(decay_arg, 2 * h)
                    act.wait_ge(g_rows_exp, h)
                else:
                    act.wait_ge(len_done, 8)
                nc.scalar.copy(gs[:, 0], banks[2][:]).then_inc(g_rows, 1)
                act.wait_ge(g_rows, h + 1)
                if h:
                    act.wait_ge(q_decayed, h)
                A(gs[:, 1], gs[:, 0], ACT.Exp).then_inc(g_rows_exp, 1)
                for part, bias in ((0, s_ngc), (1, s_c[:, 0])):
                    act.wait_ge(decay_arg, 2 * h + part + 1)
                    for p in range(4):
                        e = (sq, hf)[h % 2][:, part, p * P:(p + 1) * P]
                        A(e, e, ACT.Exp,
                          bias=bias[:, 4 * h + p:4 * h + p + 1]).then_inc(decay_exp, 1)
                for j in ((0, 1), (2, 3), (), (4, 5, 6, 7))[h]:
                    gate_ev(j)
            for g in range(2):
                if g:
                    act.wait_ge(ln_stats, 8)
                    A(rln[:], mv[:, :, 1], ACT.Ln, bias=epsc).then_inc(ln_root, 1)
                    act.wait_ge(ln_root, 1)
                    A(rln[:], rln[:], ACT.Exp, scale=-0.5).then_inc(ln_root, 1)
                for level in range(1, LEVELS):
                    for hh in range(2):
                        n = (g * (LEVELS - 1) + level - 1) * 2 + hh
                        act.wait_ge(mz_mm, n + 1)
                        if n >= 2:
                            act.wait_ge(zt_mm, n - 1)
                        nc.scalar.copy(Pp[:, hh], banks[hh][:]).then_inc(mz_out, 1)
                    if g == 0 and level == 1:
                        act.wait_ge(gate_v_out, 8)
                        for t in range(TT):
                            A(vtok[:, t], vtok[:, t], ACT.Gelu_apprx_tanh).then_inc(gate_v_gelu, 1)
                        act.preload_act_table_set("natural_log_exp_and_others")
            for h in range(H):
                act.wait_ge(w_mm, h + 1)
                nc.scalar.mul(kb[:, h], banks[6 + h % 2][:], -1.0).then_inc(neg_w_done, 1)
            for c in range(NC):
                if c >= 4:
                    act.wait_ge(ya_done, 4)
                    nc.scalar.copy(yh(c - 4), ya[:, c - 4]).then_inc(y_high, 1)
                act.wait_ge(uz_out, c + 1)
                if c < 4:
                    A(gs[:, c % 2], gs[:, c % 2], ACT.Gelu_apprx_tanh).then_inc(uz_act, 1)
                else:
                    A(zT[:, c - 4], zT[:, c - 4], ACT.Silu).then_inc(uz_act, 1)
            act.preload_act_table_set("natural_log_exp_and_others")
            for h in range(H + 2):
                if h < H:
                    act.wait_ge(o_out, h + 1)
                    if h >= 2:
                        act.wait_ge(o_sq_mm, h - 1)
                    A(sq[:, h % 2], vb[:, h], ACT.Square).then_inc(o_sq, 1)
                e = h - 1
                if 0 <= e < H:
                    act.wait_ge(o_sq_mm, e + 1)
                    if e >= 2:
                        act.wait_ge(o_normed, e - 1)
                    A(gs[:, e % 2], banks[4 + e % 2][:], ACT.Ln, bias=epsc, scale=1.0 / P).then_inc(o_root, 1)
                    act.wait_ge(o_root, 2 * e + 1)
                    A(gs[:, e % 2], gs[:, e % 2], ACT.Exp, scale=-0.5).then_inc(o_root, 1)
                e = h - 2
                if e >= 0:
                    act.wait_ge(yb_done, e + 1)
                    nc.scalar.copy(yh(4 + e), vb[:, e]).then_inc(y_high, 1)

            norm(2)
            ffn(2 * FP)

            for d in range(KD):
                high(3, d)
            for d in range(KD):
                act.wait_ge(sq_added, 24 + 2 * d)
                A(sq[:, 0], xT[:, d], ACT.Square).then_inc(sq_done, 1)
                A(sq[:, 1], xT[:, d], ACT.Square, scale=cols[:, V_FIN1 + d:V_FIN1 + d + 1]).then_inc(sq_done, 1)
            root(3)
            act.wait_ge(two_norms_dve, 2)
            A(gs[:, 1], gs[:, 1], ACT.Ln, bias=epsc, scale=1.0 / D).then_inc(two_norms_act, 1)
            act.wait_ge(two_norms_act, 1)
            A(gs[:, 1], gs[:, 1], ACT.Exp, scale=-0.5).then_inc(two_norms_act, 1)
            act.wait_ge(rtok_done, 2)
            for s in range(2):
                for t in range(TT):
                    if t % 2 == 0:
                        act.wait_ge(eighths_used, 8 * (N_P2 + 4 + s) + 2 * t + 4)
                    nc.scalar.mul(Vs[:, t, s * SC:(s + 1) * SC], banks[4 + t // 2][:, SC * (t % 2):SC * (t % 2) + SC], rtok[:, t:t + 1]).then_inc(v_out, 1)
                nc.scalar.copy(Vm[:, s * SC:(s + 1) * SC], banks[6][0:META, 0:SC]).then_inc(v_out, 1)
            act.wait_ge(vw_turned, 2)
            nc.scalar.copy(Vw[:].rearrange("p a b -> p (a b)"), banks[4][:]).then_inc(v_out, 1)
            nc.scalar.copy(Vwm[:], banks[6][0:META, 0:P]).then_inc(v_out, 1)

            act.preload_act_table_set("natural_log_exp_and_others")
            act.wait_ge(zm_mm, 1)
            A(sq[:, 0], banks[2][:], ACT.Abs).then_inc(zm_act, 1)
            act.wait_ge(zm_act, 1)
            A(sq[:, 0], sq[:, 0], ACT.Exp, scale=-1.0).then_inc(zm_act, 1)
            act.wait_ge(zm_act, 2)
            A(sq[:, 0], sq[:, 0], ACT.Ln, bias=1.0).then_inc(zm_act, 1)
            act.wait_ge(zm_dve, 1)
            for step in range(32 + 3):
                u = step
                if u < 32:
                    n = (u % 4 + 1) * P
                    act.wait_ge(z_mm, u + 1)
                    if u >= 2:
                        act.wait_ge(arg_done, u - 1)
                    A(sq[:, u % 2, 0:n], banks[u % 2][:, 0:n], ACT.Abs).then_inc(sp_act, 1)
                    act.wait_ge(sp_act, 3 * u + 1)
                    A(sq[:, u % 2, 0:n], sq[:, u % 2, 0:n], ACT.Exp, scale=-1.0).then_inc(sp_act, 1)
                    act.wait_ge(sp_act, 3 * u + 2)
                    A(sq[:, u % 2, 0:n], sq[:, u % 2, 0:n], ACT.Ln, bias=1.0).then_inc(sp_act, 1)
                u = step - 1
                if 0 <= u < 32:
                    n = (u % 4 + 1) * P
                    act.wait_ge(arg_done, u + 1)
                    A(unit_buf(u)[:, 0:n], unit_buf(u)[:, 0:n], ACT.Exp).then_inc(weights_done, 1)
                    if u % 4 == 3:
                        h = u // 4
                        act.wait_ge(argm_done, h + 1)
                        A(wm[:, h % 2], wm[:, h % 2], ACT.Exp).then_inc(weightsm_done, 1)
                u = step - 2
                if 0 <= u < 32:
                    n = (u % 4 + 1) * P
                    act.wait_ge(weights_mm, u + 1)
                    if u >= 2:
                        act.wait_ge(pv_mm, u - 1)
                    nc.scalar.copy(wT[:, u % 2, 0:n], banks[2 + u % 2][:, 0:n]).then_inc(weights_out, 1)
                    if u % 4 == 3:
                        h = u // 4
                        act.wait_ge(weightsm_mm, h + 1)
                        if h:
                            act.wait_ge(pvm_mm, h)
                        nc.scalar.copy(wTm[:], banks[5][0:META, :]).then_inc(weightsm_out, 1)
            act.preload_act_table(ACT.Silu)
            for t in range(12):
                act.wait_ge(gates_out, t + 1)
                A(zs[:, t], zs[:, t], ACT.Silu).then_inc(zs_silu, 1)
            act.preload_act_table_set("exp_and_others")

            def tanh(m):
                act.wait_ge(gates_out, 12 + m + 1)
                A(gt(m), gt(m), ACT.Tanh, scale=0.5).then_inc(merge_tanh, 1)
            for step in range(32 + 3):
                v = step
                if v < 32:
                    o = 112 if v % 4 == 0 else 0
                    s2 = unit_buf(v).rearrange("p (a b) -> p a b", a=2)
                    act.wait_ge(score_done, v + 1)
                    if v >= 2:
                        act.wait_ge(weights2_done, v - 1)
                    for i in range(2):
                        A(s2[:, i, o:], s2[:, i, o:], ACT.Exp, bias=tiny[:, 8 * (v % 2) + 2 + i:8 * (v % 2) + 3 + i],
                          accum_out=tiny[:, 16 + 4 * (v % 2) + i:17 + 4 * (v % 2) + i]).then_inc(exp2_done, 1)
                    A(tiny[:, 18 + 4 * (v % 2):20 + 4 * (v % 2)], tiny[:, 8 * (v % 2) + 4:8 * (v % 2) + 6], ACT.Exp).then_inc(exp2_done, 1)
                v = step - 2
                if 0 <= v < 32:
                    act.wait_ge(weights2_mm, v + 1)
                    if v >= 2:
                        act.wait_ge(pv2_mm, v - 1)
                    if v % 4:
                        nc.scalar.copy(wT[:, v % 2, 0:256], banks[2 + v % 2][:, 0:256]).then_inc(weights2_out, 1)
                        nc.scalar.copy(wT[:, v % 2, 256:512], banks[2 + v % 2][:, 256:512]).then_inc(weights2_out, 1)
                    else:
                        w2 = wT[:, v % 2].rearrange("p (a b c) -> p a b c", a=2, b=2)
                        b2 = banks[2 + v % 2][:].rearrange("p (a b c) -> p a b c", a=2, b=2)
                        nc.scalar.copy(w2[:, :, 1], b2[:, :, 1]).then_inc(weights2_out, 1)
                        nc.scalar.copy(w2[0:META, :, 0], b2[0:META, :, 0]).then_inc(weights2_out, 1)
                if step < 32 and (3 * step + 3) // 8 > 3 * step // 8:
                    tanh(3 * step // 8)
            act.wait_ge(pv2_mm, 32)
            for j in range(4):
                act.wait_ge(sb_gated, j + 1)
                nc.scalar.copy(asb_hi[:, j], zs[:, j]).then_inc(br_high, 1)
            for m in range(12, 16):
                tanh(m)
            act.wait_ge(eighths_used, 8 * N_BR)
            for j in range(8):
                act.wait_ge(sw_gated, j + 1)
                nc.scalar.copy(xn_hi[:, j, META:TM], zs[:, 4 + j]).then_inc(br_high, 1)
            act.wait_ge(br_split, 12)
            for m in range(KD):
                act.wait_ge(merged, m + 1)
                nc.scalar.mul(mg_hi[:, m], gt(m), 0.5).then_inc(merged_high, 1)
            for half in range(2):
                for t in range(TT):
                    act.wait_ge(eighths_used, 8 * (N_OUT2 + 2 * half + 1) + 2 * t + 2)
                    if half or t:
                        act.wait_ge(out_sq, 4 * half + t)
                    A(sq[:, 0], banks[(4, 0)[half] + t][:], ACT.Square, accum_out=tiny[:, 2 * t + half:2 * t + half + 1]).then_inc(out_sq, 1)
                    if half:
                        if t == 0:
                            act.preload_act_table_set("natural_log_exp_and_others")
                        act.wait_ge(out_sum, t + 1)
                        A(tiny[:, 20 + t:21 + t], tiny[:, 16 + t:17 + t], ACT.Ln, bias=epsc, scale=1.0 / D).then_inc(out_root, 1)
                        act.wait_ge(out_root, 2 * t + 1)
                        A(tiny[:, 24 + t:25 + t], tiny[:, 20 + t:21 + t], ACT.Exp, scale=-0.5).then_inc(out_root, 1)

        @block.vector
        def _(dve):
            V = nc.vector

            def low(q, d):
                dve.wait_ge(xn_high, 8 * q + d + 1)
                V.scalar_tensor_tensor(out=xn_lo[:, d, META:TM], in0=xT[:, d], scalar=gain(q, d), in1=xn_hi[:, d, META:TM].bitcast(F32),
                                       op0=ALU.mult, op1=ALU.subtract).then_inc(xn_split, 1)

            def add_square(q, d):
                dve.wait_ge(sq_done, 8 * q + d + 1)
                if d == 0:
                    V.tensor_copy(sums, sq[:, 0]).then_inc(sq_added, 1)
                else:
                    dve.wait_ge(sq_added, 8 * q + d)
                    V.tensor_tensor(sums, sums, sq[:, d % 2], ALU.add).then_inc(sq_added, 1)

            def add_squares(d):
                for i, total in enumerate((sums, sums2)):
                    n = 24 + 2 * d + i
                    dve.wait_ge(sq_done, n + 1)
                    if d == 0:
                        V.tensor_copy(total, sq[:, i]).then_inc(sq_added, 1)
                    else:
                        dve.wait_ge(sq_added, n - 1)
                        V.tensor_tensor(total, total, sq[:, i], ALU.add).then_inc(sq_added, 1)

            def norm_step(q, d):
                dve.wait_ge(x_ready, 8 * q + d + 1)
                low(q, d)
                if q < 3:
                    add_square(q, d)

            def token_factor(n):
                dve.wait_ge(rtok_mm, n)
                V.tensor_copy(rtok[:], banks[7][:, 0:TT]).then_inc(rtok_done, 1)

            def ffn(base, n0, q):
                def pair(i, guard):
                    for f in range(2):
                        dve.wait_ge(eighths_used, 8 * (n0 + 2 * i) + 4 * f + 4)
                        if guard:
                            dve.wait_ge(inner_done, base + 2 * i + f - 1)
                        V.tensor_tensor(gs[:, f], banks[f][:], rstd[:], ALU.mult).then_inc(gate_out, 1)
                    for f in range(2):
                        dve.wait_ge(eighths_used, 8 * (n0 + 2 * i + 1) + 4 * f + 4)
                        if guard:
                            dve.wait_ge(inner_split, base + 2 * i + f - 1)
                        V.tensor_tensor(hf[:, f], banks[2 + f][:], rstd[:], ALU.mult).then_inc(up_out, 1)
                        dve.wait_ge(gate_silu, base + 2 * i + f + 1)
                        dve.wait_ge(up_out, base + 2 * i + f + 1)
                        V.tensor_tensor(hf[:, f], hf[:, f], gs[:, f], ALU.mult).then_inc(inner_done, 1)
                    for f in range(2):
                        dve.wait_ge(inner_done, base + 2 * i + f + 1)
                        dve.wait_ge(inner_high, base + 2 * i + f + 1)
                        at = bass.ds(2 * i + f, 1) if guard else slice(f, f + 1)
                        V.tensor_tensor(h_lo[:, at, :].rearrange("p a t -> p (a t)"), hf[:, f],
                                        h_hi[:, at, :].bitcast(F32).rearrange("p a t -> p (a t)"), ALU.subtract).then_inc(inner_split, 1)
                dve.wait_ge(rstd_done, q + 1)
                pair(0, False)
                if q == 0:
                    meta_split()
                with dve.Fori(1, FP) as i:
                    pair(i, True)
                for d in range(KD + 1):
                    if d < KD:
                        dve.wait_ge(eighths_used, 8 * (n0 + 3 * FP - 1) + d + 1)
                        V.scalar_tensor_tensor(out=xT[:, d], in0=banks[(d + 4) % 8][:], scalar=0.5, in1=xT[:, d],
                                               op0=ALU.mult, op1=ALU.add).then_inc(x_ready, 1)
                    if d:
                        norm_step(q + 1, d - 1)

            dve.wait_ge(slab_high, 1)
            V.tensor_tensor(w_lo[:, 0], raw[:, 0], w_hi[:, 0].bitcast(F32), ALU.subtract).then_inc(slab_split, 1)
            dve.wait_ge(x_turned, 1)
            V.tensor_copy(cols[:, 0:KD], banks[7][:, 0:KD]).then_inc(cols_ready, 1)
            dve.wait_ge(cols_ready, 1)
            for d in range(KD + 1):
                if d < KD:
                    dve.wait_ge(x_turned, d + 2)
                    V.tensor_copy(xT[:, d], banks[d][:]).then_inc(x_ready, 1)
                if d:
                    dve.wait_ge(x_ready, d)
                    low(0, d - 1)
            for d in range(KD):
                add_square(0, d)
            dve.wait_ge(meta_act, 3)
            V.tensor_scalar(meta_in[:], meta_in[:], tiny[0:META, 2:3], None, ALU.mult).then_inc(meta_dve, 1)

            def meta_split():
                dve.wait_ge(meta_turned, 1)
                V.tensor_copy(cols[:, KD:ROWS], banks[6][:, KD:ROWS]).then_inc(cols_ready, 1)
                dve.wait_ge(cols_ready, 2)
                V.tensor_tensor(cols[:, V_FG2:V_FG2 + KD], cols[:, V_FIN1:V_FIN1 + KD], cols[:, V_N2:V_N2 + KD], ALU.mult).then_inc(cols_ready, 1)
                V.tensor_tensor(meta_f[:], banks[5][:, 0:KD * META].rearrange("p (k m) -> p k m", k=KD),
                                cols[:, V_N2:V_N2 + KD].unsqueeze(2).to_broadcast([P, KD, META]), ALU.mult).then_inc(meta_dve, 1)
                dve.wait_ge(meta_act, 4)
                dve.wait_ge(meta_dve, 2)
                V.tensor_tensor(xn_lo[:, :, 0:META], meta_f[:], xn_hi[:, :, 0:META].bitcast(F32), ALU.subtract).then_inc(meta_dve, 1)
            ffn(0, N_FFN1, 0)

            dve.wait_ge(mix_loaded, 80)
            dve.wait_ge(ba_split, 1)
            V.tensor_tensor(wba_lo[:, 0:KD * 8], wba[:].rearrange("p k c -> p (k c)"), wba_hi[:, 0:KD * 8].bitcast(F32), ALU.subtract).then_inc(ba_split, 1)
            for w in (wba_hi, wba_lo):
                V.memset(w[:, KD * 8:wba_w].bitcast(F32), 0.0).then_inc(ba_split, 1)
            V.memset(rw[:, :, 0:3], 0.0).then_inc(conv_step, 1)
            for j in range(12):
                dve.wait_ge(eighths_used, 8 * N_MIX + 4 * j + 4)
                if j >= 2:
                    dve.wait_ge(conv_done, j - 1)
                V.tensor_tensor(rw[:, j % 2, 3:3 + T], banks[j % 4][:], rstd[:], ALU.mult).then_inc(conv_in, 1)
                dve.wait_ge(conv_in, j + 1)
                if j >= 2:
                    dve.wait_ge(qkv_done, j - 1)
                acc = hf[:, j % 2]
                tap = lambda i: cols[:, V_CONV + 12 * i + j:V_CONV + 12 * i + j + 1]
                dve.wait_ge(conv_step, 3 * j + 1)
                V.tensor_scalar(acc, rw[:, j % 2, 0:T], tap(0), None, ALU.mult).then_inc(conv_step, 1)
                for i in range(1, 4):
                    dve.wait_ge(conv_step, 3 * j + i + 1)
                    V.scalar_tensor_tensor(out=acc, in0=rw[:, j % 2, i:i + T], scalar=tap(i), in1=acc, op0=ALU.mult, op1=ALU.add)\
                        .then_inc(conv_done if i == 3 else conv_step, 1)
                if j == 3:
                    token_factor(1)
                if j == 5:
                    dve.wait_ge(gate_w_mm, 1)
                    for half in range(2):
                        V.tensor_copy(wsT[:, 4 * half:4 * half + 4].rearrange("p g i -> p (g i)"), banks[6 + half][:]).then_inc(gate_w_done, 1)
                    dve.wait_ge(gate_w_done, 2)
                    V.memset(wsT[CH:P, :, 0:CH], 0.0).then_inc(gate_w_done, 1)
                if j == 4:
                    dve.wait_ge(ba_mm, 1)
                    V.tensor_tensor(baf[:], banks[4][0:8, :], rstd[0:8, :], ALU.mult).then_inc(decay_dve, 1)
                if j == 7:
                    hp = lambda ap: ap.rearrange("p (h t) -> p h t", h=4)
                    head4 = lambda ap: ap.unsqueeze(2).to_broadcast([P, 4, 4])
                    ba = banks[5][:, 0:32].rearrange("p (t c) -> p c t", c=8)
                    dve.wait_ge(ba_mm, 2)
                    dve.wait_ge(decay_act, 1)
                    V.tensor_tensor(hp(s_a), ba[:, 4:8], head4(hvec[:, 0]), ALU.add).then_inc(decay_dve, 1)
                    V.tensor_scalar(s_e, s_e, 1.0, None, ALU.add).then_inc(decay_dve, 1)
                    dve.wait_ge(decay_dve, 3)
                    V.reciprocal(s_beta, s_e).then_inc(decay_dve, 1)
                    dve.wait_ge(decay_act, 5)
                    V.scalar_tensor_tensor(out=s_t, in0=s_a, scalar=0.0, in1=s_t, op0=ALU.max, op1=ALU.add).then_inc(decay_dve, 1)
                    dve.wait_ge(decay_dve, 5)
                    V.scalar_tensor_tensor(out=hp(s_g), in0=hp(s_t), scalar=-1.0, in1=head4(s_ea[:, 0:4]), op0=ALU.mult, op1=ALU.mult).then_inc(decay_dve, 1)
                    dve.wait_ge(cum_mm, 1)
                    V.tensor_copy(s_c.rearrange("p a b -> p (a b)"), banks[5][:, 0:64]).then_inc(decay_dve, 1)
                    dve.wait_ge(decay_dve, 7)
                    V.tensor_scalar(s_ngc, s_c[:, 0], -1.0, None, ALU.mult).then_inc(decay_dve, 1)
                    V.tensor_tensor(s_kd, s_c[:, 1], s_c[:, 0], ALU.subtract).then_inc(decay_dve, 1)
                    dve.wait_ge(decay_act, 6)
                    V.tensor_tensor(s_be, s_beta, s_eg, ALU.mult).then_inc(decay_dve, 1)
                if j == 9:
                    for i in range(8):
                        dve.wait_ge(len_root, 2 * i + 2)
                        V.scalar_tensor_tensor(out=qkv[:, i], in0=qkv[:, i], scalar=P ** -0.5 if i < 4 else 1.0, in1=gs[:, i % 2],
                                               op0=ALU.mult, op1=ALU.mult).then_inc(len_done, 1)
            dve.wait_ge(decay_act, 8)
            dve.wait_ge(decay_dve, 10)
            for h in range(H):
                at = slice(4 * h, 4 * h + 4)
                e = (sq, hf)[h % 2]
                dve.wait_ge(k_turned, h + 1)
                V.tensor_tensor(quarters(kb[:, h]), quarters(banks[5][:]), per_block(s_be[:, at]), ALU.mult).then_inc(k_tok_done, 1)
                V.tensor_tensor(quarters(kd[:, h]), quarters(banks[5][:]), per_block(s_kd[:, at]), ALU.mult).then_inc(k_tok_done, 1)
                dve.wait_ge(v_turned, h + 1)
                V.tensor_tensor(quarters(vb[:, h]), quarters(banks[6][:]), per_block(s_beta[:, at]), ALU.mult).then_inc(v_beta, 1)
                dve.wait_ge(decay_exp, 8 * h + 4)
                dve.wait_ge(kq_mm, h + 1)
                V.tensor_tensor(atT(h), banks[4][:], e[:, 0], ALU.mult).then_inc(qk_decayed, 1)
                dve.wait_ge(g_rows_exp, h + 1)
                V.tensor_tensor(qT(h), qT(h), gs[:, 1], ALU.mult).then_inc(q_decayed, 1)
                dve.wait_ge(decay_exp, 8 * h + 8)
                for p in range(4):
                    c = slice(p * P, (p + 1) * P)
                    ins = V.scalar_tensor_tensor(out=Lm(h)[:, c], in0=banks[3][:, c], scalar=s_beta[:, 4 * h + p:4 * h + p + 1], in1=e[:, 1, c],
                                                 op0=ALU.mult, op1=ALU.mult)
                ins.then_inc(l_done, 1)
            for g in range(2):
                for hh in range(2):
                    h = 2 * g + hh
                    dve.wait_ge(l_done, h + 1)
                    if g:
                        dve.wait_ge(zt_mm, 2 * (LEVELS - 1) - 1 + hh)
                    V.tensor_tensor(quarters(Mm[:, hh]), quarters(Lm(h)), over4(mixm[:, 6]), ALU.mult).then_inc(m_done, 1)
                    dve.wait_ge(m_done, (g * LEVELS) * 2 + hh + 1)
                    V.tensor_tensor(quarters(Tm[:, hh]), over4(ident), quarters(Mm[:, hh]), ALU.subtract).then_inc(t_init, 1)
                for hh in range(2):
                    h = 2 * g + hh
                    dve.wait_ge(m_turned, h + 1)
                    V.tensor_tensor(quarters(Z[:, h]), over4(ident), quarters(banks[2 + hh][:]), ALU.subtract).then_inc(z_done, 1)
                for level in range(LEVELS):
                    for hh in range(2 if level < LEVELS - 1 else 0):
                        h = 2 * g + hh
                        if level == 0:
                            dve.wait_ge(m_turned, h + 1)
                            dve.wait_ge(t_init, h + 1)
                        else:
                            dve.wait_ge(mz_mm, (g * (LEVELS - 1) + level - 1) * 2 + hh + 1)
                        V.tensor_tensor(quarters(Mm[:, hh]), quarters(Lm(h)), over4(mixm[:, 7 + level]), ALU.mult).then_inc(m_done, 1)
                    for hh in range(2 if level else 0):
                        h = 2 * g + hh
                        n = (g * (LEVELS - 1) + level - 1) * 2 + hh
                        dve.wait_ge(zt_mm, n + 1)
                        if level == 1:
                            dve.wait_ge(z_done, g * 2 * LEVELS + hh + 1)
                        V.tensor_tensor(Z[:, h], Z[:, h], banks[2 + hh][:], ALU.subtract).then_inc(z_done, 1)
                        if level < LEVELS - 1:
                            V.tensor_tensor(Tm[:, hh], Tm[:, hh], banks[4 + hh][:], ALU.subtract).then_inc(t_done, 1)
                    if g == 0 and level in (3, 4):
                        dve.wait_ge(gate_v_gelu, TT)
                        for t in range(2 * level - 6, 2 * level - 4):
                            V.bn_stats(st6[:, t], vtok[:, t]).then_inc(ln_stats, 1)
                    if g == 0 and level == 5:
                        dve.wait_ge(ln_stats, 4)
                        for t in range(TT):
                            V.bn_aggr(mv[:, t], st6[:, t]).then_inc(ln_stats, 1)
            for m in range(4):
                dve.wait_ge(gate_mm, m + 1)
                V.tensor_tensor(quarters(ya[:, m]), quarters(banks[m][:]), over4(bs[:, m]), ALU.add).then_inc(gate_mixed, 1)
            def ya_low(m):
                dve.wait_ge(y_high, m + 1)
                V.tensor_tensor(yl(m), ya[:, m], yh(m).bitcast(F32), ALU.subtract).then_inc(y_split, 1)

            for c in range(NC):
                r = slice(CH * (c % 2), CH * (c % 2) + CH)
                dve.wait_ge(vnew_mm, c + 1)
                V.tensor_copy(vnew[r], banks[4][r]).then_inc(vnew_done, 1)
                if c < NC - 1:
                    dve.wait_ge(state_mm, c + 1)
                    if c == 0:
                        V.tensor_copy(S[:, 1], banks[5][:]).then_inc(state_done, 1)
                    else:
                        dve.wait_ge(state_done, c)
                        for h in range(H):
                            hc = slice(h * P, (h + 1) * P)
                            ins = V.scalar_tensor_tensor(out=S[:, (c + 1) % 2, hc], in0=S[:, c % 2, hc],
                                                         scalar=egl[:, c % 2, 4 * h + c // 2:4 * h + c // 2 + 1], in1=banks[5][:, hc],
                                                         op0=ALU.mult, op1=ALU.add)
                        ins.then_inc(state_done, 1)
                if 1 <= c <= 4:
                    dve.wait_ge(uz_act, c)
                    dve.wait_ge(gate_mixed, c)
                    V.tensor_tensor(ya[:, c - 1], ya[:, c - 1], gs[:, (c - 1) % 2], ALU.mult).then_inc(ya_done, 1)
                if c > 4:
                    ya_low(c - 5)
                if c == NC - 1:
                    ya_low(3)
                    dve.wait_ge(chunk_out_mm, NC)
                    for h in range(H):
                        V.tensor_copy(vb[:, h], banks[h][:]).then_inc(o_out, 1)
                dve.wait_ge(eighths_used, 8 * (N_MIX + 8) + 4 * c + 4)
                if 2 <= c < 4:
                    dve.wait_ge(ya_done, c - 1)
                V.tensor_tensor(gs[:, c % 2] if c < 4 else zT[:, c - 4], banks[6 + c % 2][:], rstd[:], ALU.mult).then_inc(uz_out, 1)
            for h in range(H + 1):
                if h < H:
                    dve.wait_ge(o_root, 2 * h + 2)
                    V.scalar_tensor_tensor(out=vb[:, h], in0=vb[:, h], scalar=cols[:, V_DN:V_DN + 1], in1=gs[:, h % 2],
                                           op0=ALU.mult, op1=ALU.mult).then_inc(o_normed, 1)
                    dve.wait_ge(o_normed, h + 1)
                    dve.wait_ge(uz_act, 4 + h + 1)
                    V.tensor_tensor(vb[:, h], vb[:, h], zT[:, h], ALU.mult).then_inc(yb_done, 1)
                e = h - 1
                if e >= 0:
                    dve.wait_ge(y_high, 4 + e + 1)
                    dve.wait_ge(yb_done, e + 1)
                    V.tensor_tensor(yl(4 + e), vb[:, e], yh(4 + e).bitcast(F32), ALU.subtract).then_inc(y_split, 1)
            for m in range(KD + 1):
                if m < KD:
                    dve.wait_ge(eighths_used, 8 * N_OUT1 + 4 * m + 4)
                    V.tensor_tensor(xT[:, m], xT[:, m], banks[m % 4][:], ALU.add).then_inc(x_ready, 1)
                if m:
                    norm_step(2, m - 1)

            ffn(2 * FP, N_FFN2, 2)

            for d in range(KD):
                add_squares(d)
            dve.wait_ge(rstd_done, 4)
            V.tensor_tensor(gs[:, 1], banks[5][:], rstd[:], ALU.mult).then_inc(two_norms_dve, 1)
            dve.wait_ge(two_norms_dve, 1)
            V.tensor_tensor(gs[:, 1], gs[:, 1], rstd[:], ALU.mult).then_inc(two_norms_dve, 1)
            V.memset(factor[:, 0:META], 1.0).then_inc(factor_done, 1)
            dve.wait_ge(two_norms_act, 2)
            V.tensor_tensor(factor_t, rstd[:], gs[:, 1], ALU.mult).then_inc(factor_done, 1)
            dve.wait_ge(factor_done, 2)
            for j in range(4):
                dve.wait_ge(eighths_used, 8 * N_P2 + 4 * j + 4)
                V.scalar_tensor_tensor(out=Qs[:, j], in0=banks[j][:], scalar=0.125, in1=factor_t, op0=ALU.mult, op1=ALU.mult).then_inc(qk_out, 1)
                if j == 0:
                    token_factor(2)
            for j in range(6):
                dst = Ks[:, j] if j < 4 else kraw[:] if j == 4 else vwf
                dve.wait_ge(eighths_used, 8 * (N_P2 + 2) + 4 * j + 4 if j < 4 else 8 * (N_P2 + 6) + 4 * (j - 4) + 4)
                if j == 4:
                    dve.wait_ge(sq_done, 40)
                    for d in range(KD):
                        V.scalar_tensor_tensor(out=xT[:, d], in0=xT[:, d], scalar=cols[:, V_FIN1 + d:V_FIN1 + d + 1], in1=rstd[:],
                                               op0=ALU.mult, op1=ALU.mult).then_inc(x_ready, 1)
                    dve.wait_ge(att_loaded, 32)
                for half in range(2):
                    hc = slice(264 * half, 264 * half + 264)
                    V.tensor_tensor(dst[:, hc], banks[2 * (j % 2) + half][:, 0:264], factor[:, hc], ALU.mult).then_inc(qk_out, 1)

            def rope_k(g):
                dve.wait_ge(k_rot_mm, g + 1)
                if g:
                    dve.wait_ge(k_rot_done, 2)
                    dve.wait_ge(q_rot_done, 1)
                for half in range(2):
                    hc = slice(264 * half, 264 * half + 264)
                    V.tensor_tensor(hf[:, half, 0:264], banks[(5, 7)[half]][:, 0:264], sinT[:, hc], ALU.mult).then_inc(k_rot_step, 1)
                    V.tensor_tensor(Kw[:, g, hc], banks[2 + half][:, 0:264], cosT[:, hc], ALU.mult).then_inc(k_rot_step, 1)
                for half in range(2):
                    hc = slice(264 * half, 264 * half + 264)
                    dve.wait_ge(k_rot_step, 4 * g + 2 * half + 2)
                    V.tensor_tensor(Kw[:, g, hc], Kw[:, g, hc], hf[:, half, 0:264], ALU.add).then_inc(k_rot_done, 1)

            def q_ev(j):
                dve.wait_ge(eighths_used, 8 * (N_P2 + 7) + 4 * j + 4)
                if j >= 2:
                    dve.wait_ge(q_rot_mm, j - 1)
                    dve.wait_ge(q_rot_step, 2 * (j - 1))
                else:
                    dve.wait_ge(vw_turned, 2)
                V.scalar_tensor_tensor(out=gs[:, j % 2], in0=banks[j % 2][:], scalar=0.125, in1=factor_t, op0=ALU.mult, op1=ALU.mult).then_inc(qk_out, 1)

            V.memset(kblk[:], 0.0).then_inc(kblk_done, 1)
            dve.wait_ge(kblk_done, 1)
            dve.wait_ge(qk_out, 12)
            for half in range(2):
                r = slice(HD * half, HD * half + HD)
                V.tensor_copy(kblk[r, :, META * half:META * half + META], Ks[r, :, 0:META]).then_inc(kblk_done, 1)
            rope_k(0)
            q_ev(0)
            for j in range(8):
                if j < 7:
                    q_ev(j + 1)
                dve.wait_ge(q_rot_mm, j + 1)
                dve.wait_ge(qk_out, 16 + j + 1)
                if j < 2:
                    dve.wait_ge(k_rot_done, 2 + 2 * j)
                else:
                    dve.wait_ge(q_rot_done, j - 1)
                V.tensor_tensor(hf[:, j % 2], banks[(6, 4)[j % 2]][:], sinT[:, META:], ALU.mult).then_inc(q_rot_step, 1)
                V.tensor_tensor(Qw[:, j], gs[:, j % 2], cosT[:, META:], ALU.mult).then_inc(q_rot_step, 1)
                dve.wait_ge(q_rot_step, 2 * j + 2)
                V.tensor_tensor(Qw[:, j], Qw[:, j], hf[:, j % 2], ALU.add).then_inc(q_rot_done, 1)
                if j == 0:
                    rope_k(1)

            def gate_ev(t):
                dve.wait_ge(eighths_used, 8 * (N_P2 + 11) + 4 * t + 4)
                V.tensor_tensor(zs[:, t] if t < 12 else gt(t - 12), banks[6 + t % 2][:], factor_t, ALU.mult).then_inc(gates_out, 1)

            dve.wait_ge(zm_act, 3)
            dve.wait_ge(q_rot_done, 8)
            V.scalar_tensor_tensor(out=hf[:, 0], in0=banks[2][:], scalar=0.0, in1=sq[:, 0], op0=ALU.max, op1=ALU.add).then_inc(zm_dve, 1)
            dve.wait_ge(zm_dve, 1)
            V.tensor_tensor_scan(gs[:, 0, ::-1], meta_mask[:, ::-1], hf[:, 0, ::-1], 0.0, ALU.mult, ALU.add).then_inc(zm_dve, 1)
            dve.wait_ge(zm_dve, 2)
            V.tensor_tensor(argm[:], banks[2][:], gs[:, 0], ALU.subtract).then_inc(zm_dve, 1)
            dve.wait_ge(zm_dve, 3)
            for u in range(32 + 4):
                if u < 32:
                    n = (u % 4 + 1) * P
                    bank = banks[u % 2]
                    dve.wait_ge(sp_act, 3 * u + 3)
                    if u >= 1:
                        dve.wait_ge(arg_step, 4 * u)
                    V.scalar_tensor_tensor(out=hf[:, 1, 0:n], in0=bank[:, 0:n], scalar=0.0, in1=sq[:, u % 2, 0:n], op0=ALU.max, op1=ALU.add).then_inc(arg_step, 1)
                    dve.wait_ge(arg_step, 4 * u + 1)
                    if u >= 3:
                        dve.wait_ge(weights_mm, u - 2)
                    w = unit_buf(u)[:, 0:n]
                    V.tensor_tensor_scan(w[:, ::-1], hf[:, 1, 0:n][:, ::-1], scan_mask[:, T - n:T][:, ::-1], 0.0, ALU.add, ALU.mult).then_inc(arg_step, 1)
                    dve.wait_ge(arg_step, 4 * u + 2)
                    V.tensor_copy(ctok[:, u:u + 1], w[:, 0:1]).then_inc(arg_step, 1)
                    dve.wait_ge(arg_step, 4 * u + 3)
                    V.tensor_tensor(w, bank[:, 0:n], w, ALU.subtract).then_inc(arg_step, 1)
                    dve.wait_ge(arg_step, 4 * u + 4)
                    V.tensor_tensor(w[:, n - P:n], w[:, n - P:n], neg_diag, ALU.add).then_inc(arg_done, 1)
                    if u % 4 == 3:
                        h = u // 4
                        if h >= 2:
                            dve.wait_ge(weightsm_mm, h - 1)
                        V.tensor_tensor(wm[:, h % 2].rearrange("p (a b) -> p a b", a=4), argm[:].rearrange("p (j t h m) -> p j h t m", j=4, t=4, h=2)[:, h // 2, h % 2],
                                        ctok[:, 4 * h:4 * h + 4].unsqueeze(2).to_broadcast([P, 4, META]), ALU.subtract).then_inc(argm_done, 1)
                if u < 32 and (3 * u + 3) // 8 > 3 * u // 8:
                    gate_ev(3 * u // 8)
                if u >= 10 and u % 8 == 2:
                    j = (u - 10) // 8
                    dve.wait_ge(pvm_mm, 2 * j + 2)
                    V.tensor_copy(Qs[:, j], banks[4][:]).then_inc(sb_out, 1)
            V.tensor_scalar(tiny[:, 32:48], sinks[:], -1.0, None, ALU.mult).then_inc(score_step, 1)
            for j in range(4):
                dve.wait_ge(zs_silu, j + 1)
                dve.wait_ge(sb_out, j + 1)
                V.tensor_tensor(zs[:, j], zs[:, j], Qs[:, j], ALU.mult).then_inc(sb_gated, 1)
            for step in range(32 + 4):
                v = step
                if v < 32:
                    o = 112 if v % 4 == 0 else 0
                    j = v // 4
                    s2 = unit_buf(v).rearrange("p (a b) -> p a b", a=2)[:, :, o:]
                    b2 = banks[v % 2][:].rearrange("p (a b) -> p a b", a=2)[:, :, o:]
                    c = 8 * (v % 2)
                    dve.wait_ge(z2_mm, 2 * v + 2)
                    if v >= 3:
                        dve.wait_ge(weights2_mm, v - 2)
                    elif v == 0:
                        dve.wait_ge(weights_mm, 32)
                    V.tensor_tensor(s2, b2, win_mask[:, o:].unsqueeze(1).to_broadcast([P, 2, 256 - o]), ALU.add).then_inc(score_step, 1)
                    dve.wait_ge(score_step, 1 + 3 * v + 1)
                    if v >= 2:
                        dve.wait_ge(exp2_done, 3 * (v - 1))
                    V.tensor_reduce(tiny[:, c:c + 2], s2, AX_X, ALU.max).then_inc(score_step, 1)
                    dve.wait_ge(score_step, 1 + 3 * v + 2)
                    V.scalar_tensor_tensor(out=tiny[:, c + 2:c + 4], in0=tiny[:, c:c + 2], scalar=-1.0, in1=tiny[:, 32 + 2 * j:34 + 2 * j],
                                           op0=ALU.mult, op1=ALU.min).then_inc(score_step, 1)
                    dve.wait_ge(score_step, 1 + 3 * v + 3)
                    V.tensor_tensor(tiny[:, c + 4:c + 6], tiny[:, c + 2:c + 4], tiny[:, 32 + 2 * j:34 + 2 * j], ALU.subtract).then_inc(score_done, 1)
                v = step - 1
                if 0 <= v < 32:
                    o = 112 if v % 4 == 0 else 0
                    e = 16 + 4 * (v % 2)
                    s2 = unit_buf(v).rearrange("p (a b) -> p a b", a=2)
                    dve.wait_ge(exp2_done, 3 * v + 3)
                    if v >= 1:
                        dve.wait_ge(weights2_done, v)
                    V.tensor_tensor(tiny[:, 24:26], tiny[:, e:e + 2], tiny[:, e + 2:e + 4], ALU.add).then_inc(norm2_step, 1)
                    dve.wait_ge(norm2_step, 2 * v + 1)
                    V.reciprocal(tiny[:, 26:28], tiny[:, 24:26]).then_inc(norm2_step, 1)
                    dve.wait_ge(norm2_step, 2 * v + 2)
                    for i in range(2):
                        ins = V.tensor_scalar(s2[:, i, o:], s2[:, i, o:], tiny[:, 26 + i:27 + i], None, ALU.mult)
                    ins.then_inc(weights2_done, 1)
                if step < 32 and (3 * step + 3) // 8 > 3 * step // 8:
                    if step < 3:
                        dve.wait_ge(sb_gated, 4)
                    gate_ev(12 + 3 * step // 8)
                if step >= 7 and step % 4 == 3:
                    j = (step - 7) // 4
                    dve.wait_ge(pv2_mm, 4 * j + 4)
                    dve.wait_ge(zs_silu, 5 + j)
                    V.tensor_tensor(zs[:, 4 + j], zs[:, 4 + j], banks[4 + j % 2][:], ALU.mult).then_inc(sw_gated, 1)
            for j in range(4):
                dve.wait_ge(br_high, j + 1)
                V.tensor_tensor(asb_lo[:, j], zs[:, j], asb_hi[:, j].bitcast(F32), ALU.subtract).then_inc(br_split, 1)
            for t in range(24, 28):
                gate_ev(t)
            for j in range(8):
                dve.wait_ge(br_high, 4 + j + 1)
                dve.wait_ge(sw_gated, j + 1)
                V.tensor_tensor(xn_lo[:, j, META:TM], zs[:, 4 + j], xn_hi[:, j, META:TM].bitcast(F32), ALU.subtract).then_inc(br_split, 1)
            dve.wait_ge(merge_tanh, 16)
            for half in range(2):
                for m in range(4 * half, 4 * half + 4):
                    dve.wait_ge(eighths_used, 8 * (N_BR + 3 * half) + 2 * (m % 4) + 2)
                    V.scalar_tensor_tensor(out=gt(m), in0=gt(m), scalar=1.0, in1=banks[m % 2][:], op0=ALU.add, op1=ALU.mult).then_inc(sb_merged, 1)
                for m in range(4 * half, 4 * half + 4):
                    dve.wait_ge(eighths_used, 8 * (N_BR + 3 * half + 1) + 4 * (m % 4) + 4)
                    if m >= 2:
                        dve.wait_ge(merged, m - 1)
                    V.scalar_tensor_tensor(out=hf[:, m % 2], in0=gt(8 + m), scalar=1.0, in1=banks[2 + m % 2][:], op0=ALU.add, op1=ALU.mult).then_inc(sw_merged, 1)
                    dve.wait_ge(sw_merged, m + 1)
                    dve.wait_ge(sb_merged, m + 1)
                    V.tensor_tensor(gt(m), gt(m), hf[:, m % 2], ALU.add).then_inc(merged, 1)
                    dve.wait_ge(merged_high, m + 1)
                    dve.wait_ge(merged, m + 1)
                    V.scalar_tensor_tensor(out=mg_lo[:, m], in0=gt(m), scalar=0.5, in1=mg_hi[:, m].bitcast(F32), op0=ALU.mult, op1=ALU.subtract).then_inc(merged_split, 1)
            dve.wait_ge(gain_row_loaded, 16)
            for t in range(TT):
                dve.wait_ge(out_sq, 4 + t + 1)
                V.tensor_tensor(tiny[:, 16 + t:17 + t], tiny[:, 2 * t:2 * t + 1], tiny[:, 2 * t + 1:2 * t + 2], ALU.add).then_inc(out_sum, 1)
                dve.wait_ge(out_root, 2 * t + 2)
                for half in range(2):
                    c = slice(512 * half, 512 * half + 512)
                    V.scalar_tensor_tensor(out=ost[:, t, c], in0=banks[(4, 0)[half] + t][:], scalar=tiny[:, 24 + t:25 + t], in1=gain_row[:, c],
                                           op0=ALU.mult, op1=ALU.mult).then_inc(out_ready, 1)

        @block.tensor
        def _(pe):
            mm1 = nc.tensor.matmul

            def three(bank, hi, lo, rhi, rlo, start, stop):
                mm1(bank, hi, rhi, start=start, stop=False)
                mm1(bank, hi, rlo, start=False, stop=False)
                return mm1(bank, lo, rhi, start=False, stop=stop)

            def feature_steps(n, f, k0, k1, bank):
                slot = n % 2
                if k0 == 0 and f == 0:
                    pe.wait_ge(slab_split, n + 1)
                for k in range(k0, k1):
                    c = k * SC + f * P
                    ins = three(bank[:], w_hi[:, slot, c:c + P], w_lo[:, slot, c:c + P], xn_hi[:, k, META:TM], xn_lo[:, k, META:TM], k == 0, k == KD - 1)
                    if k % 2:
                        ins.then_inc(eighths_used, 1)

            def stat(q):
                pe.wait_ge(sq_added, 8 * q + 8 if q < 3 else 40)
                ins = mm1(banks[4][:], ones, sums, start=True, stop=True)
                if q == 3:
                    ins = mm1(banks[5][:], ones, sums2, start=True, stop=True)
                ins.then_inc(sums_mm, 1)

            def token_factor(from_):
                for t in range(TT):
                    ins = mm1(banks[7][:, t:t + 1], from_[:, t * P:(t + 1) * P], ident[:, 0:1], start=True, stop=True)
                ins.then_inc(rtok_mm, 1)

            def first_tiles(q, n):
                pe.wait_ge(slab_split, n + 1)
                pe.wait_ge(x_ready, 8 * q + 6 if q else 2)
                for k in range(KD):
                    pe.wait_ge(xn_split, 8 * q + k + 1)
                    for f in range(2):
                        c = k * SC + f * P
                        ins = three(banks[f][:], w_hi[:, n % 2, c:c + P], w_lo[:, n % 2, c:c + P], xn_hi[:, k, META:TM], xn_lo[:, k, META:TM],
                                    k == 0, k == KD - 1)
                        if k == KD - 1:
                            ins.then_inc(eighths_used, 4)

            def ffn(base, n0, q):
                def pair(i, first):
                    for part, freed in ((0, gate_out), (1, up_out)):
                        slot = (n0 + part) % 2
                        pe.wait_ge(slab_split, n0 + 2 * i + part + 1)
                        if first and part == 0:
                            first_tiles(q, n0)
                            continue
                        for f in range(2):
                            if first:
                                pe.wait_ge(x_ready, 8 * q + 5 + 2 * part + f)
                            else:
                                pe.wait_ge(freed, base + 2 * i + f - 1)
                            for k in range(KD):
                                c = k * SC + f * P
                                ins = three(banks[2 * part + f][:], w_hi[:, slot, c:c + P], w_lo[:, slot, c:c + P],
                                            xn_hi[:, k, META:TM], xn_lo[:, k, META:TM], k == 0, k == KD - 1)
                                if k % 2:
                                    ins.then_inc(eighths_used, 1)
                            if first and f == 0:
                                stat(q)
                pair(0, True)
                if q == 0:
                    meta_turn()
                with pe.Fori(1, FP) as i:
                    pair(i, False)
                n1 = n0 + 2 * FP

                def down(m, slot, first, last):
                    pe.wait_ge(slab_split, n1 + m + 1)
                    pe.wait_ge(inner_split, base + 2 * m + 2)
                    for d in range(KD):
                        if first and d == 4:
                            pe.wait_ge(gate_out, base + 2 * FP)
                            pe.wait_ge(up_out, base + 2 * FP)
                        for kk in range(2):
                            c = kk * D + d * P
                            at = slice(2 * m + kk, 2 * m + kk + 1) if isinstance(m, int) else bass.ds(2 * m + kk, 1)
                            ins = three(banks[(d + 4) % 8][:], w_hi[:, slot, c:c + P], w_lo[:, slot, c:c + P],
                                        h_hi[:, at, :].rearrange("p a t -> p (a t)"), h_lo[:, at, :].rearrange("p a t -> p (a t)"),
                                        first and kk == 0, last and kk == 1)
                        ins.then_inc(eighths_used, 1)
                down(0, n1 % 2, True, False)
                with pe.Fori(0, (FP - 3) // 2) as j:
                    down(2 * j + 1, (n1 + 1) % 2, False, False)
                    down(2 * j + 2, n1 % 2, False, False)
                down(FP - 2, (n1 + 1) % 2, False, False)
                down(FP - 1, n1 % 2, False, True)

            pe.wait_ge(consts_loaded, 16)

            def turn(t, d, done):
                ins = nc.tensor.transpose(banks[d][:, t * P:(t + 1) * P], xload[:, t, d * P:(d + 1) * P], ident)
                if done:
                    ins.then_inc(x_turned, 1)
            for t in range(TT - 1):
                pe.wait_ge(x_loaded[t], 16)
                for d in range(KD - 1):
                    turn(t, d, False)
            pe.wait_ge(first_gain_loaded, 16)
            nc.tensor.transpose(banks[7][:, 0:KD], rows[0:KD, :], ident[0:KD, 0:KD]).then_inc(x_turned, 1)
            pe.wait_ge(x_loaded[TT - 1], 16)
            for d in range(KD - 1):
                turn(TT - 1, d, True)
            pe.wait_ge(cols_ready, 1)
            for t in range(TT):
                turn(t, KD - 1, t == TT - 1)

            def meta_turn():
                pe.wait_ge(vectors_loaded, 96)
                nc.tensor.transpose(banks[6][:, 0:ROWS], rows[0:ROWS, :], ident[0:ROWS, 0:ROWS])
                pe.wait_ge(meta_dve, 1)
                for d in range(KD):
                    ins = nc.tensor.transpose(banks[5][:, d * META:(d + 1) * META], meta_in[:, d * P:(d + 1) * P], ident[0:META, 0:META])
                ins.then_inc(meta_turned, 1)
            ffn(0, N_FFN1, 0)

            def lengths(i0):
                for i in range(i0, min(i0 + 2, 8)):
                    pe.wait_ge(len_sq, i + 1)
                    if i < 2:
                        pe.wait_ge(decay_dve, 7)
                    else:
                        pe.wait_ge(len_root, 2 * i - 3)
                    mm1(banks[4 + i % 2][:], ones, sq[:, i % 2], start=True, stop=True).then_inc(len_mm, 1)

            for j in range(12):
                n, f = N_MIX + j // 2, j % 2
                if j < 2:
                    if j == 0:
                        first_tiles(1, n)
                        stat(1)
                    continue
                if j >= 4:
                    pe.wait_ge(conv_in, j - 3)
                else:
                    pe.wait_ge(x_ready, 8 + 5 + j)
                feature_steps(n, f, 0, 4, banks[j % 4])
                if j == 9:
                    pe.wait_ge(decay_dve, 6)
                    for i, w in enumerate((cumT, same, half0, half1)):
                        ins = mm1(banks[5][:, 16 * i:16 * i + 16], w, s_g, start=True, stop=True)
                    ins.then_inc(cum_mm, 1)
                if j >= 10:
                    lengths(4 * j - 38)
                feature_steps(n, f, 4, KD, banks[j % 4])
                if j >= 9:
                    lengths(4 * j - 36)
                if j == 3:
                    pe.wait_ge(rstd_done, 2)
                    token_factor(rstd)
                if j == 4:
                    pe.wait_ge(mix_loaded, 80)
                    pe.wait_ge(rtok_done, 1)
                    for g in range(GG):
                        ins = nc.tensor.transpose(banks[6 + g // 4][:, (g % 4) * P:(g % 4 + 1) * P], wsraw[:, g], ident)
                    ins.then_inc(gate_w_mm, 1)
                if j == 3:
                    pe.wait_ge(ba_split, 4)
                    for k in range(KD):
                        c = slice(8 * k, 8 * k + P)
                        ins = three(banks[4][:], wba_hi[:, c], wba_lo[:, c], xn_hi[:, k, META:TM], xn_lo[:, k, META:TM], k == 0, k == KD - 1)
                    ins.then_inc(ba_mm, 1)
                if j == 6:
                    pe.wait_ge(decay_dve, 1)
                    for t in range(TT):
                        ins = nc.tensor.transpose(banks[5][:, 8 * t:8 * t + 8], baf[:, t * P:(t + 1) * P], ident[0:8, 0:8])
                    ins.then_inc(ba_mm, 1)

            def token_tile(n, t, bank, c0):
                c = slice(META + t * P, META + (t + 1) * P)
                for k in range(KD):
                    w = slice(k * SC, (k + 1) * SC)
                    o = bank[:, c0:c0 + SC]
                    mm1(o, xn_hi[:, k, c], w_hi[:, n % 2, w], start=k == 0, stop=False)
                    mm1(o, xn_hi[:, k, c], w_lo[:, n % 2, w], start=False, stop=False)
                    ins = mm1(o, xn_lo[:, k, c], w_hi[:, n % 2, w], start=False, stop=k == KD - 1)
                    if k % 4 == 3:
                        ins.then_inc(eighths_used, 1)
            def gate_tile(j):
                n, t = N_MIX + 6 + j // 4, j % 4
                if t == 0:
                    pe.wait_ge(slab_split, n + 1)
                if j == 0:
                    pe.wait_ge(gate_w_done, 2)
                elif j == 6:
                    pe.wait_ge(gate_v_out, 2)
                token_tile(n, t, banks[(7, 0, 1, 7)[j // 2]], SC * (j % 2))

            pair = [slice(p * P, (p + 1) * P) for p in range(4)]
            gate_tile(0)
            gate_tile(1)
            pe.wait_ge(len_done, 8)
            pe.wait_ge(conv_in, 12)
            for h in range(H):
                if h:
                    pe.wait_ge(g_rows, h)
                for p in range(4):
                    ins = mm1(banks[2][:, p * P:(p + 1) * P], s_g[:, 4 * h + p:4 * h + p + 1].to_broadcast([P, P]), cumT, start=True, stop=True)
                ins.then_inc(g_rows_mm, 1)
                if h:
                    pe.wait_ge(k_tok_done, 2 * h)
                for c in pair:
                    ins = nc.tensor.transpose(banks[5][:, c], kT(h)[:, c], ident)
                ins.then_inc(k_turned, 1)
                pe.wait_ge(qkv_done, 8 + h + 1)
                if h:
                    pe.wait_ge(v_beta, h)
                for c in pair:
                    ins = nc.tensor.transpose(banks[6][:, c], vT(h)[:, c], ident)
                ins.then_inc(v_turned, 1)
                if h:
                    pe.wait_ge(l_done, h)
                for c in pair:
                    ins = mm1(banks[3][:, c], kT(h)[:, c], kT(h)[:, c], start=True, stop=True)
                for c in pair:
                    ins = mm1(banks[4][:, c], kT(h)[:, c], qT(h)[:, c], start=True, stop=True)
                ins.then_inc(kq_mm, 1)
                for j in ((2, 3), (4,), (5,), (6, 7))[h]:
                    gate_tile(j)
            pe.wait_ge(gate_v_out, 8)
            for g in range(2):
                for hh in range(2):
                    h = 2 * g + hh
                    pe.wait_ge(m_done, g * LEVELS * 2 + hh + 1)
                    if g:
                        pe.wait_ge(z_done, 2 * LEVELS - 1 + hh)
                    for c in pair:
                        ins = nc.tensor.transpose(banks[2 + hh][:, c], Mm[:, hh, c], ident)
                    ins.then_inc(m_turned, 1)
                for level in range(1, LEVELS):
                    last = level == LEVELS - 1
                    for hh in range(2):
                        h = 2 * g + hh
                        n = (g * (LEVELS - 1) + level - 1) * 2 + hh
                        pe.wait_ge(m_done, (g * LEVELS + level) * 2 + hh + 1)
                        pe.wait_ge(z_done, (g * LEVELS + level - 1) * 2 + hh + 1)
                        if n >= 2:
                            pe.wait_ge(mz_out, n - 1)
                        for c in pair:
                            ins = mm1(banks[hh][:, c], Mm[:, hh, c], Z[:, h, c], start=True, stop=True)
                        ins.then_inc(mz_mm, 1)
                    for hh in range(2):
                        h = 2 * g + hh
                        n = (g * (LEVELS - 1) + level - 1) * 2 + hh
                        pe.wait_ge(mz_out, n + 1)
                        if level > 1:
                            pe.wait_ge(t_done, (g * (LEVELS - 2) + level - 2) * 2 + hh + 1)
                        elif g:
                            pe.wait_ge(t_done, 2 * (LEVELS - 2))
                            pe.wait_ge(t_init, 2 * g + hh + 1)
                        else:
                            pe.wait_ge(t_init, hh + 1)
                        for c in pair:
                            ins = mm1(banks[2 + hh][:, c], Tm[:, hh, c], Pp[:, hh, c], start=True, stop=True)
                        if not last:
                            for c in pair:
                                ins = mm1(banks[4 + hh][:, c], Pp[:, hh, c], Tm[:, hh, c], start=True, stop=True)
                        ins.then_inc(zt_mm, 1)
            for h in range(H):
                pe.wait_ge(z_done, 2 * LEVELS * (h // 2 + 1) - 1 + h % 2)
                if h >= 2:
                    pe.wait_ge(neg_w_done, h - 1)
                for c in pair:
                    ins = mm1(banks[6 + h % 2][:, c], kb[:, h, c], Z[:, h, c], start=True, stop=True)
                ins.then_inc(w_mm, 1)
            pe.wait_ge(ln_applied, 12)
            pe.wait_ge(gate_w_done, 3)
            pe.wait_ge(z_done, 4 * LEVELS)
            for m in range(4):
                for t in range(TT):
                    for half in range(2):
                        r = slice(CH * half, CH * half + CH)
                        ins = mm1(banks[m][r, t * P:(t + 1) * P], vtok[:, t, m * P + CH * half:m * P + CH * half + CH], wsT[:, 2 * m + half], start=True, stop=True)
                ins.then_inc(gate_mm, 1)
            pe.wait_ge(neg_w_done, 4)
            for c in range(NC):
                p, r = c // 2, slice(CH * (c % 2), CH * (c % 2) + CH)
                cc = slice(c * CH, (c + 1) * CH)
                if c:
                    pe.wait_ge(state_done, c)
                    pe.wait_ge(vnew_done, c)
                else:
                    pe.wait_ge(t_done, 4 * (LEVELS - 2))
                for h in range(H):
                    hc = slice(h * P, (h + 1) * P)
                    ins = mm1(banks[4][:, hc], Z[:, h, p * P:(p + 1) * P], vb[:, h, p * P:(p + 1) * P], start=True, stop=c == 0)
                    if c:
                        ins = mm1(banks[4][:, hc], kb[:, h, p * P:(p + 1) * P], S[:, c % 2, hc], start=False, stop=True)
                ins.then_inc(vnew_mm, 1)
                if c:
                    for h in range(H):
                        mm1(banks[h][:, cc], S[:, c % 2, h * P:(h + 1) * P], qT(h)[:, cc], start=True, stop=False)
                else:
                    pe.wait_ge(gate_mixed, 4)
                n, f = N_MIX + 8 + c // 2, c % 2
                if c >= 2:
                    pe.wait_ge(uz_out, c - 1)
                feature_steps(n, f, 0, 4, banks[6 + c % 2])
                pe.wait_ge(vnew_done, c + 1)
                if c < NC - 1:
                    for h in range(H):
                        ins = mm1(banks[5][:, h * P:(h + 1) * P], kd[r, h, p * P:(p + 1) * P], vnew[r, h * P:(h + 1) * P], start=True, stop=True)
                    ins.then_inc(state_mm, 1)
                for h in range(H):
                    ins = mm1(banks[h][:, cc], vnew[r, h * P:(h + 1) * P], atT(h)[r, cc], start=c == 0, stop=True)
                ins.then_inc(chunk_out_mm, 1)
                feature_steps(n, f, 4, KD, banks[6 + c % 2])
            def out_steps(m, k0, k1):
                n, f = N_OUT1 + m // 2, m % 2
                for k in range(k0, k1):
                    if m == 0:
                        pe.wait_ge(y_split, k + 1)
                    c = k * SC + f * P
                    ins = three(banks[m % 4][:], w_hi[:, n % 2, c:c + P], w_lo[:, n % 2, c:c + P], yh(k), yl(k), k == 0, k == KD - 1)
                if k1 == KD:
                    ins.then_inc(eighths_used, 4)
            for m in range(4):
                if m % 2 == 0:
                    pe.wait_ge(slab_split, N_OUT1 + m // 2 + 1)
                pe.wait_ge(o_out, m + 1)
                out_steps(m, 0, 4)
                for h in ((0, 1), (2, 3), (), ())[m]:
                    pe.wait_ge(o_sq, h + 1)
                    if h >= 2:
                        pe.wait_ge(o_root, 2 * h - 3)
                    mm1(banks[4 + h % 2][:], ones, sq[:, h % 2], start=True, stop=True).then_inc(o_sq_mm, 1)
            for m in range(4):
                out_steps(m, 4, KD)
            for m in range(4, KD):
                if m % 2 == 0:
                    pe.wait_ge(slab_split, N_OUT1 + m // 2 + 1)
                pe.wait_ge(x_ready, 16 + m - 3)
                out_steps(m, 0, KD)

            ffn(2 * FP, N_FFN2, 2)

            for j in range(4):
                if j < 2:
                    if j == 0:
                        first_tiles(3, N_P2)
                    continue
                pe.wait_ge(x_ready, 24 + 5 + j)
                feature_steps(N_P2 + j // 2, j % 2, 0, KD, banks[j])
                if j == 2:
                    stat(3)
            pe.wait_ge(factor_done, 2)
            token_factor(factor_t)

            def key_tile(n, f, b):
                for half in range(2):
                    hc = slice(264 * half, 264 * half + 264)
                    for k in range(KD):
                        c = k * SC + f * P
                        ins = three(banks[b + half][:, 0:264], w_hi[:, n % 2, c:c + P], w_lo[:, n % 2, c:c + P], xn_hi[:, k, hc], xn_lo[:, k, hc], k == 0, k == KD - 1)
                        if half and k % 2:
                            ins.then_inc(eighths_used, 1)

            def value_tile(n, t, o, f0, width, incs):
                c = slice(0, P) if t is None else slice(META + t * P, META + (t + 1) * P)
                for k in range(KD):
                    w = slice(k * SC + f0, k * SC + f0 + width)
                    mm1(o, xn_hi[:, k, c], w_hi[:, n % 2, w], start=k == 0, stop=False)
                    mm1(o, xn_hi[:, k, c], w_lo[:, n % 2, w], start=False, stop=False)
                    ins = mm1(o, xn_lo[:, k, c], w_hi[:, n % 2, w], start=False, stop=k == KD - 1)
                    if incs and (k + 1) % (KD // incs) == 0:
                        ins.then_inc(eighths_used, 1)

            for j in range(4):
                n = N_P2 + 2 + j // 2
                if j % 2 == 0:
                    pe.wait_ge(slab_split, n + 1)
                pe.wait_ge(qk_out, (2, 4, 6, 8)[j])
                key_tile(n, j % 2, 2 * (j % 2))
            for s in range(2):
                n = N_P2 + 4 + s
                pe.wait_ge(slab_split, n + 1)
                if s:
                    pe.wait_ge(v_out, 5)
                value_tile(n, None, banks[6][:, 0:SC], 0, SC, 0)
                for t in range(TT):
                    value_tile(n, t, banks[4 + t // 2][:, SC * (t % 2):SC * (t % 2) + SC], 0, SC, 2)
            n = N_P2 + 6
            pe.wait_ge(slab_split, n + 1)
            pe.wait_ge(qk_out, 10)
            key_tile(n, 0, 0)
            pe.wait_ge(v_out, 10)
            pe.wait_ge(qk_out, 12)
            key_tile(n, 1, 2)

            def turn_values():
                nc.tensor.transpose(banks[6][0:META, 0:P], vwf[:, 0:META], ident).then_inc(vw_turned, 1)
                for t in range(TT):
                    ins = nc.tensor.transpose(banks[4][:, t * P:(t + 1) * P], vwf[:, META + t * P:META + (t + 1) * P], ident)
                ins.then_inc(vw_turned, 1)

            def rotate_k(g):
                for w, bb in ((dup_k[g], (2, 3)), (rot_k[g], (5, 7))):
                    for half in range(2):
                        ins = mm1(banks[bb[half]][:, 0:264], w, kraw[:, 264 * half:264 * half + 264], start=True, stop=True)
                ins.then_inc(k_rot_mm, 1)

            def rotate_q(j):
                pe.wait_ge(qk_out, 16 + j + 1)
                if j >= 2:
                    pe.wait_ge(q_rot_done, j - 1)
                else:
                    pe.wait_ge(v_out, 12)
                mm1(banks[(6, 4)[j % 2]][:], rot_q, gs[:, j % 2], start=True, stop=True).then_inc(q_rot_mm, 1)
            pe.wait_ge(qk_out, 16)
            pe.wait_ge(att_loaded, 32)
            rotate_k(0)
            turn_values()
            for j in range(8):
                if j >= 2:
                    pe.wait_ge(qk_out, 16 + j - 1)
                feature_steps(N_P2 + 7 + j // 2, j % 2, 0, KD, banks[j % 2])
                if j:
                    rotate_q(j - 1)
                if j == 1:
                    pe.wait_ge(k_rot_done, 2)
                    rotate_k(1)
            rotate_q(7)

            gate_at = [0]

            def gate_steps(count):
                for i in range(gate_at[0], gate_at[0] + count):
                    t, k = i // KD, i % KD
                    if k == 0:
                        if t >= 2:
                            pe.wait_ge(gates_out, t - 1)
                        else:
                            pe.wait_ge(q_rot_done, 8)
                    feature_steps(N_P2 + 11 + t // 2, t % 2, k, k + 1, banks[6 + t % 2])
                gate_at[0] += count

            pe.wait_ge(k_rot_done, 4)
            pe.wait_ge(kblk_done, 3)
            for i in range(4 * TT):
                j, t, c = i // TT, i % TT, i * 2 * META
                ins = mm1(banks[2][:, c:c + 2 * META], Qs[:, j, t * P:(t + 1) * P], kblk[:, j], start=True, stop=True)
            ins.then_inc(zm_mm, 1)
            for step in range(32 + 3):
                u = step
                if u < 32:
                    h, t = u // 4, u % 4
                    r, j, n = slice(HD * (h % 2), HD * (h % 2) + HD), h // 2, (t + 1) * P
                    if u >= 2:
                        pe.wait_ge(arg_done, u - 1)
                    else:
                        pe.wait_ge(qk_out, 24)
                    mm1(banks[u % 2][:, 0:n], Qs[r, j, t * P:(t + 1) * P], Ks[r, j, META:META + n], start=True, stop=True).then_inc(z_mm, 1)
                    gate_steps(1)
                u = step - 2
                if 0 <= u < 32:
                    h, t = u // 4, u % 4
                    pe.wait_ge(weights_done, u + 1)
                    if u >= 2:
                        pe.wait_ge(weights_out, u - 1)
                    for b in range(t + 1):
                        ins = nc.tensor.transpose(banks[2 + u % 2][:, b * P:(b + 1) * P], unit_buf(u)[:, b * P:(b + 1) * P], ident)
                    ins.then_inc(weights_mm, 1)
                    if t == 3:
                        pe.wait_ge(weightsm_done, h + 1)
                        if h:
                            pe.wait_ge(weightsm_out, h)
                        for b in range(TT):
                            ins = nc.tensor.transpose(banks[5][0:META, b * P:(b + 1) * P], wm[:, h % 2, b * META:(b + 1) * META], ident)
                        ins.then_inc(weightsm_mm, 1)
                if step < 32:
                    gate_steps(1)
                u = step - 3
                if 0 <= u < 32:
                    h, t = u // 4, u % 4
                    r, hc = slice(HD * (h % 2), HD * (h % 2) + HD), slice(HD * h, HD * h + HD)
                    pe.wait_ge(weights_out, u + 1)
                    if u % 8 == 0:
                        if u:
                            pe.wait_ge(sb_out, u // 8)
                        else:
                            pe.wait_ge(q_rot_done, 8)
                    for b in range(t + 1):
                        ins = mm1(banks[4][r, t * P:(t + 1) * P], Vs[:, b, hc], wT[:, u % 2, b * P:(b + 1) * P],
                                  start=t == 0 and b == 0, stop=False, skip_group_check=True)
                    ins.then_inc(pv_mm, 1)
                    if t == 3:
                        pe.wait_ge(weightsm_out, h + 1)
                        mm1(banks[4][r, :], Vm[:, hc], wTm[:], start=False, stop=True, skip_group_check=True).then_inc(pvm_mm, 1)
                if step < 32:
                    gate_steps(1)
            for step in range(32 + 3):
                v = step
                if v < 32:
                    j, t = v // 4, v % 4
                    if v >= 2:
                        pe.wait_ge(score_done, v - 1)
                    else:
                        pe.wait_ge(arg_done, 32)
                    for i in range(2):
                        r = slice(HD * i, HD * i + HD)
                        keys = slice(0, META + P) if t == 0 else slice(META + (t - 1) * P, META + (t + 1) * P)
                        n = keys.stop - keys.start
                        if i:
                            gate_steps(1)
                            pe.wait_ge(z2_mm, 2 * v + 1)
                        mm1(banks[v % 2][:, 256 * (i + 1) - n:256 * (i + 1)], Qw[r, j, t * P:(t + 1) * P], Kw[r, j // 4, keys], start=True, stop=True).then_inc(z2_mm, 1)
                v = step - 2
                if 0 <= v < 32:
                    t = v % 4
                    pe.wait_ge(weights2_done, v + 1)
                    if v >= 2:
                        pe.wait_ge(weights2_out, 2 * (v - 1))
                    else:
                        pe.wait_ge(weights_out, 31 + v)
                    for i in range(2):
                        o = 256 * i
                        bank = banks[2 + v % 2]
                        if t:
                            nc.tensor.transpose(bank[:, o:o + P], unit_buf(v)[:, o:o + P], ident)
                        else:
                            nc.tensor.transpose(bank[0:META, o:o + P], unit_buf(v)[:, o + 112:o + P], ident)
                        ins = nc.tensor.transpose(bank[:, o + P:o + 2 * P], unit_buf(v)[:, o + P:o + 2 * P], ident)
                    ins.then_inc(weights2_mm, 1)
                if step < 32:
                    gate_steps(1)
                v = step - 3
                if 0 <= v < 32:
                    j, t = v // 4, v % 4
                    pe.wait_ge(weights2_out, 2 * v + 2)
                    if t == 0:
                        if j >= 2:
                            pe.wait_ge(sw_gated, j - 1)
                        else:
                            pe.wait_ge(sb_out, 4)
                    vc = slice(HD * (j // 4), HD * (j // 4) + HD)
                    for i in range(2):
                        o = banks[4 + j % 2][HD * i:HD * i + HD, t * P:(t + 1) * P]
                        w = wT[:, v % 2, 256 * i:256 * i + 256]
                        if t:
                            mm1(o, Vw[:, t - 1, vc], w[:, 0:P], start=True, stop=False)
                        else:
                            mm1(o, Vwm[:, vc], w[0:META, 0:P], start=True, stop=False)
                        ins = mm1(o, Vw[:, t, vc], w[:, P:2 * P], start=False, stop=True)
                    ins.then_inc(pv2_mm, 1)
                if step < 32:
                    gate_steps(1)
            gate_steps(32)

            for half in range(2):
                n = N_BR + 3 * half
                pe.wait_ge(slab_split, n + 1)
                for m in range(4 * half, 4 * half + 4):
                    if m >= 2:
                        pe.wait_ge(sb_merged, m - 1)
                    for k in range(4):
                        if m == 0:
                            pe.wait_ge(br_split, k + 1)
                        c = k * 512 + (m % 4) * P
                        ins = three(banks[m % 2][:], w_hi[:, n % 2, c:c + P], w_lo[:, n % 2, c:c + P], asb_hi[:, k], asb_lo[:, k], k == 0, k == 3)
                        if k % 2:
                            ins.then_inc(eighths_used, 1)
                for m in range(4 * half, 4 * half + 4):
                    if m >= 2:
                        pe.wait_ge(sw_merged, m - 1)
                    for k in range(KD):
                        if m == 0:
                            pe.wait_ge(br_split, 4 + k + 1)
                        feature_steps(n + 1 + m % 4 // 2, m % 2, k, k + 1, banks[2 + m % 2])
            pe.wait_ge(gates_out, 28)
            pe.wait_ge(sw_gated, 8)
            pe.wait_ge(x_ready, 40)
            for s in range(4):
                n = N_OUT2 + s
                pe.wait_ge(slab_split, n + 1)
                for t in range(TT):
                    o, c = out_bank(s, t), slice(t * P, (t + 1) * P)
                    for i in range(2):
                        mm1(o[:, i * P:(i + 1) * P], xT[:, 2 * s + i, c], ident, start=s % 2 == 0 and i == 0, stop=False, skip_group_check=True)
                    for k in range(KD):
                        if s == 0 and t == 0:
                            pe.wait_ge(merged_split, k + 1)
                        w = slice(k * SC, (k + 1) * SC)
                        mm1(o, mg_hi[:, k, c], w_hi[:, n % 2, w], start=False, stop=False, skip_group_check=True)
                        mm1(o, mg_hi[:, k, c], w_lo[:, n % 2, w], start=False, stop=False, skip_group_check=True)
                        ins = mm1(o, mg_lo[:, k, c], w_hi[:, n % 2, w], start=False, stop=k == KD - 1, skip_group_check=True)
                        if k % 4 == 3:
                            ins.then_inc(eighths_used, 1)


INPUTS = ("x", "ffn1_norm", "ffn1_w_gate", "ffn1_w_up", "ffn1_w_down", "mix_norm", "w_in", "gm_ln_g", "gm_ln_b", "gm_w_s",
          "gm_b_s", "dn_conv_w", "dn_a_log", "dn_dt_bias", "dn_norm", "w_out", "ffn2_norm", "ffn2_w_gate", "ffn2_w_up",
          "ffn2_w_down", "final_norm", "meta_tokens_2", "norm_gain_2", "w_in_2", "w_branch_sb_2", "w_branch_swa_2",
          "w_out_2", "attn_sinks_2", "final_norm_gain_2")


def kernel(**inputs):
    import concourse.bacc as bacc
    from concourse.bass_utils import run_bass_kernel_spmd

    nc = bacc.Bacc("TRN2", target_bir_lowering=False, num_devices=1)
    arrays, aps = {}, {}
    given = {name: inputs[name] for name in INPUTS}
    given.update(constants())
    for name, value in given.items():
        value = np.ascontiguousarray(value)
        arrays[f"in_{name}_dram"] = value
        aps[name] = nc.dram_tensor(f"in_{name}_dram", value.shape, mybir.dt.from_np(value.dtype), kind="ExternalInput").ap()
    out = nc.dram_tensor("out_0_dram", (1, T, D), F32, kind="ExternalOutput").ap()
    program(nc, aps, out)
    result = run_bass_kernel_spmd(nc, [arrays], core_ids=[0])
    return result.results[0]["out_0_dram"]
```
